# Optimizing a Trainium2 kernel written in Bass

```python
import jax, jax.numpy as jnp
from jax import lax
import numpy as np

D_MODEL = 1024
BATCH = 1
SEQ = 256
DEPTH = 1

MEM_LEN = 256
HEAD_DIM = 64
LRU_WIDTH = D_MODEL // 2
LRU_BLOCKS = 8
LRU_BLOCK_W = LRU_WIDTH // LRU_BLOCKS
CONV_W = 4
LRU_C = 8.0
MOBA_HEADS = 4
MOBA_WIDTH = MOBA_HEADS * HEAD_DIM
MOBA_BLOCK = 256
MOBA_TOPK = 3
Q_CHUNK = 128
MEM_HEADS = 4
MEM_WIDTH = MEM_HEADS * HEAD_DIM
MIX_WIDTH = LRU_WIDTH + MOBA_WIDTH + MEM_WIDTH
IN_WIDTH = 2 * LRU_WIDTH + 3 * MOBA_WIDTH + MEM_WIDTH
D_FF = ((8 * D_MODEL // 3 + 127) // 128) * 128
NORM_EPS = 1e-6


def rms_norm(x, g):
    xf = x.astype(jnp.float32)
    y = xf * lax.rsqrt(jnp.mean(xf * xf, axis=-1, keepdims=True) + NORM_EPS)
    return (y * g.astype(jnp.float32)).astype(x.dtype)

def swiglu(x, w_in, w_out):
    a, b = jnp.split(x @ w_in, 2, axis=-1)
    return (jax.nn.silu(a) * b) @ w_out

def alibi_slopes(n_heads):
    return 2.0 ** (-8.0 * jnp.arange(1, n_heads + 1, dtype=jnp.float32) / n_heads)

def split_heads(t, n_heads):
    b, s, _ = t.shape
    return t.reshape(b, s, n_heads, HEAD_DIM).transpose(0, 2, 1, 3)

def merge_heads(t):
    b, h, s, d = t.shape
    return t.transpose(0, 2, 1, 3).reshape(b, s, h * d)

def causal_depthwise_conv(x, w, bias):
    c = x.shape[-1]
    y = lax.conv_general_dilated(
        x, w[:, None, :].astype(x.dtype), window_strides=(1,), padding=[(CONV_W - 1, 0)],
        dimension_numbers=("NWC", "WIO", "NWC"), feature_group_count=c)
    return y + bias.astype(x.dtype)

def rg_lru(xb, a_w, a_b, x_w, x_b, lam):
    b, s, c = xb.shape
    xf = xb.astype(jnp.float32)
    xblk = xf.reshape(b, s, LRU_BLOCKS, LRU_BLOCK_W)
    r = jax.nn.sigmoid(jnp.einsum("bsnc,ncd->bsnd", xblk, a_w.astype(jnp.float32)) + a_b.astype(jnp.float32)).reshape(b, s, c)
    i = jax.nn.sigmoid(jnp.einsum("bsnc,ncd->bsnd", xblk, x_w.astype(jnp.float32)) + x_b.astype(jnp.float32)).reshape(b, s, c)
    log_a = -LRU_C * r * jax.nn.softplus(-lam.astype(jnp.float32))
    a = jnp.exp(log_a)
    mult = jnp.sqrt(-jnp.expm1(2.0 * log_a))
    mult = jnp.where(jnp.arange(s)[None, :, None] == 0, 1.0, mult)
    bt = mult * i * xf

    def combine(left, right):
        a1, b1 = left
        a2, b2 = right
        return a1 * a2, a2 * b1 + b2

    _, h = lax.associative_scan(combine, (a, bt), axis=1)
    return h

def moba_attention(q, k, v):
    b, h, s, hd = q.shape
    n_blk = -(-s // MOBA_BLOCK)
    s_pad = n_blk * MOBA_BLOCK
    pad = s_pad - s
    if pad:
        widths = ((0, 0), (0, 0), (0, pad), (0, 0))
        q, k, v = jnp.pad(q, widths), jnp.pad(k, widths), jnp.pad(v, widths)
    kb = k.reshape(b, h, n_blk, MOBA_BLOCK, hd)
    vb = v.reshape(b, h, n_blk, MOBA_BLOCK, hd)
    k_mean = jnp.mean(kb.astype(jnp.float32), axis=3)
    gate = jnp.einsum("bhsd,bhnd->bhsn", q.astype(jnp.float32), k_mean)
    q_blk = jnp.arange(s_pad) // MOBA_BLOCK
    fully_past = jnp.arange(n_blk)[None, :] < q_blk[:, None]
    gate = jnp.where(fully_past, gate, -jnp.inf)
    n_sel = min(MOBA_TOPK, n_blk)
    gate_top, sel = lax.top_k(gate, n_sel)
    sel_ok = gate_top > -jnp.inf
    slopes = alibi_slopes(h)
    scale = hd ** -0.5
    offs = jnp.arange(MOBA_BLOCK)
    gather_blocks = jax.vmap(jax.vmap(lambda blocks, idx: blocks[idx]))

    def chunk(c):
        start = c * Q_CHUNK
        qc = lax.dynamic_slice_in_dim(q, start, Q_CHUNK, axis=2)
        selc = lax.dynamic_slice_in_dim(sel, start, Q_CHUNK, axis=2)
        okc = lax.dynamic_slice_in_dim(sel_ok, start, Q_CHUNK, axis=2)
        own = start // MOBA_BLOCK
        k_own = lax.dynamic_index_in_dim(kb, own, axis=2, keepdims=False)
        v_own = lax.dynamic_index_in_dim(vb, own, axis=2, keepdims=False)
        k_sel = gather_blocks(kb, selc)
        v_sel = gather_blocks(vb, selc)
        t_q = start + jnp.arange(Q_CHUNK)
        s_own = jnp.einsum("bhqd,bhkd->bhqk", qc, k_own).astype(jnp.float32) * scale
        d_own = t_q[:, None] - (own * MOBA_BLOCK + offs)[None, :]
        s_own = jnp.where(d_own >= 0, s_own - slopes[:, None, None] * d_own.astype(jnp.float32), -jnp.inf)
        s_sel = jnp.einsum("bhqd,bhqjkd->bhqjk", qc, k_sel).astype(jnp.float32) * scale
        d_sel = t_q[None, None, :, None, None] - (selc[..., None] * MOBA_BLOCK + offs)
        s_sel = jnp.where(okc[..., None], s_sel - slopes[None, :, None, None, None] * d_sel.astype(jnp.float32), -jnp.inf)
        scores = jnp.concatenate([s_sel.reshape(b, h, Q_CHUNK, n_sel * MOBA_BLOCK), s_own], axis=-1)
        p = jax.nn.softmax(scores, axis=-1)
        p_sel = p[..., :n_sel * MOBA_BLOCK].reshape(b, h, Q_CHUNK, n_sel, MOBA_BLOCK).astype(v.dtype)
        p_own = p[..., n_sel * MOBA_BLOCK:].astype(v.dtype)
        return (jnp.einsum("bhqjk,bhqjkd->bhqd", p_sel, v_sel)
                + jnp.einsum("bhqk,bhkd->bhqd", p_own, v_own))

    out = lax.map(chunk, jnp.arange(s_pad // Q_CHUNK))
    out = out.transpose(1, 2, 0, 3, 4).reshape(b, h, s_pad, hd)
    return out[:, :, :s]

def memory_attention(q, k, v):
    scores = jnp.einsum("bhsd,bhmd->bhsm", q, k).astype(jnp.float32) * (HEAD_DIM ** -0.5)
    p = jax.nn.softmax(scores, axis=-1)
    return jnp.einsum("bhsm,bhmd->bhsd", p.astype(v.dtype), v)

def first_inputs(seed: int = 0) -> dict:
    key = jax.random.key(seed)
    ks = jax.random.split(key, 24)

    def normal(k, shape, scale):
        return jax.random.normal(k, shape, jnp.float32) * scale

    def gain(k, n):
        return 1.0 + 0.02 * jax.random.normal(k, (DEPTH, n), jnp.float32)

    u = jax.random.uniform(ks[12], (DEPTH, LRU_WIDTH), jnp.float32, minval=0.9, maxval=0.999)
    a0 = u ** (1.0 / LRU_C)
    lam = jnp.log(a0) - jnp.log1p(-a0)
    return {
        "x": normal(ks[0], (BATCH, SEQ, D_MODEL), 1.0),
        "mem": normal(ks[1], (BATCH, MEM_LEN, D_MODEL), 1.0),
        "ffn1_norm": gain(ks[2], D_MODEL),
        "ffn1_w_in": normal(ks[3], (DEPTH, D_MODEL, 2 * D_FF), D_MODEL ** -0.5),
        "ffn1_w_out": normal(ks[4], (DEPTH, D_FF, D_MODEL), D_FF ** -0.5),
        "mix_norm": gain(ks[5], D_MODEL),
        "mem_norm": gain(ks[6], D_MODEL),
        "w_in": normal(ks[7], (DEPTH, D_MODEL, IN_WIDTH), D_MODEL ** -0.5),
        "lru_conv_w": normal(ks[8], (DEPTH, CONV_W, LRU_WIDTH), CONV_W ** -0.5),
        "lru_conv_b": normal(ks[9], (DEPTH, LRU_WIDTH), 0.01),
        "lru_a_w": normal(ks[10], (DEPTH, LRU_BLOCKS, LRU_BLOCK_W, LRU_BLOCK_W), LRU_BLOCK_W ** -0.5),
        "lru_a_b": normal(ks[11], (DEPTH, LRU_BLOCKS, LRU_BLOCK_W), 0.01),
        "lru_x_w": normal(ks[13], (DEPTH, LRU_BLOCKS, LRU_BLOCK_W, LRU_BLOCK_W), LRU_BLOCK_W ** -0.5),
        "lru_x_b": normal(ks[14], (DEPTH, LRU_BLOCKS, LRU_BLOCK_W), 0.01),
        "lru_lambda": lam,
        "moba_q_norm": gain(ks[15], HEAD_DIM),
        "moba_k_norm": gain(ks[16], HEAD_DIM),
        "mem_w_kv": normal(ks[17], (DEPTH, D_MODEL, 2 * MEM_WIDTH), D_MODEL ** -0.5),
        "mem_q_norm": gain(ks[18], HEAD_DIM),
        "mem_k_norm": gain(ks[19], HEAD_DIM),
        "w_out": normal(ks[20], (DEPTH, MIX_WIDTH, D_MODEL), MIX_WIDTH ** -0.5),
        "ffn2_norm": gain(ks[21], D_MODEL),
        "ffn2_w_in": normal(ks[22], (DEPTH, D_MODEL, 2 * D_FF), D_MODEL ** -0.5),
        "ffn2_w_out": normal(ks[23], (DEPTH, D_FF, D_MODEL), D_FF ** -0.5),
    }

def first_block(x, mem, ffn1_norm, ffn1_w_in, ffn1_w_out, mix_norm, mem_norm, w_in,
              lru_conv_w, lru_conv_b, lru_a_w, lru_a_b, lru_x_w, lru_x_b, lru_lambda,
              moba_q_norm, moba_k_norm, mem_w_kv, mem_q_norm, mem_k_norm, w_out,
              ffn2_norm, ffn2_w_in, ffn2_w_out):
    split_at = np.cumsum([LRU_WIDTH, LRU_WIDTH, MOBA_WIDTH, MOBA_WIDTH, MOBA_WIDTH])
    for l in range(DEPTH):
        x = x + 0.5 * swiglu(rms_norm(x, ffn1_norm[l]), ffn1_w_in[l], ffn1_w_out[l])

        u = rms_norm(x, mix_norm[l]) @ w_in[l]
        lru_x, lru_g, mq, mk, mv, cq = jnp.split(u, split_at, axis=-1)

        xb = causal_depthwise_conv(lru_x, lru_conv_w[l], lru_conv_b[l])
        h_lru = rg_lru(xb, lru_a_w[l], lru_a_b[l], lru_x_w[l], lru_x_b[l], lru_lambda[l])
        y_lru = (h_lru * jax.nn.gelu(lru_g.astype(jnp.float32))).astype(x.dtype)

        q = rms_norm(split_heads(mq, MOBA_HEADS), moba_q_norm[l])
        k = rms_norm(split_heads(mk, MOBA_HEADS), moba_k_norm[l])
        v = split_heads(mv, MOBA_HEADS)
        y_moba = merge_heads(moba_attention(q, k, v))

        mkv = rms_norm(mem, mem_norm[l]) @ mem_w_kv[l]
        mem_k, mem_v = jnp.split(mkv, 2, axis=-1)
        qc = rms_norm(split_heads(cq, MEM_HEADS), mem_q_norm[l])
        kc = rms_norm(split_heads(mem_k, MEM_HEADS), mem_k_norm[l])
        y_mem = merge_heads(memory_attention(qc, kc, split_heads(mem_v, MEM_HEADS)))

        mixed = jnp.concatenate([y_lru, y_moba.astype(x.dtype), y_mem.astype(x.dtype)], axis=-1)
        x = x + mixed @ w_out[l]

        x = x + 0.5 * swiglu(rms_norm(x, ffn2_norm[l]), ffn2_w_in[l], ffn2_w_out[l])
    return x


DEPTH_2 = 2

CONV_DIM = 512
CONV_WIDTH = 3
NSA_HEADS = 8
NSA_GROUPS = 2
HEADS_PER_GROUP = NSA_HEADS // NSA_GROUPS
ROT_DIM = HEAD_DIM // 4
ROPE_THETA = 500000.0
CMP_BLOCK = 32
CMP_STRIDE = 16
CMP_HIDDEN = 256
SLC_BLOCK = 64
N_SELECT = 16
WINDOW = 512
MEM_HEAD_DIM = 128
D_FF_2 = 2816
Q_BLOCK = 128
EPS = 1e-6
NEG = -1e30
BIG = 1e30
SPLIT_SIZES = (CONV_DIM, CONV_DIM, CONV_DIM, NSA_HEADS * HEAD_DIM, 6 * NSA_GROUPS * HEAD_DIM, 3 * NSA_HEADS, MEM_HEADS * MEM_HEAD_DIM, 3 * D_MODEL)
MIX_IN = 3 * CONV_DIM + NSA_HEADS * HEAD_DIM + 6 * NSA_GROUPS * HEAD_DIM + 3 * NSA_HEADS + MEM_HEADS * MEM_HEAD_DIM + 3 * D_MODEL


def rms_norm_2(x, g):
    xf = x.astype(jnp.float32)
    y = xf * lax.rsqrt(jnp.mean(xf * xf, axis=-1, keepdims=True) + EPS)
    return (y * g.astype(jnp.float32)).astype(x.dtype)

def swiglu_2(h, w_in, w_out):
    a, b = jnp.split(h @ w_in, 2, axis=-1)
    return (jax.nn.silu(a) * b) @ w_out

def rope_tables(positions):
    inv_freq = ROPE_THETA ** (-jnp.arange(0, ROT_DIM, 2, dtype=jnp.float32) / ROT_DIM)
    ang = positions.astype(jnp.float32)[..., None] * inv_freq
    return jnp.cos(ang)[:, :, None, :], jnp.sin(ang)[:, :, None, :]

def partial_rope(t, cos, sin):
    half = ROT_DIM // 2
    t1, t2, rest = t[..., :half], t[..., half:ROT_DIM], t[..., ROT_DIM:]
    return jnp.concatenate([t1 * cos - t2 * sin, t2 * cos + t1 * sin, rest], axis=-1)

def masked_softmax(s, mask):
    s = jnp.where(mask, s.astype(jnp.float32), NEG)
    m = jnp.max(s, axis=-1, keepdims=True)
    p = jnp.where(mask, jnp.exp(s - m), 0.0)
    return p / jnp.maximum(jnp.sum(p, axis=-1, keepdims=True), 1e-30)

def short_conv(v, w):
    return lax.conv_general_dilated(v, w[:, None, :].astype(v.dtype), window_strides=(1,),
                                    padding=[(CONV_WIDTH - 1, 0)],
                                    dimension_numbers=('NWC', 'WIO', 'NWC'),
                                    feature_group_count=v.shape[-1])

def compress(t, pos_emb, w1, b1, w2):
    b, s, g, d = t.shape
    chunks = t.reshape(b, s // CMP_STRIDE, CMP_STRIDE, g, d)
    blocks = jnp.concatenate([chunks[:, :-1], chunks[:, 1:]], axis=2)
    blocks = blocks + pos_emb[None, None, :, None, :]
    flat = jnp.moveaxis(blocks, 3, 2).reshape(b, -1, g, CMP_BLOCK * d)
    return jax.nn.gelu(flat @ w1 + b1) @ w2

def cmp_to_slc_matrix(n_cmp, n_slc):
    i = jnp.arange(n_cmp)[:, None] * CMP_STRIDE
    j = jnp.arange(n_slc)[None, :] * SLC_BLOCK
    ov = jnp.minimum(i + CMP_BLOCK, j + SLC_BLOCK) - jnp.maximum(i, j)
    return jnp.maximum(ov, 0).astype(jnp.float32) / CMP_BLOCK

def nsa_attention(q, q_rot, k_cmp, v_cmp, k_slc, v_slc, k_win, v_win, gates):
    b, s, h, d = q.shape
    n_cmp = k_cmp.shape[1]
    n_slc = s // SLC_BLOCK
    top = min(N_SELECT, n_slc)
    scale = HEAD_DIM ** -0.5
    q_plain_g = q.reshape(b, s, NSA_GROUPS, HEADS_PER_GROUP, d)
    q_rot_g = q_rot.reshape(b, s, NSA_GROUPS, HEADS_PER_GROUP, d)
    kc = jnp.transpose(k_cmp, (0, 2, 1, 3))
    vc = jnp.transpose(v_cmp, (0, 2, 1, 3))
    cmp_end = jnp.arange(n_cmp) * CMP_STRIDE + CMP_BLOCK - 1
    overlap = cmp_to_slc_matrix(n_cmp, n_slc)
    ks_blocks = k_slc.reshape(b, n_slc, SLC_BLOCK, NSA_GROUPS, d).transpose(0, 3, 1, 2, 4)
    vs_blocks = v_slc.reshape(b, n_slc, SLC_BLOCK, NSA_GROUPS, d).transpose(0, 3, 1, 2, 4)
    pad = ((0, 0), (WINDOW, 0), (0, 0), (0, 0))
    kw_pad = jnp.pad(k_win, pad)
    vw_pad = jnp.pad(v_win, pad)
    bi = jnp.arange(b)[:, None, None, None]
    gi = jnp.arange(NSA_GROUPS)[None, :, None, None]
    blk = jnp.arange(n_slc)

    def block(start):
        t = start + jnp.arange(Q_BLOCK)
        qp = lax.dynamic_slice_in_dim(q_plain_g, start, Q_BLOCK, axis=1)
        qr = lax.dynamic_slice_in_dim(q_rot_g, start, Q_BLOCK, axis=1)
        s_c = jnp.einsum('bqghd,bgnd->bghqn', qp, kc) * scale
        p_c = masked_softmax(s_c, cmp_end[None, :] <= t[:, None])
        o_c = jnp.einsum('bghqn,bgnd->bqghd', p_c.astype(vc.dtype), vc)
        imp = jnp.einsum('bghqn,nj->bgqj', p_c, overlap)
        cur = (t // SLC_BLOCK)[:, None]
        forced = (blk == 0) | (blk == cur) | (blk == cur - 1)
        imp = jnp.where(blk > cur, NEG, jnp.where(forced, BIG, imp))
        _, idx = lax.top_k(imp, top)
        ks = ks_blocks[bi, gi, idx].reshape(b, NSA_GROUPS, Q_BLOCK, top * SLC_BLOCK, d)
        vs = vs_blocks[bi, gi, idx].reshape(b, NSA_GROUPS, Q_BLOCK, top * SLC_BLOCK, d)
        kpos = (idx[..., None] * SLC_BLOCK + jnp.arange(SLC_BLOCK)).reshape(b, NSA_GROUPS, Q_BLOCK, top * SLC_BLOCK)
        m_s = kpos <= t[None, None, :, None]
        s_s = jnp.einsum('bqghd,bgqld->bghql', qr, ks) * scale
        p_s = masked_softmax(s_s, m_s[:, :, None])
        o_s = jnp.einsum('bghql,bgqld->bqghd', p_s.astype(vs.dtype), vs)
        kw = lax.dynamic_slice_in_dim(kw_pad, start, WINDOW + Q_BLOCK, axis=1)
        vw = lax.dynamic_slice_in_dim(vw_pad, start, WINDOW + Q_BLOCK, axis=1)
        wpos = start - WINDOW + jnp.arange(WINDOW + Q_BLOCK)
        m_w = (wpos[None, :] >= 0) & (wpos[None, :] <= t[:, None]) & (wpos[None, :] > t[:, None] - WINDOW)
        s_w = jnp.einsum('bqghd,bkgd->bghqk', qr, kw) * scale
        p_w = masked_softmax(s_w, m_w)
        o_w = jnp.einsum('bghqk,bkgd->bqghd', p_w.astype(vw.dtype), vw)
        g = lax.dynamic_slice_in_dim(gates, start, Q_BLOCK, axis=1)
        return g[..., 0:1] * o_c + g[..., 1:2] * o_s + g[..., 2:3] * o_w

    out = lax.map(block, jnp.arange(s // Q_BLOCK) * Q_BLOCK)
    return jnp.moveaxis(out, 0, 1).reshape(b, s, h * d)

def token_mixer(h, mem, cos, sin, mem_g, w_in, conv_w, cmp_pos_k, cmp_pos_v,
                ck_w1, ck_b1, ck_w2, cv_w1, cv_b1, cv_w2,
                w_mem_kv, w_br_conv, w_br_nsa, w_br_mem, w_out):
    b, s, _ = h.shape
    points, acc = [], 0
    for n in SPLIT_SIZES[:-1]:
        acc += n
        points.append(acc)
    u, bg, cg, q, kv, nsa_g, q_mem, merge_g = jnp.split(h @ w_in, points, axis=-1)
    cos = cos.astype(h.dtype)
    sin = sin.astype(h.dtype)
    y_conv = bg * short_conv(cg * u, conv_w)
    q = q.reshape(b, s, NSA_HEADS, HEAD_DIM)
    kv = kv.reshape(b, s, 6, NSA_GROUPS, HEAD_DIM)
    k_cmp = compress(kv[:, :, 0], cmp_pos_k, ck_w1, ck_b1, ck_w2)
    v_cmp = compress(kv[:, :, 1], cmp_pos_v, cv_w1, cv_b1, cv_w2)
    k_slc = partial_rope(kv[:, :, 2], cos, sin)
    k_win = partial_rope(kv[:, :, 4], cos, sin)
    q_rot = partial_rope(q, cos, sin)
    gates = jax.nn.sigmoid(nsa_g).reshape(b, s, NSA_GROUPS, HEADS_PER_GROUP, 3)
    y_nsa = nsa_attention(q, q_rot, k_cmp, v_cmp, k_slc, kv[:, :, 3], k_win, kv[:, :, 5], gates)
    m_len = mem.shape[1]
    mkv = (rms_norm_2(mem, mem_g) @ w_mem_kv).reshape(b, m_len, 2, MEM_HEADS, MEM_HEAD_DIM)
    q_m = q_mem.reshape(b, s, MEM_HEADS, MEM_HEAD_DIM)
    s_m = jnp.einsum('bshd,bmhd->bhsm', q_m, mkv[:, :, 0]).astype(jnp.float32) * (MEM_HEAD_DIM ** -0.5)
    p_m = jax.nn.softmax(s_m, axis=-1)
    y_mem = jnp.einsum('bhsm,bmhd->bshd', p_m.astype(mkv.dtype), mkv[:, :, 1]).reshape(b, s, MEM_HEADS * MEM_HEAD_DIM)
    g_conv, g_nsa, g_mem = jnp.split(jax.nn.sigmoid(merge_g), 3, axis=-1)
    merged = g_conv * (y_conv @ w_br_conv) + g_nsa * (y_nsa @ w_br_nsa) + g_mem * (y_mem @ w_br_mem)
    return merged @ w_out

def second_inputs(seed: int = 0) -> dict:
    key = jax.random.key(seed)
    keys = iter(jax.random.split(key, 40))
    L = DEPTH_2

    def dense(shape, fan_in):
        return jax.random.normal(next(keys), shape, jnp.float32) * fan_in ** -0.5

    def gain(shape):
        return 1.0 + 0.05 * jax.random.normal(next(keys), shape, jnp.float32)

    def small(shape, scale):
        return scale * jax.random.normal(next(keys), shape, jnp.float32)

    x = jax.random.normal(next(keys), (BATCH, SEQ, D_MODEL), jnp.float32)
    mem = jax.random.normal(next(keys), (BATCH, MEM_LEN, D_MODEL), jnp.float32)
    offset = jax.random.randint(next(keys), (BATCH, 1), 0, 4096, dtype=jnp.int32)
    positions = (jnp.arange(SEQ, dtype=jnp.int32)[None, :] + offset).astype(jnp.int32)
    return {
        'x': x,
        'mem': mem,
        'positions': positions,
        'ffn1_norm_pre': gain((L, D_MODEL)),
        'ffn1_norm_post': gain((L, D_MODEL)),
        'ffn1_w_in': dense((L, D_MODEL, 2 * D_FF_2), D_MODEL),
        'ffn1_w_out': dense((L, D_FF_2, D_MODEL), D_FF_2),
        'mix_norm_pre': gain((L, D_MODEL)),
        'mix_norm_post': gain((L, D_MODEL)),
        'mem_norm': gain((L, D_MODEL)),
        'w_mix_in': dense((L, D_MODEL, MIX_IN), D_MODEL),
        'conv_w': dense((L, CONV_WIDTH, CONV_DIM), CONV_WIDTH),
        'cmp_pos_k': small((L, CMP_BLOCK, HEAD_DIM), 0.1),
        'cmp_pos_v': small((L, CMP_BLOCK, HEAD_DIM), 0.1),
        'cmp_k_w1': dense((L, CMP_BLOCK * HEAD_DIM, CMP_HIDDEN), CMP_BLOCK * HEAD_DIM),
        'cmp_k_b1': small((L, CMP_HIDDEN), 0.01),
        'cmp_k_w2': dense((L, CMP_HIDDEN, HEAD_DIM), CMP_HIDDEN),
        'cmp_v_w1': dense((L, CMP_BLOCK * HEAD_DIM, CMP_HIDDEN), CMP_BLOCK * HEAD_DIM),
        'cmp_v_b1': small((L, CMP_HIDDEN), 0.01),
        'cmp_v_w2': dense((L, CMP_HIDDEN, HEAD_DIM), CMP_HIDDEN),
        'w_mem_kv': dense((L, D_MODEL, 2 * MEM_HEADS * MEM_HEAD_DIM), D_MODEL),
        'w_branch_conv': dense((L, CONV_DIM, D_MODEL), CONV_DIM),
        'w_branch_nsa': dense((L, NSA_HEADS * HEAD_DIM, D_MODEL), NSA_HEADS * HEAD_DIM),
        'w_branch_mem': dense((L, MEM_HEADS * MEM_HEAD_DIM, D_MODEL), MEM_HEADS * MEM_HEAD_DIM),
        'w_mix_out': dense((L, D_MODEL, D_MODEL), D_MODEL),
        'ffn2_norm_pre': gain((L, D_MODEL)),
        'ffn2_norm_post': gain((L, D_MODEL)),
        'ffn2_w_in': dense((L, D_MODEL, 2 * D_FF_2), D_MODEL),
        'ffn2_w_out': dense((L, D_FF_2, D_MODEL), D_FF_2),
    }

def second_block(x, mem, positions, ffn1_norm_pre, ffn1_norm_post, ffn1_w_in, ffn1_w_out,
              mix_norm_pre, mix_norm_post, mem_norm, w_mix_in, conv_w,
              cmp_pos_k, cmp_pos_v, cmp_k_w1, cmp_k_b1, cmp_k_w2, cmp_v_w1, cmp_v_b1, cmp_v_w2,
              w_mem_kv, w_branch_conv, w_branch_nsa, w_branch_mem, w_mix_out,
              ffn2_norm_pre, ffn2_norm_post, ffn2_w_in, ffn2_w_out):
    cos, sin = rope_tables(positions)
    for l in range(DEPTH_2):
        h = rms_norm_2(x, ffn1_norm_pre[l])
        x = x + 0.5 * rms_norm_2(swiglu_2(h, ffn1_w_in[l], ffn1_w_out[l]), ffn1_norm_post[l])
        h = rms_norm_2(x, mix_norm_pre[l])
        y = token_mixer(h, mem, cos, sin, mem_norm[l], w_mix_in[l], conv_w[l],
                        cmp_pos_k[l], cmp_pos_v[l], cmp_k_w1[l], cmp_k_b1[l], cmp_k_w2[l],
                        cmp_v_w1[l], cmp_v_b1[l], cmp_v_w2[l], w_mem_kv[l],
                        w_branch_conv[l], w_branch_nsa[l], w_branch_mem[l], w_mix_out[l])
        x = x + rms_norm_2(y, mix_norm_post[l])
        h = rms_norm_2(x, ffn2_norm_pre[l])
        x = x + 0.5 * rms_norm_2(swiglu_2(h, ffn2_w_in[l], ffn2_w_out[l]), ffn2_norm_post[l])
    return x


def setup_inputs(seed=0):
    out = dict(first_inputs(seed))
    for name, value in second_inputs(seed + 1).items():
        if name != "x":
            out[name + "_2"] = value
    return out


def reference(
    x, mem, ffn1_norm, ffn1_w_in, ffn1_w_out, mix_norm, mem_norm, w_in, lru_conv_w, lru_conv_b,
    lru_a_w, lru_a_b, lru_x_w, lru_x_b, lru_lambda, moba_q_norm, moba_k_norm, mem_w_kv,
    mem_q_norm, mem_k_norm, w_out, ffn2_norm, ffn2_w_in, ffn2_w_out, mem_2, positions_2,
    ffn1_norm_pre_2, ffn1_norm_post_2, ffn1_w_in_2, ffn1_w_out_2, mix_norm_pre_2,
    mix_norm_post_2, mem_norm_2, w_mix_in_2, conv_w_2, cmp_pos_k_2, cmp_pos_v_2, cmp_k_w1_2,
    cmp_k_b1_2, cmp_k_w2_2, cmp_v_w1_2, cmp_v_b1_2, cmp_v_w2_2, w_mem_kv_2, w_branch_conv_2,
    w_branch_nsa_2, w_branch_mem_2, w_mix_out_2, ffn2_norm_pre_2, ffn2_norm_post_2, ffn2_w_in_2,
    ffn2_w_out_2,
):
    x = first_block(
        x, mem, ffn1_norm, ffn1_w_in, ffn1_w_out, mix_norm, mem_norm, w_in, lru_conv_w,
        lru_conv_b, lru_a_w, lru_a_b, lru_x_w, lru_x_b, lru_lambda, moba_q_norm, moba_k_norm,
        mem_w_kv, mem_q_norm, mem_k_norm, w_out, ffn2_norm, ffn2_w_in, ffn2_w_out,
    )
    return second_block(
        x, mem_2, positions_2, ffn1_norm_pre_2, ffn1_norm_post_2, ffn1_w_in_2, ffn1_w_out_2,
        mix_norm_pre_2, mix_norm_post_2, mem_norm_2, w_mix_in_2, conv_w_2, cmp_pos_k_2,
        cmp_pos_v_2, cmp_k_w1_2, cmp_k_b1_2, cmp_k_w2_2, cmp_v_w1_2, cmp_v_b1_2, cmp_v_w2_2,
        w_mem_kv_2, w_branch_conv_2, w_branch_nsa_2, w_branch_mem_2, w_mix_out_2,
        ffn2_norm_pre_2, ffn2_norm_post_2, ffn2_w_in_2, ffn2_w_out_2,
    )


_drawn_inputs = setup_inputs


def setup_inputs(seed=0):
    import zlib

    import numpy as np

    out = dict(_drawn_inputs(seed))
    spreads = {}
    factors = {'ffn1_norm': 3.093,
     'mix_norm': 3.153,
     'mem_norm': 8.0,
     'lru_a_b': 55.08,
     'lru_x_b': 46.236,
     'moba_q_norm': 8.0,
     'moba_k_norm': 8.0,
     'mem_q_norm': 8.0,
     'mem_k_norm': 8.0,
     'ffn2_norm': 10.843,
     'mem_norm_2': 39.869,
     'cmp_pos_k_2': 64.0,
     'cmp_k_b1_2': 200.0,
     'cmp_v_b1_2': 200.0,
     'lru_conv_b': 4.967,
     'ffn1_norm_pre_2': 38.467,
     'ffn1_norm_post_2': 55.275,
     'mix_norm_post_2': 30.786,
     'cmp_pos_v_2': 8.0,
     'cmp_k_w1_2': 8.0,
     'cmp_k_w2_2': 8.0,
     'cmp_v_w1_2': 8.0,
     'cmp_v_w2_2': 8.0,
     'w_branch_nsa_2': 6.361,
     'ffn2_norm_pre_2': 44.349,
     'ffn2_norm_post_2': 64.0,
     'conv_w_2': 4.635,
     'w_branch_conv_2': 4.719}
    for name, (base, spread) in spreads.items():
        noise = np.random.default_rng([zlib.crc32(name.encode()), seed]).standard_normal(out[name].shape)
        drawn = base * np.exp(spread * noise) if base else spread * noise
        out[name] = __import__('jax').numpy.asarray(drawn.astype(out[name].dtype))
    for name, factor in factors.items():
        out[name] = (out[name] * factor).astype(out[name].dtype)
    return out
```

```python
from contextlib import ExitStack

import numpy as np

import concourse.bass as bass
from concourse import mybir

F32 = mybir.dt.float32
F32R = mybir.dt.float32r
I32 = mybir.dt.int32
ALU = mybir.AluOpType
ACT = mybir.ActivationFunctionType
AX_X = mybir.AxisListType.X

P = 128
T = 256
TT = T // P
D = 1024
KD = D // P
D_FF = 2816
LAYERS = 2
EPS = 1e-6
NEG = -1e30
BIG = 3e38
HD = 64
MEM_HD = 128
LRU_TILES = 4
LRU_C = 8.0
CONV_W = 4
CONV2_W = 3
CMP_BLOCK, CMP_STRIDE = 32, 16
N_CMP = T // CMP_STRIDE - 1
CMP_PAIRS = CMP_BLOCK // 2
GROUPS = 2
NSA_HEADS = 8
GATES = 3 * NSA_HEADS
ROT = 8
ROPE_THETA = 500000.0

UNIT = 2048
RING = 3
CHUNK = 256
CHUNKS = D_FF // CHUNK
FFN_UNITS = 3 * CHUNKS
B1_PARAM, B1_MEM, B1_FFN1 = 0, 1, 3
B1_QK = B1_FFN1 + FFN_UNITS
B1_VC, B1_LRU_X, B1_LRU_G, B1_OUT = B1_QK + 2, B1_QK + 4, B1_QK + 6, B1_QK + 8
B1_FFN2 = B1_OUT + 4
B1_UNITS = B1_FFN2 + FFN_UNITS
L_PARAM, L_MEM, L_FFN1 = 0, 2, 6
L_CONV = L_FFN1 + FFN_UNITS
L_KV, L_Q, L_KVS, L_QMEM, L_MERGE = L_CONV + 6, L_CONV + 7, L_CONV + 9, L_CONV + 11, L_CONV + 13
L_CMPK = L_MERGE + 12
L_CMPV, L_BR = L_CMPK + 2, L_CMPK + 4
L_OUT = L_BR + 6
L_FFN2 = L_OUT + 4
L_UNITS = L_FFN2 + FFN_UNITS
assert B1_UNITS % RING == 0 and L_UNITS % RING == 0
UNITS = B1_UNITS + LAYERS * L_UNITS

F1_MEM, F1_QK, F1_VC, F1_LRU_X, F1_LRU_G, F1_HEADS, F1_GATE, F1_FILLS = 0, 2, 4, 6, 8, 10, 14, 18
(F_MEMK, F_MEMV, F_CONV, F_KV, F_GATE, F_Q, F_KVS, F_QMEM, F_MERGE, F_ROT, F_PLAIN, F_HIDK, F_KC,
 F_HIDV, F_VC, F_FILLS) = 0, 2, 4, 10, 11, 12, 14, 16, 18, 30, 34, 36, 38, 39, 41, 42
assert F1_FILLS % 3 == 0 and F_FILLS % 3 == 0
S1_HEADS, S1_GATE, S1_SMALL = 0, 4, 8
S_GATE, S_ROT, S_PLAIN, S_KC, S_VC, S_SMALL = 0, 1, 5, 7, 8, 9

B1P, LP = {}, {}


def columns(table, widths):
    at = 0
    for name, width in widths:
        table[name] = (at, width)
        at += width
    return at


columns(B1P, [("a_w", 512), ("x_w", 512), ("conv_w", 16), ("conv_b", 4), ("a_b", 4), ("x_b", 4),
              ("lam", 4), ("g_mem", 8), ("g_ffn1", 8), ("g_mix", 8), ("g_ffn2", 8), ("g_heads", 4)])
columns(LP, [("post_ffn1", 1024), ("post_mix", 1024), ("post_ffn2", 1024), ("gate_w", KD * GATES),
             ("k_w2", 256), ("v_w2", 128), ("k_b1", 2), ("v_b1", 2), ("pos_k", 16), ("pos_v", 16),
             ("conv_w", 12), ("g_mem", 8), ("g_ffn1", 8), ("g_mix", 8), ("g_ffn2", 8)])
CONST = {}
CONST_N = columns(CONST, [("ident", P), ("causal", 384), ("zero", 1), ("cmp_mask", TT * 16),
                          ("cmp_valid", TT), ("inv_freq", ROT)])
ALIBI_N = 4 * 384


class Section:

    def __init__(self, layer=None):
        self.layer = layer

    def at(self, first, per_layer, k):
        return k if self.layer is None else self.layer * per_layer + (first + k)

    def unit(self, n):
        return self.at(B1_UNITS, L_UNITS, n)

    def landed(self, n):
        return self.at(16 * B1_UNITS // RING, 16 * L_UNITS // RING, 16 * (n // RING + 1))

    def small(self, f):
        return self.at(S1_SMALL, S_SMALL, f)

    def fill(self, f):
        return self.at(F1_FILLS, F_FILLS, f)


def wait(eng, sem, value):
    if not isinstance(value, int) or value > 0:
        eng.wait_ge(sem, value)


class Steps:

    def __init__(self, eng, sem, first, per_layer):
        self.eng, self.sem, self.totals = eng, sem, (first, per_layer)

    def enter(self, sec):
        self.sec, self.n = sec, 0

    def mark(self, ins):
        ins.then_inc(self.sem, 1)
        self.n += 1
        return self.sec.at(*self.totals, self.n)

    def after(self, value):
        self.eng.wait_ge(self.sem, value)

    def link(self, ins):
        self.after(self.mark(ins))

    def leave(self):
        want = self.totals[0 if self.sec.layer is None else 1]
        assert self.n == want, (self.n, self.totals)


class Job:

    def __init__(self, q, k, v, bias, scale, keys, causal, m, row, tile, first, last, factor=None):
        self.q, self.k, self.v, self.bias, self.scale = q, k, v, bias, scale
        self.keys, self.causal, self.m, self.row = keys, causal, m, row
        self.tile, self.first, self.last, self.factor = tile, first, last, factor
        self.key_tiles = -(-keys // P)
        self.tile_done = last and (m == P or row > 0)

    def width(self, i):
        return min(self.keys, P * (i + 1)) if self.causal else self.keys

    def rows(self, kt):
        return min(P, self.keys - P * kt)

    def span(self, kt):
        return P * kt if self.causal else 0

    def blocks(self):
        return [(kt, i, T * kt + P * i - self.span(kt))
                for kt in range(self.key_tiles) for i in range(TT) if P * i >= self.span(kt)]

    def pt_width(self):
        return T * self.key_tiles - sum(self.span(kt) for kt in range(self.key_tiles))


def build(nc, stream, x_in, mem1_in, mem2_in, pos_in, const_in, alibi_in, out):
    with ExitStack() as ctx:
        plan = {"at": -(-nc.sbuf_base // 64) * 64}

        def room(size):
            start = plan["at"]
            plan["at"] += -(-size // 32) * 32
            assert plan["at"] <= nc.sbuf_usable_end, plan["at"]
            return start

        def place(name, shape, start, dtype=F32):
            return nc.alloc_sbuf_tensor_at(name, shape, dtype, offset=start).ap()

        def new(name, shape, dtype=F32):
            return place(name, shape, room(4 * int(np.prod(shape[1:]))), dtype)

        raw = new("raw", [P, RING, UNIT])
        hi = new("hi", [P, RING, UNIT], F32R)
        lo = new("lo", [P, RING, UNIT], F32R)
        x = new("x", [P, TT, D])
        r_scaled = room(8192)
        xs = place("xs", [P, TT, D], r_scaled)
        heads1 = place("heads1", [P, TT, 16, HD], r_scaled)
        rot = place("rot", [P, TT, 16, HD], r_scaled)
        xT_hi = new("xT_hi", [P, KD, T], F32R)
        xT_lo = new("xT_lo", [P, KD, T], F32R)
        params = new("params", [P, 2 * UNIT])
        r_memk = room(4096)
        memkT = place("memkT", [P, 4, T], r_memk)
        lru_y = place("lru_y", [P, LRU_TILES, T], r_memk)
        memv = new("memv", [P, TT, 512])
        r_big = room(24576)
        mem_in = place("mem_in", [P, TT, D], r_big)
        lru_in = place("lru_in", [P, LRU_TILES, T + CONV_W - 1], r_big)
        lru_xb = place("lru_xb", [P, LRU_TILES, T], r_big + 4160)
        lru_r = place("lru_r", [P, LRU_TILES, T], r_big + 4160 + 4096)
        lru_i = place("lru_i", [P, LRU_TILES, T], r_big + 4160 + 2 * 4096)
        lru_a = place("lru_a", [P, LRU_TILES, T], r_big + 4160 + 3 * 4096)
        conv_in = place("conv_in", [P, 3 * 4 * T], r_big)
        conv_v = place("conv_v", [P, 4, T + CONV2_W - 1], r_big + 12288)
        conv_y = place("conv_y", [P, 4, T], r_big + 12288 + 4160)
        merge = place("merge", [P, 3 * KD * T], r_big)
        merged_hi = place("merged_hi", [P, KD, T], r_big, F32R)
        merged_lo = place("merged_lo", [P, KD, T], r_big + 8192, F32R)
        r_mix = room(24576)
        mix_hi = place("mix_hi", [P, KD, T], r_mix, F32R)
        mix_lo = place("mix_lo", [P, KD, T], r_mix + 8192, F32R)
        alibi = place("alibi", [P, 4, 384], r_mix + 16384)
        br_hi = [place(f"br_hi{b}", [P, 4, T], r_mix + 8192 * b, F32R) for b in range(3)]
        br_lo = [place(f"br_lo{b}", [P, 4, T], r_mix + 8192 * b + 4096, F32R) for b in range(3)]
        cmp_src = [place(f"cmp_src{c}", [P, GROUPS, T], r_mix + 8192 + 2048 * c) for c in range(2)]
        n_cmp = CMP_PAIRS * GROUPS * N_CMP * 4
        cmp_x = [place(f"cmp_x{c}", [P, CMP_PAIRS, GROUPS, N_CMP], r_mix + 12288 + 3 * n_cmp * c)
                 for c in range(2)]
        cmp_hi = [place(f"cmp_hi{c}", [P, CMP_PAIRS, GROUPS * N_CMP], r_mix + 12288 + 3 * n_cmp * c + n_cmp,
                        F32R) for c in range(2)]
        cmp_lo = [place(f"cmp_lo{c}", [P, CMP_PAIRS, GROUPS * N_CMP],
                        r_mix + 12288 + 3 * n_cmp * c + 2 * n_cmp, F32R) for c in range(2)]
        r_qT = room(4096)
        qT = place("qT", [P, 4, T], r_qT)
        lru_g = place("lru_g", [P, LRU_TILES, T], r_qT)
        hT_hi = place("hT_hi", [P, 2, T], r_qT, F32R)
        hT_lo = place("hT_lo", [P, 2, T], r_qT + 2048, F32R)
        r_headT = room(8192)
        headT = place("headT", [P, 8, T], r_headT)
        squares = place("squares", [P, TT, 16, HD], r_headT)
        merged = place("merged", [P, KD, T], r_headT)
        qmemT = new("qmemT", [P, 4, T])
        v_sb = new("v_sb", [P, TT, 2, P])
        r_prob = room(4096)
        prob = place("prob", [P, 2, TT, T], r_prob)
        lru_m = place("lru_m", [P, LRU_TILES, T], r_prob)
        silu_a = place("silu_a", [P, TT, CHUNK], r_prob)
        h_sb = place("h_sb", [P, TT, CHUNK], r_prob + 2048)
        rope_t = place("rope_t", [P, 4, TT, 16, ROT], r_prob)
        br_t = place("br_t", [P, 2, 512], r_prob)
        r_pT = room(4096)
        probT = place("probT", [P, 2, 512], r_pT)
        q_sb = place("q_sb", [P, TT, 512], r_pT)
        const = new("const", [P, CONST_N])
        gw_hi = place("gw_hi", [P, KD, GATES], r_pT, F32R)
        gw_lo = place("gw_lo", [P, KD, GATES], r_pT + 4 * KD * GATES, F32R)
        hid = [new(f"hid{c}", [P, 2, GROUPS * N_CMP]) for c in range(2)]
        kcT = new("kcT", [P, GROUPS * N_CMP])
        vc = new("vc", [P, GROUPS, HD])
        gates = new("gates", [P, TT, GATES])
        pos_i = new("pos_i", [P, TT], I32)
        angle = new("angle", [P, 6, TT * ROT])
        trig = new("trig", [P, 2, TT, ROT])
        sums = new("sums", [P, 32])
        var = new("var", [P, 32])
        rstd = new("rstd", [P, 32])
        ysums = new("ysums", [P, TT, 2])
        neg_half = new("neg_half", [P, 32])
        soft = new("soft", [P, 2, 3, TT])
        lam_t = new("lam_t", [P, 7, LRU_TILES])

        def cst(name):
            at, n = CONST[name]
            return const[:, at:at + n]

        def b1p(name):
            at, n = B1P[name]
            return params[:, at:at + n]

        def lp(name):
            at, n = LP[name]
            return params[:, at:at + n]

        ident = cst("ident")
        causal = cst("causal")
        cmp_mask = cst("cmp_mask").rearrange("p (i n) -> p i n", i=TT)

        def psum(name):
            return ctx.enter_context(nc.psum_tensor(name, [P, 4, 512], F32))

        acc = psum("acc")
        work = psum("work")

        def sem(name):
            return ctx.enter_context(nc.semaphore(name))

        landed = [sem(f"landed{s}") for s in range(RING)]
        hi_ready, lo_ready, unit_used = sem("hi_ready"), sem("lo_ready"), sem("unit_used")
        const_in_sem, x_loaded, mem_loaded = sem("const_loaded"), sem("x_loaded"), sem("mem_loaded")
        half_set = sem("half_set")
        sq_ready, pow_asked, pow_ready = sem("sq_ready"), sem("pow_asked"), sem("pow_ready")
        xs_ready, xT_ready = sem("xs_ready"), sem("xT_ready")
        xhi_ready, xlo_ready = sem("xhi_ready"), sem("xlo_ready")
        ab_ready, silu_ready, h_ready = sem("ab_ready"), sem("silu_ready"), sem("h_ready")
        hT_ready, hThi_ready, hTlo_ready = sem("hT_ready"), sem("hThi_ready"), sem("hTlo_ready")
        ysq_ready, x_ready = sem("ysq_ready"), sem("x_ready")
        small_ready, evac_done = sem("small_ready"), sem("evac_done")
        qk_ready, scored, exp_ready, p_ready = sem("qk_ready"), sem("scored"), sem("exp_ready"), sem("p_ready")
        pT_ready, pT_copied = sem("pT_ready"), sem("pT_copied")
        tile_ready, tile_hi, tile_lo = sem("tile_ready"), sem("tile_hi"), sem("tile_lo")
        trig_asked, trig_ready = sem("trig_asked"), sem("trig_ready")
        dve_step = sem("dve_step")
        heads_ready, lam_asked, lam_exp, lam_ready = (sem("heads_ready"), sem("lam_asked"), sem("lam_exp"),
                                                      sem("lam_ready"))
        xb_ready, lru_a_ready, m2_ready, mult_ready, lruy_ready, lruhi_ready = (
            sem("xb_ready"), sem("lru_a_ready"), sem("m2_ready"), sem("mult_ready"), sem("lruy_ready"),
            sem("lruhi_ready"))
        lrulo_ready = sem("lrulo_ready")
        gwhi_ready, gwlo_ready = sem("gwhi_ready"), sem("gwlo_ready")
        conv_ready, convhi_ready, convlo_ready = sem("conv_ready"), sem("convhi_ready"), sem("convlo_ready")
        rot_ready, cmpx_ready, cmphi_ready, cmplo_ready = (sem("rot_ready"), sem("cmpx_ready"),
                                                           sem("cmphi_ready"), sem("cmplo_ready"))
        valid_ready = sem("valid_ready")
        br_read, merged_ready = sem("br_read"), sem("merged_ready")
        mhi_ready, mlo_ready = sem("mhi_ready"), sem("mlo_ready")
        stored = sem("stored")

        block = ctx.enter_context(nc.Block())

        POWS = (5, 7)
        JOBS = (8, 28)
        TILES = (4, 8)

        def jobs_of(sec):
            if sec.layer is None:
                def head(kind, h):
                    return headT[HD * (h % 2):HD * (h % 2) + HD, 2 * kind + h // 2, :]

                made = []
                for h in range(4):
                    made.append(Job(
                        q=lambda i, h=h: head(0, h)[:, P * i:P * i + P], k=lambda n, h=h: head(1, h)[:, 0:n],
                        v=lambda kt, h=h: v_sb[:, kt, h // 2, HD * (h % 2):HD * (h % 2) + HD],
                        bias=lambda i, n, h=h: alibi[:, h, P * i:P * i + n], scale=HD ** -0.5, keys=T,
                        causal=True, m=HD, row=HD * (h % 2), tile=h // 2, first=True, last=True))
                for h in range(4):
                    made.append(Job(
                        q=lambda i, h=h: head(2, h)[:, P * i:P * i + P], k=lambda n, h=h: head(3, h)[:, 0:n],
                        v=lambda kt, h=h: memv[:, kt, T + HD * h:T + HD * h + HD],
                        bias=lambda i, n: cst("zero").to_broadcast([P, n]), scale=HD ** -0.5, keys=T,
                        causal=False, m=HD, row=HD * (h % 2), tile=2 + h // 2, first=True, last=True))
                return made
            made = []
            for h in range(NSA_HEADS):
                g, pair, row = h // (NSA_HEADS // GROUPS), h // 2, HD * (h % 2)
                rows = slice(row, row + HD)
                common = dict(scale=HD ** -0.5, m=HD, row=row, tile=pair)
                made.append(Job(
                    q=lambda i, rows=rows, pair=pair: qT[rows, pair, P * i:P * i + P],
                    k=lambda n, rows=rows, g=g: kcT[rows, N_CMP * g:N_CMP * g + n],
                    v=lambda kt, g=g: vc[0:N_CMP, g, :], bias=lambda i, n: cmp_mask[:, i, 0:n], keys=N_CMP,
                    causal=False, first=True, last=False,
                    factor=lambda i, h=h: gates[:, i, 3 * h:3 * h + 1], **common))
                for s in range(2):
                    made.append(Job(
                        q=lambda i, rows=rows, pair=pair: headT[rows, pair, P * i:P * i + P],
                        k=lambda n, rows=rows, g=g, s=s: headT[rows, 4 + 2 * s + g, 0:n],
                        v=lambda kt, g=g, s=s: v_sb[:, kt, s, HD * g:HD * g + HD],
                        bias=lambda i, n: causal[:, P * i:P * i + n], keys=T, causal=True,
                        first=False, last=s == 1,
                        factor=lambda i, h=h, s=s: gates[:, i, 3 * h + 1 + s:3 * h + 2 + s], **common))
            for h in range(4):
                made.append(Job(
                    q=lambda i, h=h: qmemT[:, h, P * i:P * i + P], k=lambda n, h=h: memkT[:, h, 0:n],
                    v=lambda kt, h=h: memv[:, kt, MEM_HD * h:MEM_HD * h + MEM_HD],
                    bias=lambda i, n: cst("zero").to_broadcast([P, n]), scale=MEM_HD ** -0.5, keys=T, causal=False, m=MEM_HD,
                    row=0, tile=4 + h, first=True, last=True))
            return made

        def tile_bank(t):
            return (acc, work)[t % 2][:, 3, 0:T]

        def tile_dst(sec, t):
            if sec.layer is None:
                return mix_hi[:, 4 + t, :], mix_lo[:, 4 + t, :]
            return br_hi[1 + t // 4][:, t % 4, :], br_lo[1 + t // 4][:, t % 4, :]

        @block.sync
        def _(sp):
            for s in range(RING):
                sp.dma_start(raw[:, s, :], stream[s]).then_inc(landed[s], 16)
            with sp.Fori(1, UNITS // RING) as turn:
                for s in range(RING):
                    sp.wait_ge(lo_ready, turn * RING + (s - RING + 1))
                    sp.dma_start(raw[:, s, :], stream[turn * RING + s]).then_inc(landed[s], 16)
            sp.wait_ge(x_ready, 12 * (1 + LAYERS))
            sp.dma_start(out.rearrange("(i p) d -> p i d", p=P), x).then_inc(stored, 16)
            sp.wait_ge(stored, 16)

        @block.gpsimd
        def _(pool):
            nc.gpsimd.memset(neg_half, -0.5).then_inc(half_set, 1)
            pool.wait_ge(half_set, 1)

            def inverse_roots(sec, widths):
                for k, n in enumerate(widths):
                    pool.wait_ge(pow_asked, sec.at(*POWS, k + 1))
                    nc.gpsimd.tensor_tensor(rstd[:, 0:n], var[:, 0:n], neg_half[:, 0:n], ALU.pow).then_inc(pow_ready, 1)

            inverse_roots(Section(), [TT, TT, TT, 32, TT])
            with pool.Fori(0, LAYERS) as layer:
                inverse_roots(Section(layer), [TT] * 7)

        @block.scalar
        def _(act):
            def split_high(sec, n, trip=0):
                s = n % RING
                wait(act, unit_used, sec.unit(n - RING + 1) + trip * RING)
                act.wait_ge(landed[s], sec.landed(n) + trip * 16)
                nc.scalar.activation(hi[:, s, :], raw[:, s, :], ACT.Copy).then_inc(hi_ready, 1)

            def copy_params(sec, n):
                act.wait_ge(landed[n % RING], sec.landed(n))
                nc.scalar.activation(params[:, n * UNIT:n * UNIT + 1024], raw[:, n % RING, 0:1024], ACT.Copy).then_inc(hi_ready, 1)

            def norm(sec, k, src, gain):
                for i in range(TT):
                    if k > 0:
                        wait(act, x_ready, sec.at(12, 12, 4 * (k - 2) + 2 * i + 2 if k > 1 else 0))
                    nc.scalar.activation(xs[:, i, :], src[:, i, :], ACT.Square, accum_out=sums[:, i:i + 1]).then_inc(sq_ready, 1)
                for kt in range(KD):
                    act.wait_ge(xT_ready, sec.at(16, 16, 4 * k + kt // 2 + 1))
                    nc.scalar.activation(xT_hi[:, kt, :], acc[:, kt // 2, T * (kt % 2):T * (kt % 2) + T], ACT.Copy,
                                         scale=gain[:, kt:kt + 1]).then_inc(xhi_ready, 1)

            def ffn(sec, u0, k, more):
                c0 = sec.at(2 * CHUNKS, 2 * CHUNKS, k * CHUNKS)

                def silu(j, n, trip=0):
                    for i in range(TT):
                        if i == 0:
                            act.wait_ge(ab_ready, c0 + j + 1)
                        else:
                            act.wait_ge(unit_used, sec.unit(n + 1) + trip * RING)
                        nc.scalar.activation(silu_a[:, i, :], work[:, i, 0:CHUNK], ACT.Silu).then_inc(silu_ready, 1)

                def high_hT(j):
                    act.wait_ge(hT_ready, c0 + j + 1)
                    nc.scalar.activation(hT_hi.rearrange("p f t -> p (f t)"), work[:, 2, :], ACT.Copy).then_inc(hThi_ready, 1)

                split_high(sec, u0 + 2)
                split_high(sec, u0 + 3)
                silu(0, u0 + 1)
                with act.Fori(1, CHUNKS - 1) as j:
                    high_hT(j - 1)
                    split_high(sec, u0 + 1, j)
                    split_high(sec, u0 + 2, j)
                    silu(j, u0, j)
                    split_high(sec, u0 + 3, j)
                last = CHUNKS - 1
                high_hT(last - 1)
                split_high(sec, u0 + 3 * last + 1)
                split_high(sec, u0 + 3 * last + 2)
                silu(last, u0 + 3 * last)
                if more:
                    split_high(sec, u0 + FFN_UNITS)
                high_hT(last)
                if more:
                    split_high(sec, u0 + FFN_UNITS + 1)

            def post_sums(sec, n, r):
                act.wait_ge(unit_used, sec.unit(n + 1))
                for b in range(4):
                    i, c = b // 2, b % 2
                    nc.scalar.activation(xs[:, i, 512 * c:512 * c + 512], acc[:, b, :], ACT.Square,
                                         accum_out=ysums[:, i, c:c + 1]).then_inc(ysq_ready, 1)

            def by_unit(sec, f, n, trip=0):
                act.wait_ge(unit_used, sec.unit(n + 1) + trip * RING)
                return work[:, f % 3, :]

            def by_small(sec, f, k):
                act.wait_ge(small_ready, sec.small(k + 1))
                return work[:, f % 3, :]

            def copy_out(bank, dst, func=ACT.Copy):
                nc.scalar.activation(dst, bank, func).then_inc(evac_done, 1)

            def attention(sec):
                jobs = jobs_of(sec)

                def exps(n, job):
                    for i in range(TT):
                        act.wait_ge(scored, sec.at(2 * JOBS[0], 2 * JOBS[1], 2 * n + i + 1))
                        p = prob[:, n % 2, i, 0:job.width(i)]
                        nc.scalar.activation(p, p, ACT.Exp, bias=soft[:, n % 2, 0, i:i + 1], scale=-1.0,
                                             accum_out=soft[:, n % 2, 1, i:i + 1]).then_inc(exp_ready, 1)

                def copy_pT(n, job):
                    act.wait_ge(pT_ready, sec.at(*JOBS, n + 1))
                    r, w = job.rows(0), job.pt_width()
                    nc.scalar.activation(probT[0:r, n % 2, 0:w], acc[0:r, 2, 0:w], ACT.Copy).then_inc(pT_copied, 1)

                def high_tile(job):
                    act.wait_ge(tile_ready, sec.at(*TILES, job.tile + 1))
                    nc.scalar.activation(tile_dst(sec, job.tile)[0], tile_bank(job.tile),
                                         ACT.Copy).then_inc(tile_hi, 1)

                exps(0, jobs[0])
                for n, job in enumerate(jobs):
                    if n + 1 < len(jobs):
                        exps(n + 1, jobs[n + 1])
                    copy_pT(n, job)
                    if n and jobs[n - 1].tile_done:
                        high_tile(jobs[n - 1])
                high_tile(jobs[-1])

            act.dma_start(mem_in, mem1_in.rearrange("(i p) d -> p i d", p=P)).then_inc(mem_loaded, 16)
            act.dma_start(x, x_in.rearrange("(i p) d -> p i d", p=P)).then_inc(x_loaded, 16)
            act.dma_start(const, const_in).then_inc(const_in_sem, 16)
            act.dma_start(pos_i, pos_in).then_inc(const_in_sem, 16)
            act.dma_start(alibi.rearrange("p h n -> p (h n)"), alibi_in).then_inc(const_in_sem, 16)
            sec = Section()
            copy_params(sec, 0)
            act.wait_ge(lo_ready, 1)
            act.wait_ge(trig_asked, 1)
            nc.scalar.activation(trig.rearrange("p c i r -> p (c i r)"), angle[:, 4:6, :].rearrange("p c n -> p (c n)"),
                                 ACT.Sin).then_inc(trig_ready, 1)
            act.wait_ge(lam_asked, 1)
            nc.scalar.activation(lam_t[:, 1, :], lam_t[:, 0, :], ACT.Exp).then_inc(lam_exp, 1)
            act.wait_ge(mem_loaded, 16)
            split_high(sec, B1_MEM)
            split_high(sec, B1_MEM + 1)
            norm(sec, 0, mem_in, b1p("g_mem"))
            split_high(sec, B1_MEM + 2)
            split_high(sec, B1_MEM + 3)
            act.wait_ge(x_loaded, 16)
            for i in range(TT):
                copy_out(by_unit(sec, F1_MEM + i, B1_MEM + 1), memv[:, i, :])
            norm(sec, 1, x, b1p("g_ffn1"))
            ffn(sec, B1_FFN1, 0, True)
            norm(sec, 2, x, b1p("g_mix"))
            split_high(sec, B1_QK + 2)
            split_high(sec, B1_QK + 3)
            for i in range(TT):
                copy_out(by_unit(sec, F1_QK + i, B1_QK + 1), heads1[:, i, 0:8, :].rearrange("p h d -> p (h d)"))
            split_high(sec, B1_VC + 2)
            split_high(sec, B1_VC + 3)
            for i in range(TT):
                bank = by_unit(sec, F1_VC + i, B1_VC + 1)
                nc.scalar.activation(v_sb[:, i, :, :].rearrange("p s n -> p (s n)"), bank[:, 0:T], ACT.Copy)
                nc.scalar.activation(heads1[:, i, 8:12, :].rearrange("p h d -> p (h d)"), bank[:, T:2 * T],
                                     ACT.Copy).then_inc(evac_done, 1)
            for w in range(2):
                split_high(sec, B1_LRU_X + w + 2)
                bank = by_unit(sec, F1_LRU_X + w, B1_LRU_X + w)
                nc.scalar.activation(lru_in[:, 2 * w:2 * w + 2, CONV_W - 1:], bank.rearrange("p (c t) -> p c t", c=2),
                                     ACT.Copy).then_inc(evac_done, 1)
            for w in range(2):
                split_high(sec, B1_LRU_G + w + 2)
                copy_out(by_unit(sec, F1_LRU_G + w, B1_LRU_G + w), lru_g[:, 2 * w:2 * w + 2, :].rearrange("p c t -> p (c t)"), ACT.Gelu_apprx_tanh)
            for kind in range(4):
                bank = by_small(sec, F1_HEADS + kind, S1_HEADS + kind)
                nc.scalar.activation(headT[:, 2 * kind:2 * kind + 2, :].rearrange("p c t -> p (c t)"), bank, ACT.Copy,
                                     scale=b1p("g_heads")[:, kind:kind + 1]).then_inc(evac_done, 1)
            for w in range(4):
                bank = by_small(sec, F1_GATE + w, S1_GATE + w)
                dst, bias = (lru_r, b1p("a_b")) if w < 2 else (lru_i, b1p("x_b"))
                for c in range(2):
                    ct = 2 * (w % 2) + c
                    ins = nc.scalar.activation(dst[:, ct, :], bank[:, T * c:T * c + T], ACT.Sigmoid, bias=bias[:, ct:ct + 1])
                ins.then_inc(evac_done, 1)
            act.wait_ge(lam_ready, 1)
            act.wait_ge(evac_done, F1_GATE + 2)
            for ct in range(LRU_TILES):
                nc.scalar.activation(lru_a[:, ct, :], lru_r[:, ct, :], ACT.Exp, scale=lam_t[:, 5, ct:ct + 1])
                ins = nc.scalar.activation(lru_m[:, ct, :], lru_r[:, ct, :], ACT.Tanh, scale=lam_t[:, 6, ct:ct + 1])
            ins.then_inc(lru_a_ready, 1)
            act.wait_ge(m2_ready, 1)
            nc.scalar.activation(lru_r, lru_m, ACT.Sqrt).then_inc(mult_ready, 1)
            act.wait_ge(lruy_ready, 1)
            nc.scalar.activation(mix_hi[:, 0:LRU_TILES, :], lru_y, ACT.Copy).then_inc(lruhi_ready, 1)
            attention(sec)
            for w in range(4):
                split_high(sec, B1_OUT + w + 2)
            norm(sec, 3, x, b1p("g_ffn2"))
            ffn(sec, B1_FFN2, 1, False)

            with act.Fori(0, LAYERS) as layer:
                sec = Section(layer)
                act.wait_ge(x_ready, layer * 12 + 8)
                act.dma_start(mem_in, mem2_in.rearrange("(i p) d -> p i d", p=P)).then_inc(mem_loaded, 16)
                act.wait_ge(x_ready, layer * 12 + 12)
                copy_params(sec, 0)
                copy_params(sec, 1)
                act.wait_ge(lo_ready, sec.unit(2))
                split_high(sec, L_MEM)
                split_high(sec, L_MEM + 1)
                nc.scalar.activation(gw_hi.rearrange("p k n -> p (k n)"), lp("gate_w"), ACT.Copy).then_inc(gwhi_ready, 1)
                act.wait_ge(mem_loaded, layer * 16 + 32)
                norm(sec, 0, mem_in, lp("g_mem"))
                for w in range(2):
                    split_high(sec, L_MEM + w + 2)
                    copy_out(by_unit(sec, F_MEMK + w, L_MEM + w), memkT[:, 2 * w:2 * w + 2, :].rearrange("p c t -> p (c t)"))
                split_high(sec, L_MEM + 4)
                split_high(sec, L_MEM + 5)
                for i in range(TT):
                    copy_out(by_unit(sec, F_MEMV + i, L_MEM + 3), memv[:, i, :])
                norm(sec, 1, x, lp("g_ffn1"))
                ffn(sec, L_FFN1, 0, True)
                post_sums(sec, L_CONV - 1, 0)
                norm(sec, 2, x, lp("g_mix"))
                with act.Fori(0, 2) as trip:
                    for w in range(3):
                        split_high(sec, L_CONV + w + 2, trip)
                        copy_out(by_unit(sec, F_CONV + w, L_CONV + w, trip), conv_in[:, bass.ds(trip * 1536 + 512 * w, 512)])
                split_high(sec, L_KV + 2)
                bank = by_unit(sec, F_KV, L_KV)
                for c in range(2):
                    for g in range(GROUPS):
                        part = bank[HD * g:HD * g + HD, T * c:T * c + T]
                        nc.scalar.activation(cmp_src[c][0:HD, g, :], part, ACT.Copy)
                        ins = nc.scalar.activation(cmp_src[c][HD:P, g, 0:T - 1], part[:, 1:T], ACT.Copy)
                ins.then_inc(evac_done, 1)
                bank = by_small(sec, F_GATE, S_GATE)
                nc.scalar.activation(gates.rearrange("p i n -> p (i n)"), bank[:, 0:TT * GATES], ACT.Sigmoid).then_inc(evac_done, 1)
                split_high(sec, L_Q + 2)
                split_high(sec, L_Q + 3)
                for i in range(TT):
                    bank = by_unit(sec, F_Q + i, L_Q + 1)
                    nc.scalar.activation(q_sb[:, i, :], bank, ACT.Copy)
                    nc.scalar.activation(rot[:, i, 0:8, :].rearrange("p h d -> p (h d)"), bank, ACT.Copy).then_inc(evac_done, 1)
                split_high(sec, L_KVS + 2)
                split_high(sec, L_KVS + 3)
                for i in range(TT):
                    bank = by_unit(sec, F_KVS + i, L_KVS + 1).rearrange("p (s kv g d) -> p s kv g d", s=2, kv=2, g=GROUPS)
                    dst = rot[:, i, 8:16, :].rearrange("p (s g u) d -> p s g u d", s=2, g=GROUPS)
                    for u in range(2):
                        nc.scalar.activation(dst[:, :, :, u, :], bank[:, :, 0, :, :], ACT.Copy)
                    nc.scalar.activation(v_sb[:, i, :, :].rearrange("p s (g d) -> p s g d", g=GROUPS),
                                         bank[:, :, 1, :, :], ACT.Copy).then_inc(evac_done, 1)
                for w in range(2):
                    split_high(sec, L_QMEM + w + 2)
                    copy_out(by_unit(sec, F_QMEM + w, L_QMEM + w), qmemT[:, 2 * w:2 * w + 2, :].rearrange("p c t -> p (c t)"))
                act.wait_ge(conv_ready, layer + 1)
                nc.scalar.activation(br_hi[0], conv_y, ACT.Copy).then_inc(convhi_ready, 1)
                act.wait_ge(cmpx_ready, layer * 2 + 2)
                for c in range(2):
                    nc.scalar.activation(cmp_hi[c], cmp_x[c].rearrange("p m g n -> p m (g n)"), ACT.Copy).then_inc(cmphi_ready, 1)
                act.wait_ge(convlo_ready, layer + 1)
                with act.Fori(0, 4) as trip:
                    for w in range(3):
                        split_high(sec, L_MERGE + w + 2, trip)
                        copy_out(by_unit(sec, F_MERGE + w, L_MERGE + w, trip), merge[:, bass.ds(trip * 1536 + 512 * w, 512)],
                                 ACT.Sigmoid)
                for w in range(4):
                    copy_out(by_small(sec, F_ROT + w, S_ROT + w), headT[:, 2 * w:2 * w + 2, :].rearrange("p c t -> p (c t)"))
                for w in range(2):
                    copy_out(by_small(sec, F_PLAIN + w, S_PLAIN + w), qT[:, 2 * w:2 * w + 2, :].rearrange("p c t -> p (c t)"))
                for c, (units, fills, bias) in enumerate(((L_CMPK, F_HIDK, "k_b1"), (L_CMPV, F_HIDV, "v_b1"))):
                    for t in range(2):
                        split_high(sec, units + t + 2)
                        bank = by_unit(sec, fills + t, units + t)
                        nc.scalar.activation(hid[c][:, t, :], bank[:, 0:GROUPS * N_CMP], ACT.Gelu_apprx_tanh,
                                             bias=lp(bias)[:, t:t + 1]).then_inc(evac_done, 1)
                    if c == 0:
                        bank = by_small(sec, F_KC, S_KC)
                        nc.scalar.activation(kcT, bank[:, 0:GROUPS * N_CMP], ACT.Copy).then_inc(evac_done, 1)
                    else:
                        bank = by_small(sec, F_VC, S_VC)
                        nc.scalar.activation(vc[0:N_CMP, :, :].rearrange("p g d -> p (g d)"), bank[0:N_CMP, 0:GROUPS * HD],
                                             ACT.Copy).then_inc(evac_done, 1)
                attention(sec)
                for w in range(6):
                    split_high(sec, L_BR + w + 2)
                act.wait_ge(merged_ready, layer * 2 + 2)
                for c in range(2):
                    nc.scalar.activation(merged_hi[:, 4 * c:4 * c + 4, :], merged[:, 4 * c:4 * c + 4, :], ACT.Copy).then_inc(mhi_ready, 1)
                for w in range(4):
                    split_high(sec, L_OUT + w + 2)
                post_sums(sec, L_FFN2 - 1, 1)
                norm(sec, 3, x, lp("g_ffn2"))
                ffn(sec, L_FFN2, 1, False)
                post_sums(sec, L_UNITS - 1, 2)
    
        @block.vector
        def _(dve):
            step = Steps(dve, dve_step, DVE_STEPS[0], DVE_STEPS[1])

            def split_low(sec, n, trip=0):
                s = n % RING
                dve.wait_ge(hi_ready, sec.unit(n + 1) + trip * RING)
                nc.vector.tensor_tensor(lo[:, s, :], raw[:, s, :], hi[:, s, :].bitcast(F32), ALU.subtract).then_inc(lo_ready, 1)

            def copy_params(sec, n):
                dve.wait_ge(hi_ready, sec.unit(n + 1))
                nc.vector.tensor_copy(params[:, n * UNIT + 1024:(n + 1) * UNIT], raw[:, n % RING, 1024:UNIT]).then_inc(lo_ready, 1)

            def norm(sec, k, p, src, gain):
                dve.wait_ge(sq_ready, sec.at(8, 8, 2 * k + 2))
                nc.vector.tensor_scalar(var[:, 0:TT], sums[:, 0:TT], 1.0 / D, EPS, ALU.mult, ALU.add).then_inc(pow_asked, 1)
                dve.wait_ge(pow_ready, sec.at(*POWS, p + 1))
                for i in range(TT):
                    nc.vector.tensor_scalar(xs[:, i, :], src[:, i, :], rstd[:, i:i + 1], None, ALU.mult).then_inc(xs_ready, 1)
                for kt in range(KD):
                    if kt % 2 == 0:
                        dve.wait_ge(xhi_ready, sec.at(32, 32, 8 * k + kt + 2))
                    nc.vector.scalar_tensor_tensor(xT_lo[:, kt, :], acc[:, kt // 2, T * (kt % 2):T * (kt % 2) + T],
                                                   gain[:, kt:kt + 1], xT_hi[:, kt, :].bitcast(F32), ALU.mult,
                                                   ALU.subtract).then_inc(xlo_ready, 1)

            def ffn(sec, u0, k, more):
                c0 = sec.at(2 * CHUNKS, 2 * CHUNKS, k * CHUNKS)

                def gated(j):
                    for i in range(TT):
                        dve.wait_ge(silu_ready, (c0 + j) * 2 + (i + 1))
                        nc.vector.tensor_tensor(h_sb[:, i, :], silu_a[:, i, :], work[:, i, CHUNK:2 * CHUNK], ALU.mult).then_inc(h_ready, 1)

                def low_hT(j):
                    dve.wait_ge(hThi_ready, c0 + j + 1)
                    nc.vector.tensor_tensor(hT_lo.rearrange("p f t -> p (f t)"), work[:, 2, :],
                                            hT_hi.rearrange("p f t -> p (f t)").bitcast(F32), ALU.subtract).then_inc(hTlo_ready, 1)

                split_low(sec, u0 + 2)
                split_low(sec, u0 + 3)
                gated(0)
                with dve.Fori(1, CHUNKS - 1) as j:
                    low_hT(j - 1)
                    split_low(sec, u0 + 1, j)
                    split_low(sec, u0 + 2, j)
                    gated(j)
                    split_low(sec, u0 + 3, j)
                last = CHUNKS - 1
                low_hT(last - 1)
                split_low(sec, u0 + 3 * last + 1)
                split_low(sec, u0 + 3 * last + 2)
                gated(last)
                if more:
                    split_low(sec, u0 + FFN_UNITS)
                low_hT(last)
                if more:
                    split_low(sec, u0 + FFN_UNITS + 1)

            def residual(sec, n, scale):
                dve.wait_ge(unit_used, sec.unit(n + 1))
                for b in range(4):
                    part = x[:, b // 2, 512 * (b % 2):512 * (b % 2) + 512]
                    nc.vector.scalar_tensor_tensor(part, acc[:, b, :], scale, part, ALU.mult, ALU.add).then_inc(x_ready, 1)

            def post_residual(sec, r, p, scale, gain):
                dve.wait_ge(ysq_ready, sec.at(0, 12, 4 * r + 4))
                step.link(nc.vector.tensor_tensor(var[:, 2:4], ysums[:, :, 0], ysums[:, :, 1], ALU.add))
                nc.vector.tensor_scalar(var[:, 0:TT], var[:, 2:4], 1.0 / D, EPS, ALU.mult, ALU.add).then_inc(pow_asked, 1)
                dve.wait_ge(pow_ready, sec.at(*POWS, p + 1))
                marks = []
                for b in range(4):
                    i, c = b // 2, slice(512 * (b % 2), 512 * (b % 2) + 512)
                    marks.append(step.mark(nc.vector.scalar_tensor_tensor(
                        xs[:, i, c], acc[:, b, :], rstd[:, i:i + 1], gain[:, c], ALU.mult, ALU.mult)))
                for b in range(4):
                    i, c = b // 2, slice(512 * (b % 2), 512 * (b % 2) + 512)
                    step.after(marks[b])
                    nc.vector.scalar_tensor_tensor(x[:, i, c], xs[:, i, c], scale, x[:, i, c], ALU.mult, ALU.add).then_inc(x_ready, 1)

            def attention(sec):
                jobs = jobs_of(sec)

                def score(n, job):
                    dve.wait_ge(qk_ready, sec.at(*JOBS, n + 1))
                    nc.vector.memset(soft[:, n % 2, 2, :], 0.0)
                    for i in range(TT):
                        w = job.width(i)
                        nc.vector.tensor_tensor_reduce(
                            out=prob[:, n % 2, i, 0:w], in0=acc[:, n % 2, T * i:T * i + w], in1=job.bias(i, w),
                            scale=-job.scale, scalar=BIG, op0=ALU.add, op1=ALU.min,
                            accum_out=soft[:, n % 2, 0, i:i + 1]).then_inc(scored, 1)

                def normalise(n, job):
                    dve.wait_ge(exp_ready, sec.at(2 * JOBS[0], 2 * JOBS[1], 2 * n + 2))
                    step.link(nc.vector.reciprocal(soft[:, n % 2, 2, :], soft[:, n % 2, 1, :]))
                    for i in range(TT):
                        p = prob[:, n % 2, i, 0:job.width(i)]
                        if job.factor is None:
                            ins = nc.vector.tensor_scalar(p, p, soft[:, n % 2, 2, i:i + 1], None, ALU.mult)
                        else:
                            ins = nc.vector.tensor_scalar(p, p, soft[:, n % 2, 2, i:i + 1], job.factor(i), ALU.mult, ALU.mult)
                        ins.then_inc(p_ready, 1)

                def low_tile(job):
                    dve.wait_ge(tile_hi, sec.at(*TILES, job.tile + 1))
                    high, low = tile_dst(sec, job.tile)
                    nc.vector.tensor_tensor(low, tile_bank(job.tile), high.bitcast(F32),
                                            ALU.subtract).then_inc(tile_lo, 1)

                score(0, jobs[0])
                for n, job in enumerate(jobs):
                    if n + 1 < len(jobs):
                        score(n + 1, jobs[n + 1])
                    normalise(n, job)
                    if n and jobs[n - 1].tile_done:
                        low_tile(jobs[n - 1])
                low_tile(jobs[-1])

            sec = Section()
            step.enter(sec)
            copy_params(sec, 0)
            dve.wait_ge(const_in_sem, 48)
            step.link(nc.vector.tensor_copy(angle[:, 0, 0:TT], pos_i))
            for i in range(TT):
                ins = nc.vector.tensor_scalar(angle[:, 1, ROT * i:ROT * i + ROT], cst("inv_freq"), angle[:, 0, i:i + 1],
                                              None, ALU.mult)
            step.link(ins)
            step.link(nc.vector.tensor_scalar(angle[:, 2, :], angle[:, 1, :], 1.0 / TURN, ROUND, ALU.mult, ALU.add))
            step.link(nc.vector.tensor_scalar(angle[:, 2, :], angle[:, 2, :], -ROUND, None, ALU.add))
            for part in TURN_PARTS:
                step.link(nc.vector.scalar_tensor_tensor(angle[:, 1, :], angle[:, 2, :], -part, angle[:, 1, :], ALU.mult, ALU.add))
            step.link(nc.vector.tensor_scalar(angle[:, 5, :], angle[:, 1, :], PI, -PI, ALU.min, ALU.max))
            step.link(nc.vector.tensor_scalar(angle[:, 3, :], angle[:, 5, :], -1.0, None, ALU.mult))
            step.link(nc.vector.tensor_tensor(angle[:, 3, :], angle[:, 3, :], angle[:, 5, :], ALU.max))
            nc.vector.tensor_scalar(angle[:, 4, :], angle[:, 3, :], -1.0, PI / 2, ALU.mult, ALU.add).then_inc(trig_asked, 1)
            lam = b1p("lam")
            dve.wait_ge(lo_ready, 1)
            step.link(nc.vector.tensor_scalar(lam_t[:, 2, :], lam, -1.0, None, ALU.mult))
            nc.vector.tensor_tensor(lam_t[:, 0, :], lam, lam_t[:, 2, :], ALU.min).then_inc(lam_asked, 1)
            dve.wait_ge(lam_exp, 1)
            step.link(nc.vector.tensor_scalar(lam_t[:, 3, :], lam_t[:, 1, :], 2.0, None, ALU.add))
            step.link(nc.vector.reciprocal(lam_t[:, 3, :], lam_t[:, 3, :]))
            step.link(nc.vector.tensor_tensor(lam_t[:, 3, :], lam_t[:, 1, :], lam_t[:, 3, :], ALU.mult))
            step.link(nc.vector.tensor_tensor(lam_t[:, 4, :], lam_t[:, 3, :], lam_t[:, 3, :], ALU.mult))
            step.link(nc.vector.tensor_scalar(lam_t[:, 5, :], lam_t[:, 4, :], 1.0 / 17, None, ALU.mult))
            for odd in (15, 13, 11, 9, 7, 5, 3):
                step.link(nc.vector.scalar_tensor_tensor(lam_t[:, 5, :], lam_t[:, 5, :], 1.0 / odd, lam_t[:, 4, :], ALU.add, ALU.mult))
            step.link(nc.vector.scalar_tensor_tensor(lam_t[:, 5, :], lam_t[:, 5, :], 1.0, lam_t[:, 3, :], ALU.add, ALU.mult))
            step.link(nc.vector.tensor_scalar(lam_t[:, 2, :], lam_t[:, 2, :], 0.0, None, ALU.max))
            step.link(nc.vector.scalar_tensor_tensor(lam_t[:, 2, :], lam_t[:, 5, :], 2.0, lam_t[:, 2, :], ALU.mult, ALU.add))
            nc.vector.tensor_scalar(lam_t[:, 5, :], lam_t[:, 2, :], -LRU_C, None, ALU.mult)
            nc.vector.tensor_scalar(lam_t[:, 6, :], lam_t[:, 2, :], LRU_C, None, ALU.mult).then_inc(lam_ready, 1)
            split_low(sec, B1_MEM)
            split_low(sec, B1_MEM + 1)
            norm(sec, 0, 0, mem_in, b1p("g_mem"))
            split_low(sec, B1_MEM + 2)
            split_low(sec, B1_MEM + 3)
            norm(sec, 1, 1, x, b1p("g_ffn1"))
            ffn(sec, B1_FFN1, 0, True)
            residual(sec, B1_QK - 1, 0.5)
            norm(sec, 2, 2, x, b1p("g_mix"))
            split_low(sec, B1_QK + 2)
            split_low(sec, B1_QK + 3)
            dve.wait_ge(evac_done, F1_MEM + 2)
            pads = step.mark(nc.vector.memset(lru_in[:, :, 0:CONV_W - 1], 0.0))
            split_low(sec, B1_VC + 2)
            split_low(sec, B1_VC + 3)
            dve.wait_ge(evac_done, F1_VC)
            for i in range(TT):
                ins = nc.vector.tensor_copy(heads1[:, i, 12:16, :].rearrange("p h d -> p (h d)"), memv[:, i, 0:T])
            step.link(ins)
            split_low(sec, B1_LRU_X + 2)
            dve.wait_ge(evac_done, F1_VC + 2)
            flat = heads1.rearrange("p i h d -> p (i h) d")
            flat_sq = squares.rearrange("p i h d -> p (i h) d")
            step.link(nc.vector.tensor_tensor(flat_sq, flat, flat, ALU.mult))
            step.link(nc.vector.reduce_sum(sums, flat_sq, axis=AX_X))
            nc.vector.tensor_scalar(var, sums, 1.0 / HD, EPS, ALU.mult, ALU.add).then_inc(pow_asked, 1)
            split_low(sec, B1_LRU_X + 3)
            dve.wait_ge(pow_ready, 4)
            nc.vector.tensor_tensor(flat, flat, rstd.unsqueeze(2).to_broadcast([P, 32, HD]), ALU.mult).then_inc(heads_ready, 1)
            conv_w = b1p("conv_w").rearrange("p (c w) -> p c w", c=LRU_TILES)
            for pair in range(2):
                split_low(sec, B1_LRU_G + pair + 2)
                dve.wait_ge(evac_done, F1_LRU_X + pair + 1)
                step.after(pads)
                for tap in range(CONV_W):
                    for c in (2 * pair, 2 * pair + 1):
                        shifted = lru_in[:, c, tap:tap + T]
                        if tap == 0:
                            m = step.mark(nc.vector.tensor_scalar(lru_xb[:, c, :], shifted, conv_w[:, c, 0:1],
                                                                  b1p("conv_b")[:, c:c + 1], ALU.mult, ALU.add))
                            continue
                        step.after(m - 1 + c % 2 if tap == 1 or c % 2 == 0 else m)
                        ins = nc.vector.scalar_tensor_tensor(lru_xb[:, c, :], shifted, conv_w[:, c, tap:tap + 1],
                                                             lru_xb[:, c, :], ALU.mult, ALU.add)
                        if tap < CONV_W - 1:
                            m = step.mark(ins)
                        elif c % 2:
                            ins.then_inc(xb_ready, 1)
            dve.wait_ge(lru_a_ready, 1)
            step.link(nc.vector.tensor_tensor(lru_y, lru_a, lru_a, ALU.mult))
            nc.vector.scalar_tensor_tensor(lru_m, lru_y, 1.0, lru_m, ALU.add, ALU.mult).then_inc(m2_ready, 1)
            dve.wait_ge(evac_done, F1_GATE + 4)
            step.link(nc.vector.tensor_tensor(lru_xb, lru_xb, lru_i, ALU.mult))
            dve.wait_ge(mult_ready, 1)
            step.link(nc.vector.memset(lru_r[:, :, 0:1], 1.0))
            step.link(nc.vector.tensor_tensor(lru_xb, lru_xb, lru_r, ALU.mult))
            for c in range(LRU_TILES):
                ins = nc.vector.tensor_tensor_scan(lru_m[:, c, :], lru_a[:, c, :], lru_xb[:, c, :], 0.0, ALU.mult, ALU.add)
            step.link(ins)
            nc.vector.tensor_tensor(lru_y, lru_m, lru_g, ALU.mult).then_inc(lruy_ready, 1)
            dve.wait_ge(lruhi_ready, 1)
            nc.vector.tensor_tensor(mix_lo[:, 0:LRU_TILES, :], lru_y, mix_hi[:, 0:LRU_TILES, :].bitcast(F32),
                                    ALU.subtract).then_inc(lrulo_ready, 1)
            attention(sec)
            for w in range(4):
                split_low(sec, B1_OUT + w + 2)
            residual(sec, B1_FFN2 - 1, 1.0)
            norm(sec, 3, 4, x, b1p("g_ffn2"))
            ffn(sec, B1_FFN2, 1, False)
            residual(sec, B1_UNITS - 1, 0.5)
            step.leave()

            with dve.Fori(0, LAYERS) as layer:
                sec = Section(layer)
                step.enter(sec)
                copy_params(sec, 0)
                copy_params(sec, 1)
                split_low(sec, L_MEM)
                split_low(sec, L_MEM + 1)
                dve.wait_ge(lo_ready, sec.unit(2))
                dve.wait_ge(gwhi_ready, layer + 1)
                nc.vector.tensor_tensor(gw_lo.rearrange("p k n -> p (k n)"), lp("gate_w"),
                                        gw_hi.rearrange("p k n -> p (k n)").bitcast(F32), ALU.subtract).then_inc(gwlo_ready, 1)
                norm(sec, 0, 0, mem_in, lp("g_mem"))
                for w in range(4):
                    split_low(sec, L_MEM + w + 2)
                norm(sec, 1, 1, x, lp("g_ffn1"))
                ffn(sec, L_FFN1, 0, True)
                post_residual(sec, 0, 2, 0.5, lp("post_ffn1"))
                norm(sec, 2, 3, x, lp("g_mix"))
                with dve.Fori(0, 2) as trip:
                    for w in range(3):
                        split_low(sec, L_CONV + w + 2, trip)
                split_low(sec, L_KV + 2)
                convolved = conv_in.rearrange("p (k c t) -> p k c t", k=3, c=4)
                conv_w = lp("conv_w").rearrange("p (c w) -> p c w", c=4)

                def conv_tile(c):
                    for tap in range(CONV2_W):
                        shifted = conv_v[:, c, tap:tap + T]
                        if tap == 0:
                            step.link(nc.vector.tensor_scalar(conv_y[:, c, :], shifted, conv_w[:, c, 0:1], None, ALU.mult))
                        else:
                            step.link(nc.vector.scalar_tensor_tensor(conv_y[:, c, :], shifted, conv_w[:, c, tap:tap + 1],
                                                                     conv_y[:, c, :], ALU.mult, ALU.add))
                    return nc.vector.tensor_tensor(conv_y[:, c, :], conv_y[:, c, :], convolved[:, 1, c, :], ALU.mult)

                dve.wait_ge(evac_done, sec.fill(F_KV))
                step.link(nc.vector.memset(conv_v[:, :, 0:CONV2_W - 1], 0.0))
                step.link(nc.vector.tensor_tensor(conv_v[:, :, CONV2_W - 1:], convolved[:, 2, :, :], convolved[:, 0, :, :], ALU.mult))
                split_low(sec, L_Q + 2)
                conv_tile(0)
                split_low(sec, L_Q + 3)
                conv_tile(1)
                dve.wait_ge(evac_done, sec.fill(F_GATE + 1))
                for i in range(TT):
                    g0 = gates[:, i, :].rearrange("p (h b) -> p h b", b=3)[:, :, 0]
                    ins = nc.vector.tensor_scalar(g0, g0, cst("cmp_valid")[:, i:i + 1], None, ALU.mult)
                step.link(ins)
                split_low(sec, L_KVS + 2)
                conv_tile(2)
                split_low(sec, L_KVS + 3)
                conv_tile(3).then_inc(conv_ready, 1)
                split_low(sec, L_QMEM + 2)
                split_low(sec, L_QMEM + 3)
                dve.wait_ge(evac_done, sec.fill(F_KVS + 2))
                t1, t2 = rot[:, :, :, 0:ROT], rot[:, :, :, ROT:2 * ROT]
                cosines, sines = (trig[:, c, :, :].unsqueeze(2).to_broadcast([P, TT, 16, ROT]) for c in range(2))
                for n, (a, b) in enumerate(((t1, cosines), (t2, sines), (t2, cosines), (t1, sines))):
                    for i in range(TT):
                        ins = nc.vector.tensor_tensor(rope_t[:, n, i], a[:, i], b[:, i], ALU.mult)
                step.link(ins)
                nc.vector.tensor_tensor(t1, rope_t[:, 0], rope_t[:, 1], ALU.subtract)
                nc.vector.tensor_tensor(t2, rope_t[:, 2], rope_t[:, 3], ALU.add).then_inc(rot_ready, 1)
                dve.wait_ge(convhi_ready, layer + 1)
                nc.vector.tensor_tensor(br_lo[0], conv_y, br_hi[0].bitcast(F32), ALU.subtract).then_inc(convlo_ready, 1)
                for c, name in enumerate(("pos_k", "pos_v")):
                    for g in range(GROUPS):
                        base = cmp_src[c][:, g, :]
                        windows = bass.AP(base.tensor, base.offset, [base.ap[0], [2, CMP_PAIRS], [CMP_STRIDE, N_CMP]])
                        ins = nc.vector.tensor_tensor(cmp_x[c][:, :, g, :], windows,
                                                      lp(name).unsqueeze(2).to_broadcast([P, CMP_PAIRS, N_CMP]), ALU.add)
                    ins.then_inc(cmpx_ready, 1)
                for c in range(2):
                    dve.wait_ge(cmphi_ready, layer * 2 + c + 1)
                    nc.vector.tensor_tensor(cmp_lo[c], cmp_x[c].rearrange("p m g n -> p m (g n)"), cmp_hi[c].bitcast(F32),
                                            ALU.subtract).then_inc(cmplo_ready, 1)
                with dve.Fori(0, 4) as trip:
                    for w in range(3):
                        split_low(sec, L_MERGE + w + 2, trip)
                for w in range(4):
                    split_low(sec, L_CMPK + w + 2)
                attention(sec)
                partial = []
                gate = merge.rearrange("p (b c t) -> p b c t", b=3, c=KD)
                for w in range(6):
                    split_low(sec, L_BR + w + 2)
                    b, half = w // 2, w % 2
                    dve.wait_ge(unit_used, sec.unit(L_BR + w + 1))
                    for k in range(2):
                        c = slice(4 * half + 2 * k, 4 * half + 2 * k + 2)
                        bank = work[:, 2 * (w % 2) + k, :].rearrange("p (c t) -> p c t", c=2)
                        if b == 0:
                            nc.vector.tensor_tensor(merged[:, c, :], bank, gate[:, b, c, :], ALU.mult).then_inc(br_read, 1)
                            continue
                        t = br_t[:, k, :].rearrange("p (c t) -> p c t", c=2)
                        nc.vector.tensor_tensor(t, bank, gate[:, b, c, :], ALU.mult).then_inc(br_read, 1)
                        dve.wait_ge(br_read, layer * 12 + (2 * w + k + 1))
                        if b == 2:
                            step.after(partial[2 * half + k])
                        ins = nc.vector.tensor_tensor(merged[:, c, :], merged[:, c, :], t, ALU.add)
                        if b == 1:
                            partial.append(step.mark(ins))
                        elif k == 1:
                            ins.then_inc(merged_ready, 1)
                for c in range(2):
                    dve.wait_ge(mhi_ready, layer * 2 + c + 1)
                    nc.vector.tensor_tensor(merged_lo[:, 4 * c:4 * c + 4, :], merged[:, 4 * c:4 * c + 4, :],
                                            merged_hi[:, 4 * c:4 * c + 4, :].bitcast(F32), ALU.subtract).then_inc(mlo_ready, 1)
                for w in range(4):
                    split_low(sec, L_OUT + w + 2)
                post_residual(sec, 1, 4, 1.0, lp("post_mix"))
                norm(sec, 3, 5, x, lp("g_ffn2"))
                ffn(sec, L_FFN2, 1, False)
                post_residual(sec, 2, 6, 0.5, lp("post_ffn2"))
                step.leave()

        @block.tensor
        def _(pe):
            def product(dst, a_hi, a_lo, b_hi, b_lo, start, stop):
                nc.tensor.matmul(dst, a_hi, b_hi, start=start, stop=False)
                nc.tensor.matmul(dst, a_hi, b_lo, start=False, stop=False)
                return nc.tensor.matmul(dst, a_lo, b_hi, start=False, stop=stop)

            def parts_ready(sec, n, trip=0):
                pe.wait_ge(lo_ready, sec.unit(n + 1) + trip * RING)

            def rows_half(n, half, i, dst, a_hi, a_lo):
                s = n % RING
                for q in range(4):
                    kt = 4 * half + q
                    last = product(dst, a_hi[:, kt, P * i:P * i + P], a_lo[:, kt, P * i:P * i + P],
                                   hi[:, s, 512 * q:512 * q + 512], lo[:, s, 512 * q:512 * q + 512],
                                   kt == 0, kt == KD - 1)
                return last

            def bank_free(sec, f, trip=0):
                wait(pe, evac_done, sec.fill(f - 2) + trip * 3)

            def rows(sec, n, f):
                for i in range(TT):
                    bank_free(sec, f + i)
                for half in range(2):
                    parts_ready(sec, n + half)
                    for i in range(TT):
                        last = rows_half(n + half, half, i, work[:, (f + i) % 3, :], xT_hi, xT_lo)
                    last.then_inc(unit_used, 1)

            def channels(sec, n, f, trip=0):
                s = n % RING
                bank_free(sec, f, trip)
                parts_ready(sec, n, trip)
                for c in range(2):
                    for kt in range(KD):
                        w = slice(P * (KD * c + kt), P * (KD * c + kt) + P)
                        last = product(work[:, f % 3, T * c:T * c + T], hi[:, s, w], lo[:, s, w],
                                       xT_hi[:, kt, :], xT_lo[:, kt, :], kt == 0, kt == KD - 1)
                last.then_inc(unit_used, 1)

            def transposes(sec, f, src):
                bank_free(sec, f)
                for c in range(2):
                    for i in range(TT):
                        last = nc.tensor.transpose(work[:, f % 3, T * c + P * i:T * c + P * i + P], src(c, i), ident)
                last.then_inc(small_ready, 1)

            def norm(sec, k):
                pe.wait_ge(xs_ready, sec.at(8, 8, 2 * k + 2))
                for kt in range(KD):
                    for i in range(TT):
                        at = T * (kt % 2) + P * i
                        last = nc.tensor.transpose(acc[:, kt // 2, at:at + P], xs[:, i, P * kt:P * kt + P], ident)
                    if kt % 2:
                        last.then_inc(xT_ready, 1)

            def operand_ready(sec, k):
                pe.wait_ge(xlo_ready, sec.at(32, 32, 8 * k + 8))

            def ffn(sec, u0, k, before):
                c0 = sec.at(2 * CHUNKS, 2 * CHUNKS, k * CHUNKS)
                pe.wait_ge(evac_done, sec.fill(before))

                def chunk_in(n, j, trip, first=False):
                    for half in range(2):
                        parts_ready(sec, n + half, trip)
                        for i in range(TT):
                            if half == 0 and not first:
                                pe.wait_ge(h_ready, (c0 + j) * 2 + (i - 1))
                            last = rows_half(n + half, half, i, work[:, i, :], xT_hi, xT_lo)
                            if half == 1 and i == 0:
                                last.then_inc(ab_ready, 1)
                        last.then_inc(unit_used, 1)

                def chunk_out(n, j, trip, first=False, final=False):
                    s = n % RING
                    pe.wait_ge(hTlo_ready, c0 + j + 1)
                    parts_ready(sec, n, trip)
                    for i in range(TT):
                        for f in range(2):
                            for c in range(2):
                                w = slice(D * f + 512 * c, D * f + 512 * c + 512)
                                last = product(acc[:, 2 * i + c, :], hT_hi[:, f, P * i:P * i + P], hT_lo[:, f, P * i:P * i + P],
                                               hi[:, s, w], lo[:, s, w], first and f == 0, final and f == 1)
                    last.then_inc(unit_used, 1)

                def turn(j):
                    pe.wait_ge(h_ready, (c0 + j) * 2 + 2)
                    for f in range(2):
                        for i in range(TT):
                            last = nc.tensor.transpose(work[:, 2, T * f + P * i:T * f + P * i + P], h_sb[:, i, P * f:P * f + P], ident)
                    last.then_inc(hT_ready, 1)

                chunk_in(u0, 0, 0, first=True)
                turn(0)
                chunk_in(u0 + 2, 1, 0)
                chunk_out(u0 + 4, 0, 0, first=True)
                turn(1)
                with pe.Fori(2, CHUNKS - 1) as j:
                    chunk_in(u0 - 1, j, j)
                    chunk_out(u0 + 1, j - 1, j)
                    turn(j)
                j = CHUNKS - 1
                chunk_in(u0 + 3 * j - 1, j, 0)
                chunk_out(u0 + 3 * j + 1, j - 1, 0)
                turn(j)
                chunk_out(u0 + FFN_UNITS - 1, j, 0, final=True)

            def output(sec, n, a_hi, a_lo):
                for c in range(2):
                    for half in range(2):
                        parts_ready(sec, n + 2 * c + half)
                        for i in range(TT):
                            last = rows_half(n + 2 * c + half, half, i, acc[:, 2 * i + c, :], a_hi, a_lo)
                        last.then_inc(unit_used, 1)

            def attention(sec):
                jobs = jobs_of(sec)

                def scores(n, job):
                    if n >= 2:
                        pe.wait_ge(scored, sec.at(2 * JOBS[0], 2 * JOBS[1], 2 * n - 2))
                    for i in range(TT):
                        w = job.width(i)
                        last = nc.tensor.matmul(acc[:, n % 2, T * i:T * i + w], job.q(i), job.k(w), start=True, stop=True)
                    last.then_inc(qk_ready, 1)

                def turn(n, job):
                    pe.wait_ge(p_ready, sec.at(2 * JOBS[0], 2 * JOBS[1], 2 * n + 2))
                    if n >= 1:
                        pe.wait_ge(pT_copied, sec.at(*JOBS, n))
                    for kt, i, at in job.blocks():
                        r = job.rows(kt)
                        last = nc.tensor.transpose(acc[0:r, 2, at:at + P], prob[:, n % 2, i, P * kt:P * kt + r], ident)
                    last.then_inc(pT_ready, 1)

                def values(n, job):
                    pe.wait_ge(pT_copied, sec.at(*JOBS, n + 1))
                    if job.first and job.tile >= 2:
                        pe.wait_ge(tile_lo, sec.at(*TILES, job.tile - 1))
                    at = 0
                    for kt in range(job.key_tiles):
                        r, span = job.rows(kt), job.span(kt)
                        y = tile_bank(job.tile)[job.row:job.row + job.m, span:T]
                        last = nc.tensor.matmul(y, job.v(kt), probT[0:r, n % 2, at:at + T - span],
                                                start=job.first and kt == 0, stop=job.last and kt == job.key_tiles - 1)
                        at += T - span
                    if job.tile_done:
                        last.then_inc(tile_ready, 1)

                scores(0, jobs[0])
                for n, job in enumerate(jobs):
                    if n + 1 < len(jobs):
                        scores(n + 1, jobs[n + 1])
                    turn(n, job)
                    values(n, job)
                pe.wait_ge(tile_lo, sec.at(*TILES, jobs[-1].tile + 1))

            sec = Section()
            pe.wait_ge(const_in_sem, 48)
            pe.wait_ge(lo_ready, 1)
            pe.sem_inc(unit_used, 1)
            norm(sec, 0)
            operand_ready(sec, 0)
            rows(sec, B1_MEM, F1_MEM)
            norm(sec, 1)
            operand_ready(sec, 1)
            ffn(sec, B1_FFN1, 0, F1_QK)
            norm(sec, 2)
            operand_ready(sec, 2)
            rows(sec, B1_QK, F1_QK)
            rows(sec, B1_VC, F1_VC)
            for w in range(2):
                channels(sec, B1_LRU_X + w, F1_LRU_X + w)
            for w in range(2):
                channels(sec, B1_LRU_G + w, F1_LRU_G + w)
            pe.wait_ge(heads_ready, 1)
            for kind in range(4):
                transposes(sec, F1_HEADS + kind, lambda c, i: heads1[:, i, 4 * kind + 2 * c:4 * kind + 2 * c + 2, :].rearrange("p h d -> p (h d)"))
            pe.wait_ge(xb_ready, 2)
            for w in range(4):
                bank_free(sec, F1_GATE + w)
                for c in range(2):
                    ct = 2 * (w % 2) + c
                    weights = b1p("a_w" if w < 2 else "x_w")[:, P * ct:P * ct + P]
                    last = nc.tensor.matmul(work[:, (F1_GATE + w) % 3, T * c:T * c + T], weights, lru_xb[:, ct, :],
                                            start=True, stop=True)
                last.then_inc(small_ready, 1)
            pe.wait_ge(evac_done, F1_HEADS + 4)
            attention(sec)
            pe.wait_ge(lrulo_ready, 1)
            output(sec, B1_OUT, mix_hi, mix_lo)
            norm(sec, 3)
            operand_ready(sec, 3)
            ffn(sec, B1_FFN2, 1, F1_FILLS)

            with pe.Fori(0, LAYERS) as layer:
                sec = Section(layer)
                pe.wait_ge(unit_used, sec.unit(0))
                pe.wait_ge(lo_ready, sec.unit(2))
                pe.sem_inc(unit_used, 2)
                norm(sec, 0)
                operand_ready(sec, 0)
                for w in range(2):
                    channels(sec, L_MEM + w, F_MEMK + w)
                rows(sec, L_MEM + 2, F_MEMV)
                norm(sec, 1)
                operand_ready(sec, 1)
                ffn(sec, L_FFN1, 0, F_CONV)
                norm(sec, 2)
                with pe.Fori(0, 2) as trip:
                    operand_ready(sec, 2)
                    for w in range(3):
                        channels(sec, L_CONV + w, F_CONV + w, trip)
                channels(sec, L_KV, F_KV)
                pe.wait_ge(gwlo_ready, layer + 1)
                bank_free(sec, F_GATE)
                for i in range(TT):
                    for kt in range(KD):
                        last = product(work[:, F_GATE % 3, GATES * i:GATES * i + GATES], xT_hi[:, kt, P * i:P * i + P],
                                       xT_lo[:, kt, P * i:P * i + P], gw_hi[:, kt, :], gw_lo[:, kt, :], kt == 0, kt == KD - 1)
                last.then_inc(small_ready, 1)
                rows(sec, L_Q, F_Q)
                rows(sec, L_KVS, F_KVS)
                for w in range(2):
                    channels(sec, L_QMEM + w, F_QMEM + w)
                with pe.Fori(0, 4) as trip:
                    for w in range(3):
                        channels(sec, L_MERGE + w, F_MERGE + w, trip)
                pe.wait_ge(rot_ready, layer + 1)
                for w in range(4):
                    transposes(sec, F_ROT + w, lambda c, i: rot[:, i, 4 * w + 2 * c:4 * w + 2 * c + 2, :].rearrange("p h d -> p (h d)"))
                for w in range(2):
                    transposes(sec, F_PLAIN + w, lambda c, i: q_sb[:, i, P * (2 * w + c):P * (2 * w + c) + P])
                for c, (units, fills) in enumerate(((L_CMPK, F_HIDK), (L_CMPV, F_HIDV))):
                    pe.wait_ge(cmplo_ready, layer * 2 + c + 1)
                    for t in range(2):
                        n = units + t
                        bank_free(sec, fills + t)
                        parts_ready(sec, n)
                        for m in range(CMP_PAIRS):
                            w = slice(P * m, P * m + P)
                            last = product(work[:, (fills + t) % 3, 0:GROUPS * N_CMP], hi[:, n % RING, w], lo[:, n % RING, w],
                                           cmp_hi[c][:, m, :], cmp_lo[c][:, m, :], m == 0, m == CMP_PAIRS - 1)
                        last.then_inc(unit_used, 1)
                    pe.wait_ge(evac_done, sec.fill(fills + 2))
                    if c == 0:
                        w2 = lp("k_w2").rearrange("p (t d) -> p t d", t=2)
                        for t in range(2):
                            last = nc.tensor.matmul(work[:, F_KC % 3, 0:GROUPS * N_CMP], w2[:, t, :], hid[0][:, t, :],
                                                    start=t == 0, stop=t == 1)
                    else:
                        w2 = lp("v_w2").rearrange("p (t d) -> p t d", t=2)
                        for g in range(GROUPS):
                            for t in range(2):
                                last = nc.tensor.matmul(work[0:N_CMP, F_VC % 3, HD * g:HD * g + HD],
                                                        hid[1][:, t, N_CMP * g:N_CMP * g + N_CMP], w2[:, t, :],
                                                        start=t == 0, stop=t == 1)
                    last.then_inc(small_ready, 1)
                pe.wait_ge(evac_done, sec.fill(F_FILLS))
                attention(sec)
                pe.wait_ge(convlo_ready, layer + 1)
                for w in range(6):
                    b, n = w // 2, L_BR + w
                    if w >= 2:
                        pe.wait_ge(br_read, layer * 12 + (2 * w - 2))
                    parts_ready(sec, n)
                    for c in range(4):
                        for kt in range(4):
                            at = slice(P * (4 * c + kt), P * (4 * c + kt) + P)
                            last = product(work[:, 2 * (w % 2) + c // 2, T * (c % 2):T * (c % 2) + T], hi[:, n % RING, at],
                                           lo[:, n % RING, at], br_hi[b][:, kt, :], br_lo[b][:, kt, :], kt == 0, kt == 3)
                    last.then_inc(unit_used, 1)
                pe.wait_ge(mlo_ready, layer * 2 + 2)
                output(sec, L_OUT, merged_hi, merged_lo)
                norm(sec, 3)
                operand_ready(sec, 3)
                ffn(sec, L_FFN2, 1, F_FILLS)


DVE_STEPS = (56, 63)

PI = float(np.float32(np.nextafter(np.float32(np.pi), np.float32(0))))
TURN = float(2 * np.pi)
ROUND = 1.5 * 2.0 ** 23


def turn_parts():
    rest, parts = TURN, []
    for bits in (5, 14, 23):
        part = np.floor(rest * 2.0 ** bits) / 2.0 ** bits
        parts.append(float(part))
        rest -= part
    return parts + [float(np.float32(rest))]


TURN_PARTS = turn_parts()


def rows_units(w):
    t = w.reshape(KD, P, w.shape[1]).transpose(1, 0, 2)
    return [t[:, 0:4].reshape(P, UNIT), t[:, 4:8].reshape(P, UNIT)]


def channel_units(w):
    k, n = w.shape
    t = w.reshape(k // P, P, n // P, P).transpose(1, 2, 0, 3).reshape(P, -1)
    return [t[:, a:a + UNIT] for a in range(0, t.shape[1], UNIT)]


def ffn_units(w_in, w_out):
    into, outof = [], []
    for j in range(CHUNKS):
        a = w_in[:, CHUNK * j:CHUNK * (j + 1)]
        b = w_in[:, D_FF + CHUNK * j:D_FF + CHUNK * (j + 1)]
        into.append(rows_units(np.concatenate([a, b], axis=1)))
        outof.append(w_out[CHUNK * j:CHUNK * (j + 1)].reshape(2, P, D).transpose(1, 0, 2).reshape(P, UNIT))
    order = list(into[0])
    for j in range(1, CHUNKS):
        order += [*into[j], outof[j - 1]]
    return order + [outof[-1]]


def by_partition(v):
    return v.reshape(-1, P).T


def pack(table, total, fields):
    packed = np.zeros((P, total), np.float32)
    for name, value in fields.items():
        at, n = table[name]
        packed[:, at:at + n] = value.reshape(P, n)
    return packed


def twice(v):
    return np.concatenate([v, v]).reshape(P, 1)


def block_diagonal(w):
    t = np.zeros((P, LRU_TILES, P), np.float32)
    for n in range(2 * LRU_TILES):
        at = 64 * (n % 2)
        t[at:at + 64, n // 2, at:at + 64] = w[n]
    return t


def constants():
    q = np.arange(P)
    made = np.zeros((P, CONST_N), np.float32)

    def put(name, value):
        at, n = CONST[name]
        made[:, at:at + n] = np.asarray(value, np.float32).reshape(P, n)

    distance = np.concatenate([q[:, None] - np.arange(P)[None], P + q[:, None] - np.arange(T)[None]], axis=1)
    put("ident", np.eye(P))
    put("causal", np.where(distance >= 0, 0.0, NEG))
    token = q[:, None] + P * np.arange(TT)[None]
    ends = np.arange(16) * CMP_STRIDE + CMP_BLOCK - 1
    put("cmp_mask", np.where(ends[None, None] <= token[:, :, None], 0.0, NEG))
    put("cmp_valid", token >= CMP_BLOCK - 1)
    put("inv_freq", np.broadcast_to(np.float32(ROPE_THETA) ** (-np.arange(0, 2 * ROT, 2, dtype=np.float32) / np.float32(2 * ROT)), (P, ROT)))
    slopes = 2.0 ** (-8.0 * np.arange(1, 5) / 4)
    alibi = np.stack([np.where(distance >= 0, -s * HD ** 0.5 * distance, NEG) for s in slopes], axis=1)
    return made, alibi.astype(np.float32).reshape(P, ALIBI_N)


def lay_out(a):
    s = []
    s.append(pack(B1P, UNIT, {
        "a_w": block_diagonal(a["lru_a_w"][0]), "x_w": block_diagonal(a["lru_x_w"][0]),
        "conv_w": a["lru_conv_w"][0].reshape(CONV_W, LRU_TILES, P).transpose(2, 1, 0),
        "conv_b": by_partition(a["lru_conv_b"][0]), "a_b": by_partition(a["lru_a_b"][0]),
        "x_b": by_partition(a["lru_x_b"][0]), "lam": by_partition(a["lru_lambda"][0]),
        "g_mem": by_partition(a["mem_norm"][0]), "g_ffn1": by_partition(a["ffn1_norm"][0]),
        "g_mix": by_partition(a["mix_norm"][0]), "g_ffn2": by_partition(a["ffn2_norm"][0]),
        "g_heads": np.concatenate([twice(a[n][0]) for n in ("moba_q_norm", "moba_k_norm", "mem_q_norm", "mem_k_norm")], axis=1)}))
    w = a["w_in"][0]
    s += rows_units(a["mem_w_kv"][0])
    s += ffn_units(a["ffn1_w_in"][0], a["ffn1_w_out"][0])
    s += rows_units(w[:, 1024:1536])
    s += rows_units(w[:, 1536:2048])
    s += channel_units(w[:, 0:512])
    s += channel_units(w[:, 512:1024])
    s += rows_units(a["w_out"][0][:, 0:512]) + rows_units(a["w_out"][0][:, 512:1024])
    s += ffn_units(a["ffn2_w_in"][0], a["ffn2_w_out"][0])
    for l in range(LAYERS):
        b = {name[:-2]: a[name][l] for name in a if name.endswith("_2") and name not in ("mem_2", "positions_2")}
        w = b["w_mix_in"]
        k_w2 = b["cmp_k_w2"].reshape(2, P, HD).transpose(1, 0, 2)
        p = pack(LP, 2 * UNIT, {
            **{f"post_{n}": np.broadcast_to(b[f"{n}_norm_post"], (P, D)) for n in ("ffn1", "mix", "ffn2")},
            "gate_w": w[:, 2816:2840].reshape(KD, P, GATES).transpose(1, 0, 2),
            "k_w2": np.concatenate([k_w2, k_w2], axis=2),
            "v_w2": b["cmp_v_w2"].reshape(2, P, HD).transpose(1, 0, 2),
            "k_b1": by_partition(b["cmp_k_b1"]), "v_b1": by_partition(b["cmp_v_b1"]),
            "pos_k": by_partition(b["cmp_pos_k"].reshape(-1)), "pos_v": by_partition(b["cmp_pos_v"].reshape(-1)),
            "conv_w": b["conv_w"].reshape(CONV2_W, 4, P).transpose(2, 1, 0),
            "g_mem": by_partition(b["mem_norm"]), "g_ffn1": by_partition(b["ffn1_norm_pre"]),
            "g_mix": by_partition(b["mix_norm_pre"]), "g_ffn2": by_partition(b["ffn2_norm_pre"])})
        s += [p[:, 0:UNIT], p[:, UNIT:]]
        s += channel_units(b["w_mem_kv"][:, 0:512]) + rows_units(b["w_mem_kv"][:, 512:1024])
        s += ffn_units(b["ffn1_w_in"], b["ffn1_w_out"])
        s += channel_units(w[:, 0:1536]) + channel_units(w[:, 2048:2304])
        s += rows_units(w[:, 1536:2048]) + rows_units(w[:, 2304:2816])
        s += channel_units(w[:, 2840:3352]) + channel_units(w[:, 3352:6424])
        s += channel_units(b["cmp_k_w1"]) + channel_units(b["cmp_v_w1"])
        for name in ("conv", "nsa", "mem"):
            s += channel_units(b[f"w_branch_{name}"])
        s += rows_units(b["w_mix_out"][:, 0:512]) + rows_units(b["w_mix_out"][:, 512:1024])
        s += ffn_units(b["ffn2_w_in"], b["ffn2_w_out"])
    assert len(s) == UNITS
    const, alibi = constants()
    return {"stream": np.stack(s), "x": a["x"][0], "mem1": a["mem"][0], "mem2": a["mem_2"][0],
            "positions": np.ascontiguousarray(a["positions_2"][0].reshape(TT, P).T), "const": const, "alibi": alibi}


def kernel(**inputs):
    import concourse.bacc as bacc
    from concourse.bass_utils import run_bass_kernel_spmd as run

    arrays = lay_out({name: np.asarray(value) for name, value in inputs.items()})
    nc = bacc.Bacc("TRN2", target_bir_lowering=False, num_devices=1)
    ins = [nc.dram_tensor(name, a.shape, mybir.dt.from_np(a.dtype), kind="ExternalInput").ap() for name, a in arrays.items()]
    out = nc.dram_tensor("out", (T, D), F32, kind="ExternalOutput").ap()
    build(nc, *ins, out)
    result = run(nc, [arrays], core_ids=[0])
    return result.results[0]["out"].reshape(1, T, D)
```

```python
from contextlib import ExitStack

import numpy as np

import concourse.bass as bass
from concourse import mybir

F32 = mybir.dt.float32
F32R = mybir.dt.float32r
I32 = mybir.dt.int32
ALU = mybir.AluOpType
ACT = mybir.ActivationFunctionType
AX_X = mybir.AxisListType.X

P = 128
T = 256
TT = T // P
D = 1024
KD = D // P
D_FF = 2816
LAYERS = 2
EPS = 1e-6
NEG = -1e30
BIG = 3e38
HD = 64
MEM_HD = 128
LRU_TILES = 4
LRU_C = 8.0
CONV_W = 4
CONV2_W = 3
CMP_BLOCK, CMP_STRIDE = 32, 16
N_CMP = T // CMP_STRIDE - 1
CMP_PAIRS = CMP_BLOCK // 2
GROUPS = 2
NSA_HEADS = 8
GATES = 3 * NSA_HEADS
ROT = 8
ROPE_THETA = 500000.0

UNIT = 2048
RING = 3
CHUNK = 256
CHUNKS = D_FF // CHUNK
FFN_UNITS = 3 * CHUNKS
B1_PARAM, B1_FFN1 = 0, 1
B1_MEM = B1_FFN1 + FFN_UNITS
B1_LRU_X, B1_QK, B1_VC, B1_LRU_G, B1_OUT = B1_MEM + 2, B1_MEM + 4, B1_MEM + 6, B1_MEM + 8, B1_MEM + 10
B1_FFN2 = B1_OUT + 4
B1_UNITS = B1_FFN2 + FFN_UNITS
L_PARAM, L_GAIN, L_FFN1 = 0, 1, 2
L_MEM = L_FFN1 + FFN_UNITS
L_CONV = L_MEM + 4
L_KV, L_Q, L_KVS, L_QMEM, L_STEPS = L_CONV + 6, L_CONV + 7, L_CONV + 9, L_CONV + 11, L_CONV + 13
L_MERGE = [L_STEPS + k for k in (0, 3, 5, 7)] + [L_STEPS + k for k in range(8, 16)]
L_CMPK = (L_STEPS + 1, L_STEPS + 2)
L_CMPV = (L_STEPS + 4, L_STEPS + 6)
L_BR = L_STEPS + 16
L_OUT = L_BR + 6
L_FFN2 = L_OUT + 4
L_UNITS = L_FFN2 + FFN_UNITS
assert B1_UNITS % RING == 0 and L_UNITS % RING == 0
UNITS = B1_UNITS + LAYERS * L_UNITS
WEIGHTS = UNITS - 1 - 2 * LAYERS

F1_MEM, F1_LRU_X, F1_QK, F1_VC, F1_GATE, F1_LRU_G0, F1_HEADS, F1_LRU_G1, F1_FILLS = 0, 2, 4, 6, 8, 12, 13, 17, 18
F_MEMK, F_MEMV, F_CONV, F_KV, F_GATE, F_Q, F_KVS, F_PLAIN, F_QMEM = 0, 2, 4, 10, 11, 12, 14, 16, 18
F_MERGE = [20, 24, 28, 31] + list(range(34, 42))
F_HIDK, F_HIDV, F_ROT, F_KC, F_VC, F_FILLS = (21, 22), (26, 30), (23, 25, 27, 29), 32, 33, 42
assert F1_FILLS % 3 == 0 and F_FILLS % 3 == 0
S1_GATE, S1_HEADS, S1_SMALL = 0, 4, 8
S_GATE, S_PLAIN, S_ROT, S_KC, S_VC, S_SMALL = 0, 1, 3, 7, 8, 9
STEP_WORK = {0: (("merge", 0), ("cmpk", 0)),
             1: (("cmpk", 1), ("rot", 0), ("merge", 1), ("rot", 1)),
             2: (("cmpv", 0), ("rot", 2), ("merge", 2), ("rot", 3)),
             3: (("cmpv", 1), ("merge", 3)),
             4: (("kc", 0), ("vc", 0))}
FIRST_NSA = 4
CONV_STEP = 6
CONV_FREE = 8


def merge_half(n):
    h, b = divmod(n - FIRST_NSA, 3)
    return (4 + h, b) if n >= FIRST_NSA and b < 2 else None


BRANCHES = (0, 2, 1)

B1P, LP = {}, {}


def columns(table, widths):
    at = 0
    for name, width in widths:
        table[name] = (at, width)
        at += width
    return at


B1P_N = columns(B1P, [("a_w", 512), ("x_w", 512), ("conv_w", 16), ("conv_b", 4), ("a_b", 4), ("x_b", 4),
                      ("lam", 4), ("g_mem", 8), ("g_heads", 4)])
LP_N = columns(LP, [("gate_w", KD * GATES), ("k_w2", 256), ("v_w2", 128), ("k_b1", 2), ("v_b1", 2),
                    ("pos_k", 16), ("pos_v", 16), ("conv_w", 12), ("g_mem", 8)])
CONST = {}
CONST_N = columns(CONST, [("ident", P), ("causal", 384), ("zero", 1), ("cmp_mask", TT * 16),
                          ("cmp_valid", TT), ("inv_freq", ROT)])
ALIBI_N = 4 * 384


class Section:

    def __init__(self, layer=None):
        self.layer = layer

    def at(self, first, per_layer, k):
        return k if self.layer is None else self.layer * per_layer + (first + k)

    def unit(self, n):
        return self.at(B1_UNITS, L_UNITS, n)

    def landed(self, n):
        return self.at(16 * B1_UNITS // RING, 16 * L_UNITS // RING, 16 * (n // RING + 1))

    def small(self, f):
        return self.at(S1_SMALL, S_SMALL, f)

    def fill(self, f):
        return self.at(F1_FILLS, F_FILLS, f)


def wait(eng, sem, value):
    if not isinstance(value, int) or value > 0:
        eng.wait_ge(sem, value)


class Steps:

    def __init__(self, eng, sem, first, per_layer):
        self.eng, self.sem, self.totals = eng, sem, (first, per_layer)

    def enter(self, sec):
        self.sec, self.n = sec, 0

    def mark(self, ins):
        ins.then_inc(self.sem, 1)
        self.n += 1
        return self.sec.at(*self.totals, self.n)

    def after(self, value):
        self.eng.wait_ge(self.sem, value)

    def link(self, ins):
        self.after(self.mark(ins))

    def leave(self):
        want = self.totals[0 if self.sec.layer is None else 1]
        assert self.n == want, (self.n, self.totals)


class Job:

    def __init__(self, q, k, v, bias, scale, keys, causal, m, row, tile, first, last, factor=None):
        self.q, self.k, self.v, self.bias, self.scale = q, k, v, bias, scale
        self.keys, self.causal, self.m, self.row = keys, causal, m, row
        self.tile, self.first, self.last, self.factor = tile, first, last, factor
        self.key_tiles = -(-keys // P)
        self.tile_done = last and (m == P or row > 0)

    def width(self, i):
        return min(self.keys, P * (i + 1)) if self.causal else self.keys

    def rows(self, kt):
        return min(P, self.keys - P * kt)

    def span(self, kt):
        return P * kt if self.causal else 0

    def blocks(self):
        return [(kt, i, T * kt + P * i - self.span(kt))
                for kt in range(self.key_tiles) for i in range(TT) if P * i >= self.span(kt)]

    def pt_width(self):
        return T * self.key_tiles - sum(self.span(kt) for kt in range(self.key_tiles))


def build(nc, stream, b1_params, l_params, pre_in, post_in, x_in, mem1_in, mem2_in, pos_in, const_in, alibi_in, out):
    with ExitStack() as ctx:
        plan = {"at": -(-nc.sbuf_base // 64) * 64}

        def room(size):
            start = plan["at"]
            plan["at"] += -(-size // 32) * 32
            assert plan["at"] <= nc.sbuf_usable_end, plan["at"]
            return start

        def place(name, shape, start, dtype=F32):
            return nc.alloc_sbuf_tensor_at(name, shape, dtype, offset=start).ap()

        def new(name, shape, dtype=F32):
            return place(name, shape, room(4 * int(np.prod(shape[1:]))), dtype)

        raw = new("raw", [P, RING, UNIT])
        hi = new("hi", [P, RING, UNIT], F32R)
        lo = new("lo", [P, RING, UNIT], F32R)
        x = new("x", [P, TT, D])
        r_scaled = room(8192)
        xs = place("xs", [P, TT, D], r_scaled)
        heads1 = place("heads1", [P, TT, 16, HD], r_scaled)
        rot = place("rot", [P, TT, 16, HD], r_scaled)
        xT_hi = new("xT_hi", [P, KD, T], F32R)
        xT_lo = new("xT_lo", [P, KD, T], F32R)
        params = new("params", [P, max(B1P_N, LP_N)])
        pre = new("pre", [P, D])
        post = new("post", [P, D])
        r_memk = room(4096)
        memkT = place("memkT", [P, 4, T], r_memk)
        lru_y = place("lru_y", [P, LRU_TILES, T], r_memk)
        memv = new("memv", [P, TT, 512])
        r_big = room(24576)
        mem_in = place("mem_in", [P, TT, D], r_big)
        memT_hi = place("memT_hi", [P, KD, T], r_big + 8192, F32R)
        memT_lo = place("memT_lo", [P, KD, T], r_big + 16384, F32R)
        lru_in = place("lru_in", [P, LRU_TILES, T + CONV_W - 1], r_big)
        lru_xb = place("lru_xb", [P, LRU_TILES, T], r_big + 4160)
        lru_r = place("lru_r", [P, LRU_TILES, T], r_big + 4160 + 4096)
        lru_i = place("lru_i", [P, LRU_TILES, T], r_big + 4160 + 2 * 4096)
        lru_m = place("lru_m", [P, LRU_TILES, T], r_big)
        lru_a = place("lru_a", [P, LRU_TILES, T], r_big + 4160 + 3 * 4096)
        conv_in = place("conv_in", [P, 3 * 4 * T], r_big)
        conv_v = place("conv_v", [P, 4, T + CONV2_W - 1], r_big + 12288)
        conv_y = place("conv_y", [P, 4, T], r_big + 12288 + 4160)
        merge = place("merge", [P, 3 * KD * T], r_big)
        merged_hi = place("merged_hi", [P, KD, T], r_big, F32R)
        merged_lo = place("merged_lo", [P, KD, T], r_big + 8192, F32R)
        r_mix = room(24576)
        mix_hi = place("mix_hi", [P, KD, T], r_mix, F32R)
        mix_lo = place("mix_lo", [P, KD, T], r_mix + 8192, F32R)
        alibi = place("alibi", [P, 4, 384], r_mix + 16384)
        br_hi = [place(f"br_hi{b}", [P, 4, T], r_mix + 8192 * (2 - b), F32R) for b in range(3)]
        br_lo = [place(f"br_lo{b}", [P, 4, T], r_mix + 8192 * (2 - b) + 4096, F32R) for b in range(3)]
        cmp_src = [place(f"cmp_src{c}", [P, GROUPS, T], r_mix + 8192 + 2048 * c) for c in range(2)]
        n_cmp = CMP_PAIRS * GROUPS * N_CMP * 4
        cmp_x = [place(f"cmp_x{c}", [P, CMP_PAIRS, GROUPS, N_CMP], r_mix + 12288 + 3 * n_cmp * c)
                 for c in range(2)]
        cmp_hi = [place(f"cmp_hi{c}", [P, CMP_PAIRS, GROUPS * N_CMP], r_mix + 12288 + 3 * n_cmp * c + n_cmp,
                        F32R) for c in range(2)]
        cmp_lo = [place(f"cmp_lo{c}", [P, CMP_PAIRS, GROUPS * N_CMP],
                        r_mix + 12288 + 3 * n_cmp * c + 2 * n_cmp, F32R) for c in range(2)]
        r_qT = room(4096)
        qT = place("qT", [P, 4, T], r_qT)
        lru_g = place("lru_g", [P, LRU_TILES, T], r_qT)
        hT_hi = place("hT_hi", [P, 2, T], r_qT, F32R)
        hT_lo = place("hT_lo", [P, 2, T], r_qT + 2048, F32R)
        r_headT = room(8192)
        headT = place("headT", [P, 8, T], r_headT)
        squares = place("squares", [P, TT, 16, HD], r_headT)
        merged = place("merged", [P, KD, T], r_headT)
        qmemT = new("qmemT", [P, 4, T])
        v_sb = new("v_sb", [P, TT, 2, P])
        r_prob = room(4096)
        prob = place("prob", [P, 2, TT, T], r_prob)
        silu_a = place("silu_a", [P, 2 * T], r_prob)
        h_sb = place("h_sb", [P, 2 * T], r_prob + 2048)
        rope_t = place("rope_t", [P, 4, TT, 16, ROT], r_prob)
        br_t = place("br_t", [P, 2, 512], r_prob)
        r_pT = room(4096)
        probT = place("probT", [P, 2, 512], r_pT)
        q_sb = place("q_sb", [P, TT, 512], r_pT)
        hT_last = [place(f"hT_last_{part}", [P, 2, T], r_pT + 2048 * n, F32R) for n, part in enumerate(("hi", "lo"))]
        const = new("const", [P, CONST_N])
        gw_hi = place("gw_hi", [P, KD, GATES], r_pT, F32R)
        gw_lo = place("gw_lo", [P, KD, GATES], r_pT + 4 * KD * GATES, F32R)
        hid = [new(f"hid{c}", [P, 2, GROUPS * N_CMP]) for c in range(2)]
        kcT = new("kcT", [P, GROUPS * N_CMP])
        vc = new("vc", [P, GROUPS, HD])
        gates = new("gates", [P, TT, GATES])
        pos_i = new("pos_i", [P, TT], I32)
        angle = new("angle", [P, 6, TT * ROT])
        trig = new("trig", [P, 2, TT, ROT])
        sums = new("sums", [P, 32])
        var = new("var", [P, 32])
        rstd = new("rstd", [P, 32])
        ysums = new("ysums", [P, TT])
        neg_half = new("neg_half", [P, 32])
        soft = new("soft", [P, 2, 3, TT])
        lam_t = new("lam_t", [P, 7, LRU_TILES])

        def cst(name):
            at, n = CONST[name]
            return const[:, at:at + n]

        def b1p(name):
            at, n = B1P[name]
            return params[:, at:at + n]

        def lp(name):
            at, n = LP[name]
            return params[:, at:at + n]

        ident = cst("ident")
        causal = cst("causal")
        cmp_mask = cst("cmp_mask").rearrange("p (i n) -> p i n", i=TT)

        def psum(name):
            return ctx.enter_context(nc.psum_tensor(name, [P, 4, 512], F32))

        acc = psum("acc")
        work = psum("work")

        def sem(name):
            return ctx.enter_context(nc.semaphore(name))

        landed = [sem(f"landed{s}") for s in range(RING)]
        hi_ready, lo_ready, unit_used = sem("hi_ready"), sem("lo_ready"), sem("unit_used")
        const_in_sem, x_loaded, mem_loaded = sem("const_loaded"), sem("x_loaded"), sem("mem_loaded")
        half_set = sem("half_set")
        sq_ready, pow_asked, pow_ready = sem("sq_ready"), sem("pow_asked"), sem("pow_ready")
        xs_ready, xT_ready = sem("xs_ready"), sem("xT_ready")
        xhi_ready, xlo_ready = sem("xhi_ready"), sem("xlo_ready")
        pre_loaded, post_loaded = sem("pre_loaded"), sem("post_loaded")
        silu_ready, h_ready = sem("silu_ready"), sem("h_ready")
        hThi_ready, hTlo_ready = sem("hThi_ready"), sem("hTlo_ready")
        sum0_ready = sem("sum0_ready")
        ysq_ready, x_ready = sem("ysq_ready"), sem("x_ready")
        small_ready, evac_done = sem("small_ready"), sem("evac_done")
        qk_ready, scored, exp_ready, p_ready = sem("qk_ready"), sem("scored"), sem("exp_ready"), sem("p_ready")
        pT_ready, pT_copied = sem("pT_ready"), sem("pT_copied")
        tile_ready, tile_hi, tile_lo = sem("tile_ready"), sem("tile_hi"), sem("tile_lo")
        trig_asked, trig_ready = sem("trig_asked"), sem("trig_ready")
        dve_step = sem("dve_step")
        heads_ready, lam_asked, lam_exp, lam_ready = (sem("heads_ready"), sem("lam_asked"), sem("lam_exp"),
                                                      sem("lam_ready"))
        xb_ready, lru_a_ready, m2_ready, mult_ready, lruy_ready, lruhi_ready = (
            sem("xb_ready"), sem("lru_a_ready"), sem("m2_ready"), sem("mult_ready"), sem("lruy_ready"),
            sem("lruhi_ready"))
        lrulo_ready = sem("lrulo_ready")
        gwhi_ready, gwlo_ready = sem("gwhi_ready"), sem("gwlo_ready")
        conv_ready, convhi_ready, convlo_ready = sem("conv_ready"), sem("convhi_ready"), sem("convlo_ready")
        rot_ready, cmpx_ready, cmphi_ready, cmplo_ready = (sem("rot_ready"), sem("cmpx_ready"),
                                                           sem("cmphi_ready"), sem("cmplo_ready"))
        br_half, gate_ready = sem("br_half"), sem("gate_ready")
        br_read, merged_ready = sem("br_read"), sem("merged_ready")
        mhi_ready, mlo_ready = sem("mhi_ready"), sem("mlo_ready")
        stored = sem("stored")

        block = ctx.enter_context(nc.Block())

        POWS = (8, 13)
        JOBS = (8, 28)
        TILES = (4, 8)

        def jobs_of(sec):
            if sec.layer is None:
                def head(kind, h):
                    return headT[HD * (h % 2):HD * (h % 2) + HD, 2 * kind + h // 2, :]

                made = []
                for h in range(4):
                    made.append(Job(
                        q=lambda i, h=h: head(0, h)[:, P * i:P * i + P], k=lambda n, h=h: head(1, h)[:, 0:n],
                        v=lambda kt, h=h: v_sb[:, kt, h // 2, HD * (h % 2):HD * (h % 2) + HD],
                        bias=lambda i, n, h=h: alibi[:, h, P * i:P * i + n], scale=HD ** -0.5, keys=T,
                        causal=True, m=HD, row=HD * (h % 2), tile=h // 2, first=True, last=True))
                for h in range(4):
                    made.append(Job(
                        q=lambda i, h=h: head(2, h)[:, P * i:P * i + P], k=lambda n, h=h: head(3, h)[:, 0:n],
                        v=lambda kt, h=h: memv[:, kt, T + HD * h:T + HD * h + HD],
                        bias=lambda i, n: cst("zero").to_broadcast([P, n]), scale=HD ** -0.5, keys=T,
                        causal=False, m=HD, row=HD * (h % 2), tile=2 + h // 2, first=True, last=True))
                return made
            made = []
            for h in range(4):
                made.append(Job(
                    q=lambda i, h=h: qmemT[:, h, P * i:P * i + P], k=lambda n, h=h: memkT[:, h, 0:n],
                    v=lambda kt, h=h: memv[:, kt, MEM_HD * h:MEM_HD * h + MEM_HD],
                    bias=lambda i, n: cst("zero").to_broadcast([P, n]), scale=MEM_HD ** -0.5, keys=T, causal=False,
                    m=MEM_HD, row=0, tile=h, first=True, last=True))
            for h in range(NSA_HEADS):
                g, pair, row = h // (NSA_HEADS // GROUPS), h // 2, HD * (h % 2)
                rows = slice(row, row + HD)
                common = dict(scale=HD ** -0.5, m=HD, row=row, tile=4 + pair)
                for s in range(2):
                    made.append(Job(
                        q=lambda i, rows=rows, pair=pair: headT[rows, pair, P * i:P * i + P],
                        k=lambda n, rows=rows, g=g, s=s: headT[rows, 4 + 2 * s + g, 0:n],
                        v=lambda kt, g=g, s=s: v_sb[:, kt, s, HD * g:HD * g + HD],
                        bias=lambda i, n: causal[:, P * i:P * i + n], keys=T, causal=True,
                        first=s == 0, last=False,
                        factor=lambda i, h=h, s=s: gates[:, i, 3 * h + 1 + s:3 * h + 2 + s], **common))
                made.append(Job(
                    q=lambda i, rows=rows, pair=pair: qT[rows, pair, P * i:P * i + P],
                    k=lambda n, rows=rows, g=g: kcT[rows, N_CMP * g:N_CMP * g + n],
                    v=lambda kt, g=g: vc[0:N_CMP, g, :], bias=lambda i, n: cmp_mask[:, i, 0:n], keys=N_CMP,
                    causal=False, first=False, last=True,
                    factor=lambda i, h=h: gates[:, i, 3 * h:3 * h + 1], **common))
            return made

        def tile_bank(t):
            return (acc, work)[t % 2][:, 3, 0:T]

        def tile_dst(sec, t):
            if sec.layer is None:
                return mix_hi[:, 4 + t, :], mix_lo[:, 4 + t, :]
            b = 2 if t < 4 else 1
            return br_hi[b][:, t % 4, :], br_lo[b][:, t % 4, :]

        def tile_sums(i):
            return acc[:, 2 * i:2 * i + 2, :].rearrange("p b n -> p (b n)")

        def rows_bank(i, b):
            return acc[:, 2 * i + b, :].rearrange("p (k t) -> p k t", k=4)

        def rows_operand(part, i, b):
            return part[:, 4 * b:4 * b + 4, P * i:P * i + P]

        def br_bank(w, k):
            if (w, k) == (1, 1):
                return acc[:, 0, :]
            return work[:, 2 * (w % 2) + k, :]

        @block.sync
        def _(sp):
            def load(sec, n, at, trip=0, static=False):
                wait(sp, lo_ready, sec.unit(n - RING + 1) + trip * RING)
                sp.dma_start(raw[:, n % RING, :], stream[at]).then_inc(landed[n % RING], 16)

            sec = Section()
            sp.dma_start(x[:, 0, :], x_in[0:P, :]).then_inc(x_loaded, 16)
            sp.dma_start(x[:, 1, :], x_in[P:T, :]).then_inc(x_loaded, 16)
            for n in range(1, RING):
                load(sec, n, n - 1)
            sp.dma_start(params[:, 0:B1P_N], b1_params).then_inc(landed[0], 16)
            with sp.Fori(1, B1_UNITS // RING) as turn:
                for s in range(RING):
                    load(sec, s, turn * RING + (s - 1), turn)
            with sp.Fori(0, LAYERS) as layer:
                sec = Section(layer)
                first = layer * (L_UNITS - L_FFN1) + (B1_UNITS - 1 - L_FFN1)
                sp.wait_ge(lo_ready, sec.unit(L_PARAM - RING + 1))
                sp.dma_start(params[:, 0:LP_N], l_params[bass.ds(layer, 1)].rearrange("l p n -> p (l n)")).then_inc(landed[L_PARAM], 16)
                sp.wait_ge(lo_ready, sec.unit(L_GAIN - RING + 1))
                sp.dma_start(pre, pre_in[bass.ds(layer * 3 + 3, 1)].to_broadcast([P, D])).then_inc(landed[L_GAIN], 16)
                load(sec, L_FFN1, first + L_FFN1)
                with sp.Fori(1, L_UNITS // RING) as turn:
                    for s in range(RING):
                        load(sec, s, first + turn * RING + s, turn)
            for i in range(TT):
                sp.wait_ge(x_ready, 6 * (1 + LAYERS) - 1 + i)
                sp.dma_start(out[P * i:P * i + P, :], x[:, i, :]).then_inc(stored, 16)
            sp.wait_ge(stored, 32)

        @block.gpsimd
        def _(pool):
            nc.gpsimd.memset(neg_half, -0.5).then_inc(half_set, 1)
            pool.wait_ge(half_set, 1)

            def inverse_roots(sec, columns):
                for k, (c, n) in enumerate(columns):
                    pool.wait_ge(pow_asked, sec.at(*POWS, k + 1))
                    nc.gpsimd.tensor_tensor(rstd[:, c:c + n], var[:, c:c + n], neg_half[:, c:c + n], ALU.pow).then_inc(pow_ready, 1)

            x_norm, post_norm = [(0, 1), (1, 1)], [(2, 1), (3, 1)]
            inverse_roots(Section(), x_norm + [(4, TT)] + x_norm + [(0, 32)] + x_norm)
            with pool.Fori(0, LAYERS) as layer:
                inverse_roots(Section(layer), x_norm + [(4, TT)] + 2 * (post_norm + x_norm) + post_norm)

        @block.scalar
        def _(act):
            def split_high(sec, n, trip=0):
                s = n % RING
                wait(act, unit_used, sec.unit(n - RING + 1) + trip * RING)
                act.wait_ge(landed[s], sec.landed(n) + trip * 16)
                nc.scalar.activation(hi[:, s, :], raw[:, s, :], ACT.Copy).then_inc(hi_ready, 1)

            def load_pre(sec, r):
                row = r if sec.layer is None else sec.layer * 3 + (3 + r)
                act.dma_start(pre, pre_in[bass.ds(row, 1)].to_broadcast([P, D])).then_inc(pre_loaded, 16)

            def load_post(sec, r):
                act.dma_start(post, post_in[bass.ds(sec.layer * 3 + r, 1)].to_broadcast([P, D])).then_inc(post_loaded, 16)

            def squares_of(sec, k, i, src):
                nc.scalar.activation(xs[:, i, :], src[:, i, :], ACT.Square, accum_out=sums[:, i:i + 1]).then_inc(sq_ready, 1)

            def x_squares(sec, k, r, i):
                wait(act, x_ready, sec.at(6, 6, 2 * r + i + 1))
                squares_of(sec, k, i, x)

            def x_high(sec, k):
                for i in range(TT):
                    for b in range(2):
                        act.wait_ge(xT_ready, sec.at(16, 16, 4 * k + 2 * i + b + 1))
                        nc.scalar.activation(rows_operand(xT_hi, i, b), rows_bank(i, b), ACT.Copy).then_inc(xhi_ready, 1)

            def mem_high(sec, r, gain):
                act.wait_ge(xT_ready, sec.at(16, 16, 4 + r + 1))
                for c in range(2):
                    kt = 2 * r + c
                    ins = nc.scalar.activation(memT_hi[:, kt, :], work[:, 2 + r % 2, T * c:T * c + T], ACT.Copy,
                                               scale=gain[:, kt:kt + 1])
                ins.then_inc(xhi_ready, 1)

            def ffn(sec, u0, k, begin=None, mem_gain=None, more=True):
                c0 = sec.at(2 * CHUNKS, 2 * CHUNKS, k * CHUNKS)

                def silu(j, n, trip=0):
                    act.wait_ge(unit_used, sec.unit(n + 1) + trip * RING)
                    wait(act, h_ready, c0 + j)
                    nc.scalar.activation(silu_a, work[:, 0, :], ACT.Silu).then_inc(silu_ready, 1)

                def high_h(j, n, trip=0):
                    act.wait_ge(h_ready, c0 + j + 1)
                    act.wait_ge(unit_used, sec.unit(n + 1) + trip * RING)
                    nc.scalar.activation(hT_hi.rearrange("p f t -> p (f t)"), h_sb, ACT.Copy).then_inc(hThi_ready, 1)

                split_high(sec, u0 + 2)
                silu(0, u0)
                split_high(sec, u0 + 3)
                if begin:
                    begin()
                with act.Fori(1, CHUNKS - 1) as j:
                    high_h(j - 1, u0 - 2, j)
                    split_high(sec, u0 + 1, j)
                    silu(j, u0 - 1, j)
                    split_high(sec, u0 + 2, j)
                    split_high(sec, u0 + 3, j)
                last = CHUNKS - 1
                high_h(last - 1, u0 - 2 + 3 * last)
                split_high(sec, u0 + 1 + 3 * last)
                silu(last, u0 - 1 + 3 * last)
                split_high(sec, u0 + 2 + 3 * last)
                if mem_gain is not None:
                    mem_high(sec, 0, mem_gain)
                    mem_high(sec, 1, mem_gain)
                act.wait_ge(h_ready, c0 + last + 1)
                nc.scalar.activation(hT_last[0].rearrange("p f t -> p (f t)"), h_sb, ACT.Copy).then_inc(hThi_ready, 1)
                if more:
                    split_high(sec, u0 + FFN_UNITS)
                if mem_gain is not None:
                    mem_high(sec, 2, mem_gain)
                    mem_high(sec, 3, mem_gain)
                if more:
                    split_high(sec, u0 + FFN_UNITS + 1)

            def post_sums(sec, r, n):
                for i in range(TT):
                    if i == 0:
                        act.wait_ge(sum0_ready, sec.at(3, 3, r + 1))
                    else:
                        act.wait_ge(unit_used, sec.unit(n + 1))
                    nc.scalar.activation(xs[:, i, :], tile_sums(i), ACT.Square, accum_out=ysums[:, i:i + 1]).then_inc(ysq_ready, 1)

            def by_unit(sec, f, n, trip=0):
                act.wait_ge(unit_used, sec.unit(n + 1) + trip * RING)
                return work[:, f % 3, :]

            def by_small(sec, f, k):
                act.wait_ge(small_ready, sec.small(k + 1))
                return work[:, f % 3, :]

            def copy_out(bank, dst, func=ACT.Copy):
                nc.scalar.activation(dst, bank, func).then_inc(evac_done, 1)

            def pair(tile, w):
                return tile[:, 2 * w:2 * w + 2, :].rearrange("p c t -> p (c t)")

            def exps(sec, n, job):
                for i in range(TT):
                    act.wait_ge(scored, sec.at(2 * JOBS[0], 2 * JOBS[1], 2 * n + i + 1))
                    p = prob[:, n % 2, i, 0:job.width(i)]
                    nc.scalar.activation(p, p, ACT.Exp, bias=soft[:, n % 2, 0, i:i + 1], scale=-1.0,
                                         accum_out=soft[:, n % 2, 1, i:i + 1]).then_inc(exp_ready, 1)

            def copy_pT(sec, n, job):
                act.wait_ge(pT_ready, sec.at(*JOBS, n + 1))
                r, w = job.rows(0), job.pt_width()
                nc.scalar.activation(probT[0:r, n % 2, 0:w], acc[0:r, 2, 0:w], ACT.Copy).then_inc(pT_copied, 1)

            def high_tile(sec, job):
                if job.tile_done:
                    act.wait_ge(tile_ready, sec.at(*TILES, job.tile + 1))
                    nc.scalar.activation(tile_dst(sec, job.tile)[0], tile_bank(job.tile), ACT.Copy).then_inc(tile_hi, 1)

            sec = Section()
            load_pre(sec, 0)
            act.dma_start(const, const_in).then_inc(const_in_sem, 16)
            act.dma_start(pos_i, pos_in).then_inc(const_in_sem, 16)
            act.dma_start(alibi.rearrange("p h n -> p (h n)"), alibi_in).then_inc(const_in_sem, 16)
            act.dma_start(mem_in, mem1_in.rearrange("(i p) d -> p i d", p=P)).then_inc(mem_loaded, 16)
            act.sem_inc(hi_ready, 1)
            for i in range(TT):
                act.wait_ge(x_loaded, 32)
                squares_of(sec, 0, i, x)
            split_high(sec, B1_FFN1)
            split_high(sec, B1_FFN1 + 1)
            x_high(sec, 0)
            load_pre(sec, 1)

            def tables():
                act.wait_ge(trig_asked, 1)
                nc.scalar.activation(trig.rearrange("p c i r -> p (c i r)"), angle[:, 4:6, :].rearrange("p c n -> p (c n)"),
                                     ACT.Sin).then_inc(trig_ready, 1)
                act.wait_ge(lam_asked, 1)
                nc.scalar.activation(lam_t[:, 1, :], lam_t[:, 0, :], ACT.Exp).then_inc(lam_exp, 1)

            def mem_squares(sec):
                act.wait_ge(mem_loaded, sec.at(16, 16, 16))
                for i in range(TT):
                    squares_of(sec, 1, i, mem_in)

            def begin():
                mem_squares(sec)
                tables()

            ffn(sec, B1_FFN1, 0, begin, b1p("g_mem"))
            split_high(sec, B1_MEM + 2)
            for i in range(TT):
                x_squares(sec, 2, 0, i)
            split_high(sec, B1_MEM + 3)
            x_high(sec, 2)
            load_pre(sec, 2)
            split_high(sec, B1_LRU_X + 2)
            for i in range(TT):
                copy_out(by_unit(sec, F1_MEM + i, B1_MEM + 1), memv[:, i, :])
            for w in range(2):
                bank = by_unit(sec, F1_LRU_X + w, B1_LRU_X + w)
                nc.scalar.activation(lru_in[:, 2 * w:2 * w + 2, CONV_W - 1:], bank.rearrange("p (c t) -> p c t", c=2),
                                     ACT.Copy).then_inc(evac_done, 1)
                split_high(sec, B1_LRU_X + w + 3)
            split_high(sec, B1_QK + 3)
            for i in range(TT):
                copy_out(by_unit(sec, F1_QK + i, B1_QK + 1), heads1[:, i, 0:8, :].rearrange("p h d -> p (h d)"))
            split_high(sec, B1_VC + 2)
            split_high(sec, B1_VC + 3)
            for i in range(TT):
                bank = by_unit(sec, F1_VC + i, B1_VC + 1)
                nc.scalar.activation(v_sb[:, i, :, :].rearrange("p s n -> p (s n)"), bank[:, 0:T], ACT.Copy)
                nc.scalar.activation(heads1[:, i, 8:12, :].rearrange("p h d -> p (h d)"), bank[:, T:2 * T],
                                     ACT.Copy).then_inc(evac_done, 1)
            for w in range(4):
                bank = by_small(sec, F1_GATE + w, S1_GATE + w)
                dst, bias = (lru_r, b1p("a_b")) if w < 2 else (lru_i, b1p("x_b"))
                for c in range(2):
                    ct = 2 * (w % 2) + c
                    ins = nc.scalar.activation(dst[:, ct, :], bank[:, T * c:T * c + T], ACT.Sigmoid, bias=bias[:, ct:ct + 1])
                ins.then_inc(evac_done, 1)
            split_high(sec, B1_LRU_G + 2)
            copy_out(by_unit(sec, F1_LRU_G0, B1_LRU_G), pair(lru_g, 0), ACT.Gelu_apprx_tanh)
            for kind in range(4):
                bank = by_small(sec, F1_HEADS + kind, S1_HEADS + kind)
                nc.scalar.activation(pair(headT, kind), bank, ACT.Copy,
                                     scale=b1p("g_heads")[:, kind:kind + 1]).then_inc(evac_done, 1)

            def lru_step(n):
                if n == 0:
                    act.wait_ge(lam_ready, 1)
                    act.wait_ge(evac_done, F1_GATE + 2)
                    for ct in range(LRU_TILES):
                        nc.scalar.activation(lru_a[:, ct, :], lru_r[:, ct, :], ACT.Exp, scale=lam_t[:, 5, ct:ct + 1])
                        ins = nc.scalar.activation(lru_m[:, ct, :], lru_r[:, ct, :], ACT.Tanh, scale=lam_t[:, 6, ct:ct + 1])
                    ins.then_inc(lru_a_ready, 1)
                elif n == 1:
                    copy_out(by_unit(sec, F1_LRU_G1, B1_LRU_G + 1), pair(lru_g, 1), ACT.Gelu_apprx_tanh)
                    split_high(sec, B1_OUT + 1)
                elif n == 2:
                    split_high(sec, B1_OUT + 2)
                    act.wait_ge(m2_ready, 1)
                    nc.scalar.activation(lru_r, lru_m, ACT.Sqrt).then_inc(mult_ready, 1)
                elif n == 5:
                    act.wait_ge(lruy_ready, 1)
                    nc.scalar.activation(mix_hi[:, 0:LRU_TILES, :], lru_y, ACT.Copy).then_inc(lruhi_ready, 1)

            jobs = jobs_of(sec)
            exps(sec, 0, jobs[0])
            for n, job in enumerate(jobs):
                if n + 1 < len(jobs):
                    exps(sec, n + 1, jobs[n + 1])
                lru_step(n)
                copy_pT(sec, n, job)
                if n:
                    high_tile(sec, jobs[n - 1])
            high_tile(sec, jobs[-1])
            for w in range(1, 4):
                split_high(sec, B1_OUT + w + 2)
            for i in range(TT):
                x_squares(sec, 3, 1, i)
            x_high(sec, 3)
            ffn(sec, B1_FFN2, 1, more=False)

            with act.Fori(0, LAYERS) as layer:
                sec = Section(layer)
                act.dma_start(mem_in, mem2_in.rearrange("(i p) d -> p i d", p=P)).then_inc(mem_loaded, 16)
                act.wait_ge(hi_ready, sec.unit(0))
                act.sem_inc(hi_ready, L_FFN1)
                split_high(sec, L_FFN1)
                split_high(sec, L_FFN1 + 1)
                for i in range(TT):
                    x_squares(sec, 0, -1, i)
                load_post(sec, 0)
                x_high(sec, 0)
                load_pre(sec, 1)
                ffn(sec, L_FFN1, 0, lambda: mem_squares(sec), lp("g_mem"))
                post_sums(sec, 0, L_MEM - 1)
                split_high(sec, L_MEM + 2)
                for i in range(TT):
                    x_squares(sec, 2, 0, i)
                load_post(sec, 1)
                split_high(sec, L_MEM + 3)
                copy_out(by_unit(sec, F_MEMK, L_MEM), pair(memkT, 0))
                nc.scalar.activation(gw_hi.rearrange("p k n -> p (k n)"), lp("gate_w"), ACT.Copy).then_inc(gwhi_ready, 1)
                split_high(sec, L_MEM + 4)
                copy_out(by_unit(sec, F_MEMK + 1, L_MEM + 1), pair(memkT, 1))
                x_high(sec, 2)
                load_pre(sec, 2)
                split_high(sec, L_MEM + 5)
                for i in range(TT):
                    copy_out(by_unit(sec, F_MEMV + i, L_MEM + 3), memv[:, i, :])
                with act.Fori(0, 2) as trip:
                    for w in range(3):
                        split_high(sec, L_CONV + w + 2, trip)
                        copy_out(by_unit(sec, F_CONV + w, L_CONV + w, trip), conv_in[:, bass.ds(trip * 1536 + 512 * w, 512)])
                split_high(sec, L_KV + 2)
                bank = by_unit(sec, F_KV, L_KV)
                for c in range(2):
                    for g in range(GROUPS):
                        part = bank[HD * g:HD * g + HD, T * c:T * c + T]
                        nc.scalar.activation(cmp_src[c][0:HD, g, :], part, ACT.Copy)
                        ins = nc.scalar.activation(cmp_src[c][HD:P, g, 0:T - 1], part[:, 1:T], ACT.Copy)
                ins.then_inc(evac_done, 1)
                bank = by_small(sec, F_GATE, S_GATE)
                nc.scalar.activation(gates.rearrange("p i n -> p (i n)"), bank[:, 0:TT * GATES], ACT.Sigmoid).then_inc(evac_done, 1)
                split_high(sec, L_Q + 2)
                split_high(sec, L_Q + 3)
                for i in range(TT):
                    bank = by_unit(sec, F_Q + i, L_Q + 1)
                    nc.scalar.activation(q_sb[:, i, :], bank, ACT.Copy)
                    nc.scalar.activation(rot[:, i, 0:8, :].rearrange("p h d -> p (h d)"), bank, ACT.Copy).then_inc(evac_done, 1)
                split_high(sec, L_KVS + 2)
                split_high(sec, L_KVS + 3)
                for i in range(TT):
                    bank = by_unit(sec, F_KVS + i, L_KVS + 1).rearrange("p (s kv g d) -> p s kv g d", s=2, kv=2, g=GROUPS)
                    dst = rot[:, i, 8:16, :].rearrange("p (s g u) d -> p s g u d", s=2, g=GROUPS)
                    for u in range(2):
                        nc.scalar.activation(dst[:, :, :, u, :], bank[:, :, 0, :, :], ACT.Copy)
                    nc.scalar.activation(v_sb[:, i, :, :].rearrange("p s (g d) -> p s g d", g=GROUPS),
                                         bank[:, :, 1, :, :], ACT.Copy).then_inc(evac_done, 1)
                for w in range(2):
                    copy_out(by_small(sec, F_PLAIN + w, S_PLAIN + w), pair(qT, w))
                act.wait_ge(cmpx_ready, layer * 2 + 2)
                for c in range(2):
                    nc.scalar.activation(cmp_hi[c], cmp_x[c].rearrange("p m g n -> p m (g n)"), ACT.Copy).then_inc(cmphi_ready, 1)
                for w in range(2):
                    split_high(sec, L_QMEM + w + 2)
                    copy_out(by_unit(sec, F_QMEM + w, L_QMEM + w), pair(qmemT, w))
                act.wait_ge(conv_ready, layer + 1)

                def hidden(c, t, n, f):
                    split_high(sec, n + 2)
                    bank = by_unit(sec, f, n)
                    nc.scalar.activation(hid[c][:, t, :], bank[:, 0:GROUPS * N_CMP], ACT.Gelu_apprx_tanh,
                                         bias=lp(("k_b1", "v_b1")[c])[:, t:t + 1]).then_inc(evac_done, 1)

                def merge_out(w):
                    copy_out(by_unit(sec, F_MERGE[w], L_MERGE[w]), merge[:, 512 * w:512 * w + 512])

                def step_work(kind, k):
                    if kind == "merge":
                        split_high(sec, L_MERGE[k] + 2)
                        merge_out(k)
                    elif kind == "cmpk":
                        hidden(0, k, L_CMPK[k], F_HIDK[k])
                    elif kind == "cmpv":
                        hidden(1, k, L_CMPV[k], F_HIDV[k])
                    elif kind == "rot":
                        copy_out(by_small(sec, F_ROT[k], S_ROT + k), pair(headT, k))
                    elif kind == "kc":
                        copy_out(by_small(sec, F_KC, S_KC)[:, 0:GROUPS * N_CMP], kcT)
                    else:
                        copy_out(by_small(sec, F_VC, S_VC)[0:N_CMP, 0:GROUPS * HD], vc[0:N_CMP, :, :].rearrange("p g d -> p (g d)"))

                def sigmoid(b):
                    g = merge[:, KD * T * b:KD * T * (b + 1)]
                    nc.scalar.activation(g, g, ACT.Sigmoid).then_inc(gate_ready, 1)

                jobs = jobs_of(sec)
                exps(sec, 0, jobs[0])
                for n, job in enumerate(jobs):
                    if n + 1 < len(jobs):
                        exps(sec, n + 1, jobs[n + 1])
                    for kind, k in STEP_WORK.get(n, ()):
                        step_work(kind, k)
                    if merge_half(n):
                        w, half = merge_half(n)
                        if half == 0:
                            split_high(sec, L_MERGE[w] + 2)
                        else:
                            if w == CONV_FREE:
                                act.wait_ge(convlo_ready, layer + 1)
                            merge_out(w)
                    if n == CONV_STEP:
                        nc.scalar.activation(br_hi[0], conv_y, ACT.Copy).then_inc(convhi_ready, 1)
                    copy_pT(sec, n, job)
                    if n:
                        high_tile(sec, jobs[n - 1])
                act.wait_ge(evac_done, sec.fill(F_FILLS))
                sigmoid(BRANCHES[0])
                split_high(sec, L_BR + 2)
                high_tile(sec, jobs[-1])
                split_high(sec, L_BR + 3)
                sigmoid(BRANCHES[1])
                split_high(sec, L_BR + 4)
                sigmoid(BRANCHES[2])
                for w in range(3, 6):
                    split_high(sec, L_BR + w + 2)
                for c in range(4):
                    act.wait_ge(merged_ready, layer * 4 + c + 1)
                    nc.scalar.activation(pair(merged_hi, c), pair(merged, c), ACT.Copy).then_inc(mhi_ready, 1)
                for w in range(4):
                    split_high(sec, L_OUT + w + 2)
                post_sums(sec, 1, L_FFN2 - 1)
                for i in range(TT):
                    x_squares(sec, 3, 1, i)
                load_post(sec, 2)
                x_high(sec, 3)
                ffn(sec, L_FFN2, 1, more=False)
                post_sums(sec, 2, L_UNITS - 1)

        @block.vector
        def _(dve):
            step = Steps(dve, dve_step, DVE_STEPS[0], DVE_STEPS[1])

            def split_low(sec, n, trip=0):
                s = n % RING
                dve.wait_ge(hi_ready, sec.unit(n + 1) + trip * RING)
                nc.vector.tensor_tensor(lo[:, s, :], raw[:, s, :], hi[:, s, :].bitcast(F32), ALU.subtract).then_inc(lo_ready, 1)

            def root(sec, p, c, n, sums_at, width):
                nc.vector.tensor_scalar(var[:, c:c + n], sums_at, 1.0 / width, EPS, ALU.mult, ALU.add).then_inc(pow_asked, 1)
                dve.wait_ge(pow_ready, sec.at(*POWS, p + 1))

            def x_scaled(sec, k, p, i):
                dve.wait_ge(sq_ready, sec.at(8, 8, 2 * k + i + 1))
                root(sec, p, i, 1, sums[:, i:i + 1], D)
                if i == 0:
                    if sec.layer is None:
                        dve.wait_ge(pre_loaded, 16 * max(k, 1))
                    elif k > 0:
                        dve.wait_ge(pre_loaded, sec.at(48, 32, 16 * (k - 1)))
                nc.vector.scalar_tensor_tensor(xs[:, i, :], x[:, i, :], rstd[:, i:i + 1], pre, ALU.mult, ALU.mult).then_inc(xs_ready, 1)

            def x_low(sec, k):
                for i in range(TT):
                    for b in range(2):
                        dve.wait_ge(xhi_ready, sec.at(16, 16, 4 * k + 2 * i + b + 1))
                        nc.vector.tensor_tensor(rows_operand(xT_lo, i, b), rows_bank(i, b), rows_operand(xT_hi, i, b).bitcast(F32),
                                                ALU.subtract).then_inc(xlo_ready, 1)

            def mem_scaled(sec, p):
                dve.wait_ge(sq_ready, sec.at(8, 8, 4))
                root(sec, p, 4, TT, sums[:, 0:TT], D)
                for i in range(TT):
                    nc.vector.tensor_scalar(xs[:, i, :], mem_in[:, i, :], rstd[:, 4 + i:5 + i], None, ALU.mult).then_inc(xs_ready, 1)

            def mem_low(sec, r, gain):
                dve.wait_ge(xhi_ready, sec.at(16, 16, 4 + r + 1))
                for c in range(2):
                    kt = 2 * r + c
                    ins = nc.vector.scalar_tensor_tensor(memT_lo[:, kt, :], work[:, 2 + r % 2, T * c:T * c + T], gain[:, kt:kt + 1],
                                                         memT_hi[:, kt, :].bitcast(F32), ALU.mult, ALU.subtract)
                ins.then_inc(xlo_ready, 1)

            def ffn(sec, u0, k, begin=None, mem_gain=None, more=True):
                c0 = sec.at(2 * CHUNKS, 2 * CHUNKS, k * CHUNKS)

                def gated(j, n, trip=0):
                    dve.wait_ge(silu_ready, c0 + j + 1)
                    dve.wait_ge(unit_used, sec.unit(n + 1) + trip * RING)
                    wait(dve, hTlo_ready, c0 + j)
                    nc.vector.tensor_tensor(h_sb, silu_a, work[:, 1, :], ALU.mult).then_inc(h_ready, 1)

                def low_h(j, high, low):
                    dve.wait_ge(hThi_ready, c0 + j + 1)
                    nc.vector.tensor_tensor(low.rearrange("p f t -> p (f t)"), h_sb,
                                            high.rearrange("p f t -> p (f t)").bitcast(F32), ALU.subtract).then_inc(hTlo_ready, 1)

                split_low(sec, u0 + 2)
                split_low(sec, u0 + 3)
                gated(0, u0 + 1)
                if begin:
                    begin()
                with dve.Fori(1, CHUNKS - 1) as j:
                    low_h(j - 1, hT_hi, hT_lo)
                    split_low(sec, u0 + 1, j)
                    split_low(sec, u0 + 2, j)
                    gated(j, u0, j)
                    split_low(sec, u0 + 3, j)
                last = CHUNKS - 1
                low_h(last - 1, hT_hi, hT_lo)
                split_low(sec, u0 + 1 + 3 * last)
                split_low(sec, u0 + 2 + 3 * last)
                gated(last, u0 + 3 * last)
                if mem_gain is not None:
                    mem_low(sec, 0, mem_gain)
                    mem_low(sec, 1, mem_gain)
                low_h(last, *hT_last)
                if more:
                    split_low(sec, u0 + FFN_UNITS)
                if mem_gain is not None:
                    mem_low(sec, 2, mem_gain)
                    mem_low(sec, 3, mem_gain)
                if more:
                    split_low(sec, u0 + FFN_UNITS + 1)

            def residual(sec, r, n, i, scale):
                if i == 0:
                    dve.wait_ge(sum0_ready, sec.at(3, 3, r + 1))
                else:
                    dve.wait_ge(unit_used, sec.unit(n + 1))
                nc.vector.scalar_tensor_tensor(x[:, i, :], tile_sums(i), scale, x[:, i, :], ALU.mult, ALU.add).then_inc(x_ready, 1)

            def post_residual(sec, r, p, scale):
                for i in range(TT):
                    dve.wait_ge(ysq_ready, sec.at(0, 6, 2 * r + i + 1))
                    root(sec, p + i, 2 + i, 1, ysums[:, i:i + 1], D)
                    if i == 0:
                        dve.wait_ge(post_loaded, sec.at(0, 48, 16 * (r + 1)))
                    step.link(nc.vector.scalar_tensor_tensor(xs[:, i, :], tile_sums(i), rstd[:, 2 + i:3 + i], post, ALU.mult, ALU.mult))
                    nc.vector.scalar_tensor_tensor(x[:, i, :], xs[:, i, :], scale, x[:, i, :], ALU.mult, ALU.add).then_inc(x_ready, 1)

            def score(sec, n, job):
                dve.wait_ge(qk_ready, sec.at(*JOBS, n + 1))
                nc.vector.memset(soft[:, n % 2, 2, :], 0.0)
                for i in range(TT):
                    w = job.width(i)
                    nc.vector.tensor_tensor_reduce(
                        out=prob[:, n % 2, i, 0:w], in0=acc[:, n % 2, T * i:T * i + w], in1=job.bias(i, w),
                        scale=-job.scale, scalar=BIG, op0=ALU.add, op1=ALU.min,
                        accum_out=soft[:, n % 2, 0, i:i + 1]).then_inc(scored, 1)

            def normalise(sec, n, job):
                dve.wait_ge(exp_ready, sec.at(2 * JOBS[0], 2 * JOBS[1], 2 * n + 2))
                step.link(nc.vector.reciprocal(soft[:, n % 2, 2, :], soft[:, n % 2, 1, :]))
                for i in range(TT):
                    p = prob[:, n % 2, i, 0:job.width(i)]
                    if job.factor is None:
                        ins = nc.vector.tensor_scalar(p, p, soft[:, n % 2, 2, i:i + 1], None, ALU.mult)
                    else:
                        ins = nc.vector.tensor_scalar(p, p, soft[:, n % 2, 2, i:i + 1], job.factor(i), ALU.mult, ALU.mult)
                    ins.then_inc(p_ready, 1)

            def low_tile(sec, job):
                if job.tile_done:
                    dve.wait_ge(tile_hi, sec.at(*TILES, job.tile + 1))
                    high, low = tile_dst(sec, job.tile)
                    nc.vector.tensor_tensor(low, tile_bank(job.tile), high.bitcast(F32), ALU.subtract).then_inc(tile_lo, 1)

            sec = Section()
            step.enter(sec)
            for i in range(TT):
                x_scaled(sec, 0, i, i)
            dve.wait_ge(landed[0], 16)
            dve.sem_inc(lo_ready, 1)
            split_low(sec, B1_FFN1)
            x_low(sec, 0)
            split_low(sec, B1_FFN1 + 1)

            def tables():
                dve.wait_ge(const_in_sem, 48)
                step.link(nc.vector.tensor_copy(angle[:, 0, 0:TT], pos_i))
                for i in range(TT):
                    ins = nc.vector.tensor_scalar(angle[:, 1, ROT * i:ROT * i + ROT], cst("inv_freq"), angle[:, 0, i:i + 1],
                                                  None, ALU.mult)
                step.link(ins)
                step.link(nc.vector.tensor_scalar(angle[:, 2, :], angle[:, 1, :], 1.0 / TURN, ROUND, ALU.mult, ALU.add))
                step.link(nc.vector.tensor_scalar(angle[:, 2, :], angle[:, 2, :], -ROUND, None, ALU.add))
                for part in TURN_PARTS:
                    step.link(nc.vector.scalar_tensor_tensor(angle[:, 1, :], angle[:, 2, :], -part, angle[:, 1, :], ALU.mult, ALU.add))
                step.link(nc.vector.tensor_scalar(angle[:, 5, :], angle[:, 1, :], PI, -PI, ALU.min, ALU.max))
                step.link(nc.vector.tensor_scalar(angle[:, 3, :], angle[:, 5, :], -1.0, None, ALU.mult))
                step.link(nc.vector.tensor_tensor(angle[:, 3, :], angle[:, 3, :], angle[:, 5, :], ALU.max))
                nc.vector.tensor_scalar(angle[:, 4, :], angle[:, 3, :], -1.0, PI / 2, ALU.mult, ALU.add).then_inc(trig_asked, 1)
                lam = b1p("lam")
                step.link(nc.vector.tensor_scalar(lam_t[:, 2, :], lam, -1.0, None, ALU.mult))
                nc.vector.tensor_tensor(lam_t[:, 0, :], lam, lam_t[:, 2, :], ALU.min).then_inc(lam_asked, 1)
                dve.wait_ge(lam_exp, 1)
                step.link(nc.vector.tensor_scalar(lam_t[:, 3, :], lam_t[:, 1, :], 2.0, None, ALU.add))
                step.link(nc.vector.reciprocal(lam_t[:, 3, :], lam_t[:, 3, :]))
                step.link(nc.vector.tensor_tensor(lam_t[:, 3, :], lam_t[:, 1, :], lam_t[:, 3, :], ALU.mult))
                step.link(nc.vector.tensor_tensor(lam_t[:, 4, :], lam_t[:, 3, :], lam_t[:, 3, :], ALU.mult))
                step.link(nc.vector.tensor_scalar(lam_t[:, 5, :], lam_t[:, 4, :], 1.0 / 17, None, ALU.mult))
                for odd in (15, 13, 11, 9, 7, 5, 3):
                    step.link(nc.vector.scalar_tensor_tensor(lam_t[:, 5, :], lam_t[:, 5, :], 1.0 / odd, lam_t[:, 4, :], ALU.add, ALU.mult))
                step.link(nc.vector.scalar_tensor_tensor(lam_t[:, 5, :], lam_t[:, 5, :], 1.0, lam_t[:, 3, :], ALU.add, ALU.mult))
                step.link(nc.vector.tensor_scalar(lam_t[:, 2, :], lam_t[:, 2, :], 0.0, None, ALU.max))
                step.link(nc.vector.scalar_tensor_tensor(lam_t[:, 2, :], lam_t[:, 5, :], 2.0, lam_t[:, 2, :], ALU.mult, ALU.add))
                nc.vector.tensor_scalar(lam_t[:, 5, :], lam_t[:, 2, :], -LRU_C, None, ALU.mult)
                nc.vector.tensor_scalar(lam_t[:, 6, :], lam_t[:, 2, :], LRU_C, None, ALU.mult).then_inc(lam_ready, 1)

            def begin():
                mem_scaled(sec, 2)
                tables()

            ffn(sec, B1_FFN1, 0, begin, b1p("g_mem"))
            for i in range(TT):
                residual(sec, 0, B1_MEM - 1, i, 0.5)
            split_low(sec, B1_MEM + 2)
            for i in range(TT):
                x_scaled(sec, 2, 3 + i, i)
            split_low(sec, B1_MEM + 3)
            x_low(sec, 2)
            split_low(sec, B1_LRU_X + 2)
            pads = step.mark(nc.vector.memset(lru_in[:, :, 0:CONV_W - 1], 0.0))
            conv_w = b1p("conv_w").rearrange("p (c w) -> p c w", c=LRU_TILES)
            for half in range(2):
                split_low(sec, B1_LRU_X + half + 3)
                dve.wait_ge(evac_done, F1_LRU_X + half + 1)
                step.after(pads)
                for tap in range(CONV_W):
                    for c in (2 * half, 2 * half + 1):
                        shifted = lru_in[:, c, tap:tap + T]
                        if tap == 0:
                            m = step.mark(nc.vector.tensor_scalar(lru_xb[:, c, :], shifted, conv_w[:, c, 0:1],
                                                                  b1p("conv_b")[:, c:c + 1], ALU.mult, ALU.add))
                            continue
                        step.after(m - 1 + c % 2 if tap == 1 or c % 2 == 0 else m)
                        ins = nc.vector.scalar_tensor_tensor(lru_xb[:, c, :], shifted, conv_w[:, c, tap:tap + 1],
                                                             lru_xb[:, c, :], ALU.mult, ALU.add)
                        if tap < CONV_W - 1:
                            m = step.mark(ins)
                        elif c % 2:
                            ins.then_inc(xb_ready, 1)
            split_low(sec, B1_QK + 3)
            for i in range(TT):
                ins = nc.vector.tensor_copy(heads1[:, i, 12:16, :].rearrange("p h d -> p (h d)"), memv[:, i, 0:T])
            step.link(ins)
            split_low(sec, B1_VC + 2)
            split_low(sec, B1_VC + 3)
            dve.wait_ge(evac_done, F1_VC + 2)
            flat = heads1.rearrange("p i h d -> p (i h) d")
            flat_sq = squares.rearrange("p i h d -> p (i h) d")
            step.link(nc.vector.tensor_tensor(flat_sq, flat, flat, ALU.mult))
            step.link(nc.vector.reduce_sum(sums, flat_sq, axis=AX_X))
            root(sec, 5, 0, 32, sums, HD)
            nc.vector.tensor_tensor(flat, flat, rstd.unsqueeze(2).to_broadcast([P, 32, HD]), ALU.mult).then_inc(heads_ready, 1)
            split_low(sec, B1_LRU_G + 2)

            def lru_step(n):
                if n == 0:
                    dve.wait_ge(lru_a_ready, 1)
                    step.link(nc.vector.tensor_tensor(lru_y, lru_a, lru_a, ALU.mult))
                    nc.vector.scalar_tensor_tensor(lru_m, lru_y, 1.0, lru_m, ALU.add, ALU.mult).then_inc(m2_ready, 1)
                elif n == 1:
                    split_low(sec, B1_OUT + 1)
                    step.link(nc.vector.tensor_tensor(lru_xb, lru_xb, lru_i, ALU.mult))
                elif n == 2:
                    split_low(sec, B1_OUT + 2)
                elif n == 3:
                    dve.wait_ge(mult_ready, 1)
                    step.link(nc.vector.memset(lru_r[:, :, 0:1], 1.0))
                    step.link(nc.vector.tensor_tensor(lru_xb, lru_xb, lru_r, ALU.mult))
                elif n == 4:
                    for c in range(LRU_TILES):
                        ins = nc.vector.tensor_tensor_scan(lru_m[:, c, :], lru_a[:, c, :], lru_xb[:, c, :], 0.0, ALU.mult, ALU.add)
                    step.link(ins)
                    dve.wait_ge(evac_done, F1_FILLS)
                    nc.vector.tensor_tensor(lru_y, lru_m, lru_g, ALU.mult).then_inc(lruy_ready, 1)
                elif n == 5:
                    dve.wait_ge(lruhi_ready, 1)
                    nc.vector.tensor_tensor(mix_lo[:, 0:LRU_TILES, :], lru_y, mix_hi[:, 0:LRU_TILES, :].bitcast(F32),
                                            ALU.subtract).then_inc(lrulo_ready, 1)

            jobs = jobs_of(sec)
            score(sec, 0, jobs[0])
            normalise(sec, 0, jobs[0])
            for n, job in enumerate(jobs):
                if n + 1 < len(jobs):
                    score(sec, n + 1, jobs[n + 1])
                lru_step(n)
                if n + 1 < len(jobs):
                    normalise(sec, n + 1, jobs[n + 1])
                if n:
                    low_tile(sec, jobs[n - 1])
            low_tile(sec, jobs[-1])
            for w in range(1, 4):
                split_low(sec, B1_OUT + w + 2)
            for i in range(TT):
                residual(sec, 1, B1_FFN2 - 1, i, 1.0)
            for i in range(TT):
                x_scaled(sec, 3, 6 + i, i)
            x_low(sec, 3)
            ffn(sec, B1_FFN2, 1, more=False)
            for i in range(TT):
                residual(sec, 2, B1_UNITS - 1, i, 0.5)
            step.leave()

            with dve.Fori(0, LAYERS) as layer:
                sec = Section(layer)
                step.enter(sec)
                dve.wait_ge(landed[L_PARAM], sec.landed(L_PARAM))
                dve.wait_ge(landed[L_GAIN], sec.landed(L_GAIN))
                dve.wait_ge(lo_ready, sec.unit(0))
                dve.sem_inc(lo_ready, L_FFN1)
                split_low(sec, L_FFN1)
                for i in range(TT):
                    x_scaled(sec, 0, i, i)
                x_low(sec, 0)
                split_low(sec, L_FFN1 + 1)
                ffn(sec, L_FFN1, 0, lambda: mem_scaled(sec, 2), lp("g_mem"))
                post_residual(sec, 0, 3, 0.5)
                split_low(sec, L_MEM + 2)
                for i in range(TT):
                    x_scaled(sec, 2, 5 + i, i)
                split_low(sec, L_MEM + 3)
                dve.wait_ge(gwhi_ready, layer + 1)
                nc.vector.tensor_tensor(gw_lo.rearrange("p k n -> p (k n)"), lp("gate_w"),
                                        gw_hi.rearrange("p k n -> p (k n)").bitcast(F32), ALU.subtract).then_inc(gwlo_ready, 1)
                split_low(sec, L_MEM + 4)
                x_low(sec, 2)
                split_low(sec, L_MEM + 5)
                with dve.Fori(0, 2) as trip:
                    for w in range(3):
                        split_low(sec, L_CONV + w + 2, trip)
                split_low(sec, L_KV + 2)
                convolved = conv_in.rearrange("p (k c t) -> p k c t", k=3, c=4)
                conv_w = lp("conv_w").rearrange("p (c w) -> p c w", c=4)

                def conv_tile(c):
                    for tap in range(CONV2_W):
                        shifted = conv_v[:, c, tap:tap + T]
                        if tap == 0:
                            step.link(nc.vector.tensor_scalar(conv_y[:, c, :], shifted, conv_w[:, c, 0:1], None, ALU.mult))
                        else:
                            step.link(nc.vector.scalar_tensor_tensor(conv_y[:, c, :], shifted, conv_w[:, c, tap:tap + 1],
                                                                     conv_y[:, c, :], ALU.mult, ALU.add))
                    return nc.vector.tensor_tensor(conv_y[:, c, :], conv_y[:, c, :], convolved[:, 1, c, :], ALU.mult)

                dve.wait_ge(evac_done, sec.fill(F_KV))
                step.link(nc.vector.memset(conv_v[:, :, 0:CONV2_W - 1], 0.0))
                step.link(nc.vector.tensor_tensor(conv_v[:, :, CONV2_W - 1:], convolved[:, 2, :, :], convolved[:, 0, :, :], ALU.mult))
                split_low(sec, L_Q + 2)
                conv_tile(0)
                split_low(sec, L_Q + 3)
                conv_tile(1)
                dve.wait_ge(evac_done, sec.fill(F_GATE + 1))
                for i in range(TT):
                    g0 = gates[:, i, :].rearrange("p (h b) -> p h b", b=3)[:, :, 0]
                    ins = nc.vector.tensor_scalar(g0, g0, cst("cmp_valid")[:, i:i + 1], None, ALU.mult)
                step.link(ins)
                for c, name in enumerate(("pos_k", "pos_v")):
                    for g in range(GROUPS):
                        base = cmp_src[c][:, g, :]
                        windows = bass.AP(base.tensor, base.offset, [base.ap[0], [2, CMP_PAIRS], [CMP_STRIDE, N_CMP]])
                        ins = nc.vector.tensor_tensor(cmp_x[c][:, :, g, :], windows,
                                                      lp(name).unsqueeze(2).to_broadcast([P, CMP_PAIRS, N_CMP]), ALU.add)
                    ins.then_inc(cmpx_ready, 1)
                split_low(sec, L_KVS + 2)
                conv_tile(2)
                split_low(sec, L_KVS + 3)
                conv_tile(3).then_inc(conv_ready, 1)
                for c in range(2):
                    dve.wait_ge(cmphi_ready, layer * 2 + c + 1)
                    nc.vector.tensor_tensor(cmp_lo[c], cmp_x[c].rearrange("p m g n -> p m (g n)"), cmp_hi[c].bitcast(F32),
                                            ALU.subtract).then_inc(cmplo_ready, 1)
                split_low(sec, L_QMEM + 2)
                t1, t2 = rot[:, :, :, 0:ROT], rot[:, :, :, ROT:2 * ROT]
                cosines, sines = (trig[:, c, :, :].unsqueeze(2).to_broadcast([P, TT, 16, ROT]) for c in range(2))
                for n, (a, b) in enumerate(((t1, cosines), (t2, sines), (t2, cosines), (t1, sines))):
                    for i in range(TT):
                        ins = nc.vector.tensor_tensor(rope_t[:, n, i], a[:, i], b[:, i], ALU.mult)
                step.link(ins)
                nc.vector.tensor_tensor(t1, rope_t[:, 0], rope_t[:, 1], ALU.subtract)
                nc.vector.tensor_tensor(t2, rope_t[:, 2], rope_t[:, 3], ALU.add).then_inc(rot_ready, 1)
                dve.wait_ge(rot_ready, layer + 1)
                split_low(sec, L_QMEM + 3)

                def step_work(kind, k):
                    if kind in ("merge", "cmpk", "cmpv"):
                        split_low(sec, {"merge": L_MERGE, "cmpk": L_CMPK, "cmpv": L_CMPV}[kind][k] + 2)

                jobs = jobs_of(sec)
                score(sec, 0, jobs[0])
                normalise(sec, 0, jobs[0])
                for n, job in enumerate(jobs):
                    if n + 1 < len(jobs):
                        score(sec, n + 1, jobs[n + 1])
                    for kind, k in STEP_WORK.get(n, ()):
                        step_work(kind, k)
                    if merge_half(n) and merge_half(n)[1] == 0:
                        split_low(sec, L_MERGE[merge_half(n)[0]] + 2)
                    if n == CONV_STEP + 1:
                        dve.wait_ge(convhi_ready, layer + 1)
                        nc.vector.tensor_tensor(br_lo[0], conv_y, br_hi[0].bitcast(F32), ALU.subtract).then_inc(convlo_ready, 1)
                    if n + 1 < len(jobs):
                        normalise(sec, n + 1, jobs[n + 1])
                    if n:
                        low_tile(sec, jobs[n - 1])
                partial = []
                gate = merge.rearrange("p (b c t) -> p b c t", b=3, c=KD)

                def merged_low(c):
                    dve.wait_ge(mhi_ready, layer * 4 + c + 1)
                    c2 = slice(2 * c, 2 * c + 2)
                    nc.vector.tensor_tensor(merged_lo[:, c2, :], merged[:, c2, :], merged_hi[:, c2, :].bitcast(F32),
                                            ALU.subtract).then_inc(mlo_ready, 1)

                for w in range(6):
                    split_low(sec, L_BR + w + 2)
                    b, half = w // 2, w % 2
                    if w == 1:
                        low_tile(sec, jobs[-1])
                    if w == 5:
                        merged_low(0)
                        merged_low(1)
                    dve.wait_ge(gate_ready, layer * 3 + b + 1)
                    for k in range(2):
                        if k == 0:
                            dve.wait_ge(br_half, layer * 6 + w + 1)
                        else:
                            dve.wait_ge(unit_used, sec.unit(L_BR + w + 1))
                        c = slice(4 * half + 2 * k, 4 * half + 2 * k + 2)
                        bank = br_bank(w, k).rearrange("p (c t) -> p c t", c=2)
                        g = gate[:, BRANCHES[b], c, :]
                        if b == 0:
                            nc.vector.tensor_tensor(merged[:, c, :], bank, g, ALU.mult).then_inc(br_read, 1)
                            continue
                        t = br_t[:, k, :].rearrange("p (c t) -> p c t", c=2)
                        nc.vector.tensor_tensor(t, bank, g, ALU.mult).then_inc(br_read, 1)
                        dve.wait_ge(br_read, layer * 12 + (2 * w + k + 1))
                        if b == 2:
                            step.after(partial[2 * half + k])
                        ins = nc.vector.tensor_tensor(merged[:, c, :], merged[:, c, :], t, ALU.add)
                        if b == 1:
                            partial.append(step.mark(ins))
                        else:
                            ins.then_inc(merged_ready, 1)
                merged_low(2)
                merged_low(3)
                for w in range(4):
                    split_low(sec, L_OUT + w + 2)
                post_residual(sec, 1, 7, 1.0)
                for i in range(TT):
                    x_scaled(sec, 3, 9 + i, i)
                x_low(sec, 3)
                ffn(sec, L_FFN2, 1, more=False)
                post_residual(sec, 2, 11, 0.5)
                step.leave()

        @block.tensor
        def _(pe):
            def product(dst, a_hi, a_lo, b_hi, b_lo, start, stop):
                nc.tensor.matmul(dst, a_hi, b_hi, start=start, stop=False)
                nc.tensor.matmul(dst, a_hi, b_lo, start=False, stop=False)
                return nc.tensor.matmul(dst, a_lo, b_hi, start=False, stop=stop)

            def parts_ready(sec, n, trip=0):
                pe.wait_ge(lo_ready, sec.unit(n + 1) + trip * RING)

            def rows_half(n, half, i, dst, a_hi, a_lo):
                s = n % RING
                for q in range(4):
                    kt = 4 * half + q
                    last = product(dst, a_hi[:, kt, P * i:P * i + P], a_lo[:, kt, P * i:P * i + P],
                                   hi[:, s, 512 * q:512 * q + 512], lo[:, s, 512 * q:512 * q + 512],
                                   kt == 0, kt == KD - 1)
                return last

            def bank_free(sec, f, trip=0):
                wait(pe, evac_done, sec.fill(f - 2) + trip * 3)

            def rows_unit(sec, n, f, half, a=(xT_hi, xT_lo)):
                if half == 0:
                    for i in range(TT):
                        bank_free(sec, f + i)
                parts_ready(sec, n + half)
                for i in range(TT):
                    last = rows_half(n + half, half, i, work[:, (f + i) % 3, :], *a)
                last.then_inc(unit_used, 1)

            def rows(sec, n, f, a=(xT_hi, xT_lo)):
                for half in range(2):
                    rows_unit(sec, n, f, half, a)

            def channel_tile(bank, n, c, a):
                s = n % RING
                for kt in range(KD):
                    w = slice(P * (KD * c + kt), P * (KD * c + kt) + P)
                    last = product(bank[:, T * c:T * c + T], hi[:, s, w], lo[:, s, w], a[0][:, kt, :], a[1][:, kt, :],
                                   kt == 0, kt == KD - 1)
                return last

            def channels(sec, n, f, trip=0, a=(xT_hi, xT_lo), tiles=(0, 1)):
                if 0 in tiles:
                    bank_free(sec, f, trip)
                    parts_ready(sec, n, trip)
                for c in tiles:
                    last = channel_tile(work[:, f % 3, :], n, c, a)
                if 1 in tiles:
                    last.then_inc(unit_used, 1)

            def transposes(sec, f, src):
                bank_free(sec, f)
                for c in range(2):
                    for i in range(TT):
                        last = nc.tensor.transpose(work[:, f % 3, T * c + P * i:T * c + P * i + P], src(c, i), ident)
                last.then_inc(small_ready, 1)

            def x_transposed(sec, k):
                for i in range(TT):
                    pe.wait_ge(xs_ready, sec.at(8, 8, 2 * k + i + 1))
                    for b in range(2):
                        for q in range(4):
                            last = nc.tensor.transpose(acc[:, 2 * i + b, P * q:P * q + P],
                                                       xs[:, i, P * (4 * b + q):P * (4 * b + q) + P], ident)
                        last.then_inc(xT_ready, 1)

            def mem_transposed(sec, r):
                if r == 0:
                    pe.wait_ge(xs_ready, sec.at(8, 8, 4))
                if r >= 2:
                    pe.wait_ge(xlo_ready, sec.at(16, 16, 4 + r - 1))
                for c in range(2):
                    for i in range(TT):
                        at = T * c + P * i
                        last = nc.tensor.transpose(work[:, 2 + r % 2, at:at + P], xs[:, i, P * (2 * r + c):P * (2 * r + c) + P], ident)
                last.then_inc(xT_ready, 1)

            def operand_ready(sec, k):
                pe.wait_ge(xlo_ready, sec.at(16, 16, 4 * k + 4))

            def ffn(sec, u0, k, before, mem=False):
                c0 = sec.at(2 * CHUNKS, 2 * CHUNKS, k * CHUNKS)
                wait(pe, evac_done, sec.fill(before))

                def chunk_in(n, j, trip, first=False):
                    for part in range(2):
                        if not first:
                            pe.wait_ge((silu_ready, h_ready)[part], c0 + j)
                        parts_ready(sec, n + part, trip)
                        for c in range(2):
                            last = channel_tile(work[:, part, :], n + part, c, (xT_hi, xT_lo))
                        last.then_inc(unit_used, 1)

                def chunk_out(n, j, trip, first=False, final=False):
                    s = n % RING
                    h = hT_last if final else (hT_hi, hT_lo)
                    pe.wait_ge(hTlo_ready, c0 + j + 1)
                    parts_ready(sec, n, trip)
                    for i in range(TT):
                        for f in range(2):
                            for c in range(2):
                                w = slice(D * f + 512 * c, D * f + 512 * c + 512)
                                last = product(acc[:, 2 * i + c, :], h[0][:, f, P * i:P * i + P], h[1][:, f, P * i:P * i + P],
                                               hi[:, s, w], lo[:, s, w], first and f == 0, final and f == 1)
                        if final and i == 0:
                            last.then_inc(sum0_ready, 1)
                    last.then_inc(unit_used, 1)

                chunk_in(u0, 0, 0, first=True)
                chunk_in(u0 + 2, 1, 0)
                chunk_out(u0 + 4, 0, 0, first=True)
                with pe.Fori(2, CHUNKS - 1) as j:
                    chunk_in(u0 - 1, j, j)
                    chunk_out(u0 + 1, j - 1, j)
                j = CHUNKS - 1
                chunk_in(u0 + 3 * j - 1, j, 0)
                if mem:
                    mem_transposed(sec, 0)
                    mem_transposed(sec, 1)
                chunk_out(u0 + 3 * j + 1, j - 1, 0)
                if mem:
                    mem_transposed(sec, 2)
                    mem_transposed(sec, 3)
                chunk_out(u0 + FFN_UNITS - 1, j, 0, final=True)

            def output(sec, n, a, ready):
                ready(0)
                for c in range(2):
                    parts_ready(sec, n + c)
                    for i in range(TT):
                        last = rows_half(n + c, 0, i, acc[:, 2 * i + c, :], *a)
                    last.then_inc(unit_used, 1)
                ready(1)
                parts_ready(sec, n + 2)
                for i in range(TT):
                    for c in range(2):
                        if i == 0 and c == 1:
                            parts_ready(sec, n + 3)
                        last = rows_half(n + 2 + c, 1, i, acc[:, 2 * i + c, :], *a)
                        if (i, c) == (0, 1):
                            last.then_inc(sum0_ready, 1)
                        elif i == 1:
                            last.then_inc(unit_used, 1)

            def scores(sec, n, job):
                if n >= 2:
                    pe.wait_ge(scored, sec.at(2 * JOBS[0], 2 * JOBS[1], 2 * n - 2))
                for i in range(TT):
                    w = job.width(i)
                    last = nc.tensor.matmul(acc[:, n % 2, T * i:T * i + w], job.q(i), job.k(w), start=True, stop=True)
                last.then_inc(qk_ready, 1)

            def turn(sec, n, job):
                pe.wait_ge(p_ready, sec.at(2 * JOBS[0], 2 * JOBS[1], 2 * n + 2))
                if n >= 1:
                    pe.wait_ge(pT_copied, sec.at(*JOBS, n))
                for kt, i, at in job.blocks():
                    r = job.rows(kt)
                    last = nc.tensor.transpose(acc[0:r, 2, at:at + P], prob[:, n % 2, i, P * kt:P * kt + r], ident)
                last.then_inc(pT_ready, 1)

            def values(sec, n, job):
                pe.wait_ge(pT_copied, sec.at(*JOBS, n + 1))
                if job.first and job.tile >= 2:
                    pe.wait_ge(tile_lo, sec.at(*TILES, job.tile - 1))
                at = 0
                for kt in range(job.key_tiles):
                    r, span = job.rows(kt), job.span(kt)
                    y = tile_bank(job.tile)[job.row:job.row + job.m, span:T]
                    last = nc.tensor.matmul(y, job.v(kt), probT[0:r, n % 2, at:at + T - span],
                                            start=job.first and kt == 0, stop=job.last and kt == job.key_tiles - 1)
                    at += T - span
                if job.tile_done:
                    last.then_inc(tile_ready, 1)

            sec = Section()
            pe.sem_inc(unit_used, 1)
            pe.wait_ge(const_in_sem, 48)
            x_transposed(sec, 0)
            operand_ready(sec, 0)
            ffn(sec, B1_FFN1, 0, 0, mem=True)
            operand_ready(sec, 1)
            rows_unit(sec, B1_MEM, F1_MEM, 0, (memT_hi, memT_lo))
            x_transposed(sec, 2)
            rows_unit(sec, B1_MEM, F1_MEM, 1, (memT_hi, memT_lo))
            operand_ready(sec, 2)
            for w in range(2):
                channels(sec, B1_LRU_X + w, F1_LRU_X + w)
            rows(sec, B1_QK, F1_QK)
            rows(sec, B1_VC, F1_VC)
            pe.wait_ge(xb_ready, 2)
            for w in range(4):
                bank_free(sec, F1_GATE + w)
                for c in range(2):
                    ct = 2 * (w % 2) + c
                    weights = b1p("a_w" if w < 2 else "x_w")[:, P * ct:P * ct + P]
                    last = nc.tensor.matmul(work[:, (F1_GATE + w) % 3, T * c:T * c + T], weights, lru_xb[:, ct, :],
                                            start=True, stop=True)
                last.then_inc(small_ready, 1)
            channels(sec, B1_LRU_G, F1_LRU_G0)
            pe.wait_ge(heads_ready, 1)
            for kind in range(4):
                transposes(sec, F1_HEADS + kind, lambda c, i: heads1[:, i, 4 * kind + 2 * c:4 * kind + 2 * c + 2, :].rearrange("p h d -> p (h d)"))
            jobs = jobs_of(sec)
            pe.wait_ge(evac_done, F1_HEADS + 4)
            scores(sec, 0, jobs[0])
            for n, job in enumerate(jobs):
                if n + 1 < len(jobs):
                    scores(sec, n + 1, jobs[n + 1])
                if n < 2:
                    channels(sec, B1_LRU_G + 1, F1_LRU_G1, tiles=(n,))
                turn(sec, n, job)
                if n:
                    values(sec, n - 1, jobs[n - 1])
            values(sec, len(jobs) - 1, jobs[-1])

            def mixed_ready(half):
                if half == 0:
                    pe.wait_ge(lrulo_ready, 1)
                    pe.wait_ge(tile_lo, jobs[-1].tile)
                else:
                    pe.wait_ge(tile_lo, jobs[-1].tile + 1)

            output(sec, B1_OUT, (mix_hi, mix_lo), mixed_ready)
            x_transposed(sec, 3)
            operand_ready(sec, 3)
            ffn(sec, B1_FFN2, 1, F1_FILLS)

            with pe.Fori(0, LAYERS) as layer:
                sec = Section(layer)
                pe.wait_ge(unit_used, sec.unit(0))
                pe.sem_inc(unit_used, L_FFN1)
                x_transposed(sec, 0)
                operand_ready(sec, 0)
                ffn(sec, L_FFN1, 0, 0, mem=True)
                operand_ready(sec, 1)
                for w in range(2):
                    channels(sec, L_MEM + w, F_MEMK + w, a=(memT_hi, memT_lo))
                x_transposed(sec, 2)
                rows(sec, L_MEM + 2, F_MEMV, (memT_hi, memT_lo))
                with pe.Fori(0, 2) as trip:
                    operand_ready(sec, 2)
                    for w in range(3):
                        channels(sec, L_CONV + w, F_CONV + w, trip)
                channels(sec, L_KV, F_KV)
                pe.wait_ge(gwlo_ready, layer + 1)
                bank_free(sec, F_GATE)
                for i in range(TT):
                    for kt in range(KD):
                        last = product(work[:, F_GATE % 3, GATES * i:GATES * i + GATES], xT_hi[:, kt, P * i:P * i + P],
                                       xT_lo[:, kt, P * i:P * i + P], gw_hi[:, kt, :], gw_lo[:, kt, :], kt == 0, kt == KD - 1)
                last.then_inc(small_ready, 1)
                rows(sec, L_Q, F_Q)
                rows(sec, L_KVS, F_KVS)
                for w in range(2):
                    transposes(sec, F_PLAIN + w, lambda c, i: q_sb[:, i, P * (2 * w + c):P * (2 * w + c) + P])
                for w in range(2):
                    channels(sec, L_QMEM + w, F_QMEM + w)

                def hidden(c, n, f):
                    pe.wait_ge(cmplo_ready, layer * 2 + c + 1)
                    bank_free(sec, f)
                    parts_ready(sec, n)
                    for m in range(CMP_PAIRS):
                        w = slice(P * m, P * m + P)
                        last = product(work[:, f % 3, 0:GROUPS * N_CMP], hi[:, n % RING, w], lo[:, n % RING, w],
                                       cmp_hi[c][:, m, :], cmp_lo[c][:, m, :], m == 0, m == CMP_PAIRS - 1)
                    last.then_inc(unit_used, 1)

                def compressed_keys():
                    w2 = lp("k_w2").rearrange("p (t d) -> p t d", t=2)
                    bank_free(sec, F_KC)
                    for t in range(2):
                        last = nc.tensor.matmul(work[:, F_KC % 3, 0:GROUPS * N_CMP], w2[:, t, :], hid[0][:, t, :],
                                                start=t == 0, stop=t == 1)
                    last.then_inc(small_ready, 1)

                def compressed_values():
                    w2 = lp("v_w2").rearrange("p (t d) -> p t d", t=2)
                    bank_free(sec, F_VC)
                    for g in range(GROUPS):
                        for t in range(2):
                            last = nc.tensor.matmul(work[0:N_CMP, F_VC % 3, HD * g:HD * g + HD],
                                                    hid[1][:, t, N_CMP * g:N_CMP * g + N_CMP], w2[:, t, :],
                                                    start=t == 0, stop=t == 1)
                    last.then_inc(small_ready, 1)

                def step_work(kind, k):
                    if kind == "merge":
                        channels(sec, L_MERGE[k], F_MERGE[k])
                    elif kind == "cmpk":
                        hidden(0, L_CMPK[k], F_HIDK[k])
                    elif kind == "cmpv":
                        hidden(1, L_CMPV[k], F_HIDV[k])
                    elif kind == "rot":
                        pe.wait_ge(rot_ready, layer + 1)
                        transposes(sec, F_ROT[k], lambda c, i: rot[:, i, 4 * k + 2 * c:4 * k + 2 * c + 2, :].rearrange("p h d -> p (h d)"))
                    elif kind == "kc":
                        compressed_keys()
                    else:
                        compressed_values()

                operands = {0: F_QMEM + 2, FIRST_NSA: F_ROT[3] + 1, FIRST_NSA + 2: F_VC + 1}
                jobs = jobs_of(sec)
                pe.wait_ge(evac_done, sec.fill(operands[0]))
                scores(sec, 0, jobs[0])
                for n, job in enumerate(jobs):
                    if n + 1 < len(jobs):
                        if n + 1 in operands:
                            pe.wait_ge(evac_done, sec.fill(operands[n + 1]))
                        scores(sec, n + 1, jobs[n + 1])
                    for kind, k in STEP_WORK.get(n, ()):
                        step_work(kind, k)
                    if merge_half(n):
                        w, half = merge_half(n)
                        channels(sec, L_MERGE[w], F_MERGE[w], tiles=(half,))
                    turn(sec, n, job)
                    if n:
                        values(sec, n - 1, jobs[n - 1])

                def branch(w):
                    b, n = BRANCHES[w // 2], L_BR + w
                    if w >= 2:
                        pe.wait_ge(br_read, layer * 12 + (2 * w - 2))
                    parts_ready(sec, n)
                    for c in range(4):
                        for kt in range(4):
                            at = slice(P * (4 * c + kt), P * (4 * c + kt) + P)
                            last = product(br_bank(w, c // 2)[:, T * (c % 2):T * (c % 2) + T], hi[:, n % RING, at],
                                           lo[:, n % RING, at], br_hi[b][:, kt, :], br_lo[b][:, kt, :], kt == 0, kt == 3)
                        if c == 1:
                            last.then_inc(br_half, 1)
                    last.then_inc(unit_used, 1)

                pe.wait_ge(convlo_ready, layer + 1)
                pe.wait_ge(evac_done, sec.fill(F_FILLS))
                branch(0)
                values(sec, len(jobs) - 1, jobs[-1])
                branch(1)
                branch(2)
                branch(3)
                pe.wait_ge(tile_lo, sec.at(*TILES, TILES[1]))
                branch(4)
                branch(5)
                output(sec, L_OUT, (merged_hi, merged_lo), lambda half: pe.wait_ge(mlo_ready, layer * 4 + 2 * half + 2))
                x_transposed(sec, 3)
                operand_ready(sec, 3)
                ffn(sec, L_FFN2, 1, F_FILLS)


DVE_STEPS = (56, 54)

PI = float(np.float32(np.nextafter(np.float32(np.pi), np.float32(0))))
TURN = float(2 * np.pi)
ROUND = 1.5 * 2.0 ** 23


def turn_parts():
    rest, parts = TURN, []
    for bits in (5, 14, 23):
        part = np.floor(rest * 2.0 ** bits) / 2.0 ** bits
        parts.append(float(part))
        rest -= part
    return parts + [float(np.float32(rest))]


TURN_PARTS = turn_parts()


def rows_units(w):
    t = w.reshape(KD, P, w.shape[1]).transpose(1, 0, 2)
    return [t[:, 0:4].reshape(P, UNIT), t[:, 4:8].reshape(P, UNIT)]


def channel_units(w):
    k, n = w.shape
    t = w.reshape(k // P, P, n // P, P).transpose(1, 2, 0, 3).reshape(P, -1)
    return [t[:, a:a + UNIT] for a in range(0, t.shape[1], UNIT)]


def ffn_units(w_in, w_out):
    into, outof = [], []
    for j in range(CHUNKS):
        a = w_in[:, CHUNK * j:CHUNK * (j + 1)]
        b = w_in[:, D_FF + CHUNK * j:D_FF + CHUNK * (j + 1)]
        into.append(channel_units(a) + channel_units(b))
        outof.append(w_out[CHUNK * j:CHUNK * (j + 1)].reshape(2, P, D).transpose(1, 0, 2).reshape(P, UNIT))
    order = list(into[0])
    for j in range(1, CHUNKS):
        order += [*into[j], outof[j - 1]]
    return order + [outof[-1]]


def output_units(w):
    (a, b), (c, d) = rows_units(w[:, 0:512]), rows_units(w[:, 512:1024])
    return [a, c, b, d]


def by_partition(v):
    return v.reshape(-1, P).T


def pack(table, total, fields):
    packed = np.zeros((P, total), np.float32)
    for name, value in fields.items():
        at, n = table[name]
        packed[:, at:at + n] = value.reshape(P, n)
    return packed


def twice(v):
    return np.concatenate([v, v]).reshape(P, 1)


def block_diagonal(w):
    t = np.zeros((P, LRU_TILES, P), np.float32)
    for n in range(2 * LRU_TILES):
        at = 64 * (n % 2)
        t[at:at + 64, n // 2, at:at + 64] = w[n]
    return t


def constants():
    q = np.arange(P)
    made = np.zeros((P, CONST_N), np.float32)

    def put(name, value):
        at, n = CONST[name]
        made[:, at:at + n] = np.asarray(value, np.float32).reshape(P, n)

    distance = np.concatenate([q[:, None] - np.arange(P)[None], P + q[:, None] - np.arange(T)[None]], axis=1)
    put("ident", np.eye(P))
    put("causal", np.where(distance >= 0, 0.0, NEG))
    token = q[:, None] + P * np.arange(TT)[None]
    ends = np.arange(16) * CMP_STRIDE + CMP_BLOCK - 1
    put("cmp_mask", np.where(ends[None, None] <= token[:, :, None], 0.0, NEG))
    put("cmp_valid", token >= CMP_BLOCK - 1)
    put("inv_freq", np.broadcast_to(np.float32(ROPE_THETA) ** (-np.arange(0, 2 * ROT, 2, dtype=np.float32) / np.float32(2 * ROT)), (P, ROT)))
    slopes = 2.0 ** (-8.0 * np.arange(1, 5) / 4)
    alibi = np.stack([np.where(distance >= 0, -s * HD ** 0.5 * distance, NEG) for s in slopes], axis=1)
    return made, alibi.astype(np.float32).reshape(P, ALIBI_N)


def lay_out(a):
    b1_params = pack(B1P, B1P_N, {
        "a_w": block_diagonal(a["lru_a_w"][0]), "x_w": block_diagonal(a["lru_x_w"][0]),
        "conv_w": a["lru_conv_w"][0].reshape(CONV_W, LRU_TILES, P).transpose(2, 1, 0),
        "conv_b": by_partition(a["lru_conv_b"][0]), "a_b": by_partition(a["lru_a_b"][0]),
        "x_b": by_partition(a["lru_x_b"][0]), "lam": by_partition(a["lru_lambda"][0]),
        "g_mem": by_partition(a["mem_norm"][0]),
        "g_heads": np.concatenate([twice(a[n][0]) for n in ("moba_q_norm", "moba_k_norm", "mem_q_norm", "mem_k_norm")], axis=1)})
    pre, post, l_params = [a["ffn1_norm"][0], a["mix_norm"][0], a["ffn2_norm"][0]], [], []
    s = []
    w = a["w_in"][0]
    s += ffn_units(a["ffn1_w_in"][0], a["ffn1_w_out"][0])
    s += rows_units(a["mem_w_kv"][0])
    s += channel_units(w[:, 0:512])
    s += rows_units(w[:, 1024:1536])
    s += rows_units(w[:, 1536:2048])
    s += channel_units(w[:, 512:1024])
    s += output_units(a["w_out"][0])
    s += ffn_units(a["ffn2_w_in"][0], a["ffn2_w_out"][0])
    for l in range(LAYERS):
        b = {name[:-2]: a[name][l] for name in a if name.endswith("_2") and name not in ("mem_2", "positions_2")}
        w = b["w_mix_in"]
        k_w2 = b["cmp_k_w2"].reshape(2, P, HD).transpose(1, 0, 2)
        l_params.append(pack(LP, LP_N, {
            "gate_w": w[:, 2816:2840].reshape(KD, P, GATES).transpose(1, 0, 2),
            "k_w2": np.concatenate([k_w2, k_w2], axis=2),
            "v_w2": b["cmp_v_w2"].reshape(2, P, HD).transpose(1, 0, 2),
            "k_b1": by_partition(b["cmp_k_b1"]), "v_b1": by_partition(b["cmp_v_b1"]),
            "pos_k": by_partition(b["cmp_pos_k"].reshape(-1)), "pos_v": by_partition(b["cmp_pos_v"].reshape(-1)),
            "conv_w": b["conv_w"].reshape(CONV2_W, 4, P).transpose(2, 1, 0), "g_mem": by_partition(b["mem_norm"])}))
        pre += [b[f"{n}_norm_pre"] for n in ("ffn1", "mix", "ffn2")]
        post += [b[f"{n}_norm_post"] for n in ("ffn1", "mix", "ffn2")]
        s += ffn_units(b["ffn1_w_in"], b["ffn1_w_out"])
        s += channel_units(b["w_mem_kv"][:, 0:512]) + rows_units(b["w_mem_kv"][:, 512:1024])
        s += channel_units(w[:, 0:1536]) + channel_units(w[:, 2048:2304])
        s += rows_units(w[:, 1536:2048]) + rows_units(w[:, 2304:2816])
        s += channel_units(w[:, 2840:3352])
        m, k, v = channel_units(w[:, 3352:6424]), channel_units(b["cmp_k_w1"]), channel_units(b["cmp_v_w1"])
        s += [m[0], *k, m[1], v[0], m[2], v[1], *m[3:]]
        for name in ("conv", "mem", "nsa"):
            s += channel_units(b[f"w_branch_{name}"])
        s += output_units(b["w_mix_out"])
        s += ffn_units(b["ffn2_w_in"], b["ffn2_w_out"])
    assert len(s) == WEIGHTS
    const, alibi = constants()
    return {"stream": np.stack(s), "b1_params": b1_params, "l_params": np.stack(l_params), "pre": np.stack(pre),
            "post": np.stack(post), "x": a["x"][0], "mem1": a["mem"][0], "mem2": a["mem_2"][0],
            "positions": np.ascontiguousarray(a["positions_2"][0].reshape(TT, P).T), "const": const, "alibi": alibi}


def kernel(**inputs):
    import concourse.bacc as bacc
    from concourse.bass_utils import run_bass_kernel_spmd as run

    arrays = lay_out({name: np.asarray(value) for name, value in inputs.items()})
    nc = bacc.Bacc("TRN2", target_bir_lowering=False, num_devices=1)
    ins = [nc.dram_tensor(name, a.shape, mybir.dt.from_np(a.dtype), kind="ExternalInput").ap() for name, a in arrays.items()]
    out = nc.dram_tensor("out", (T, D), F32, kind="ExternalOutput").ap()
    build(nc, *ins, out)
    result = run(nc, [arrays], core_ids=[0])
    return result.results[0]["out"].reshape(1, T, D)
```

```python
from contextlib import ExitStack

import numpy as np

import concourse.bass as bass
from concourse import mybir

F32 = mybir.dt.float32
F32R = mybir.dt.float32r
I32 = mybir.dt.int32
ALU = mybir.AluOpType
ACT = mybir.ActivationFunctionType
AX_X = mybir.AxisListType.X

P = 128
T = 256
TT = T // P
D = 1024
KD = D // P
D_FF = 2816
LAYERS = 2
ROOT_D = 32.0
assert ROOT_D ** 2 == D
EPS = 1e-6
NEG = -1e30
BIG = 3e38
HD = 64
MEM_HD = 128
LRU_TILES = 4
LRU_C = 8.0
CONV_W = 4
CONV2_W = 3
CMP_BLOCK, CMP_STRIDE = 32, 16
N_CMP = T // CMP_STRIDE - 1
CMP_HIDDEN = 256
CMP_PAIRS = CMP_BLOCK // 2
GROUPS = 2
NSA_HEADS = 8
GATES = 3 * NSA_HEADS
ROT = 8
ROPE_THETA = 500000.0

UNIT = 2048
RING = 3
CHUNK = 256
CHUNKS = D_FF // CHUNK
FFN_UNITS = 3 * CHUNKS
B1_PARAM, B1_FFN1 = 0, 1
B1_MEM = B1_FFN1 + FFN_UNITS
B1_LRU_X, B1_QK, B1_VC, B1_LRU_G, B1_OUT = B1_MEM + 2, B1_MEM + 4, B1_MEM + 6, B1_MEM + 8, B1_MEM + 10
B1_FFN2 = B1_OUT + 4
B1_UNITS = B1_FFN2 + FFN_UNITS
L_PARAM, L_GAIN, L_FFN1 = 0, 1, 2
L_MEM = L_FFN1 + FFN_UNITS
L_CONV = L_MEM + 4
L_KV, L_Q, L_KVS, L_QMEM, L_STEPS = L_CONV + 6, L_CONV + 7, L_CONV + 9, L_CONV + 11, L_CONV + 13
L_MERGE = [L_STEPS + k for k in (0, 3, 6, 7)] + [L_STEPS + k for k in range(8, 16)]
L_CMP = (L_STEPS + 1, L_STEPS + 4)
L_BR = L_STEPS + 16
L_OUT = L_BR + 6
L_FFN2 = L_OUT + 4
L_UNITS = L_FFN2 + FFN_UNITS
assert B1_UNITS % RING == 0 and L_UNITS % RING == 0
UNITS = B1_UNITS + LAYERS * L_UNITS
WEIGHTS = UNITS - 1 - 2 * LAYERS

F1_MEM, F1_LRU_X, F1_QK, F1_VC, F1_GATE, F1_FILLS = 0, 2, 4, 6, 8, 18
F1_LRU_G = (16, 17)
F1_HEADS = {"q": 12, "k": 13, "mem_k": 14, "mem_q": 15}
F_MEMK, F_MEMV, F_CONV, F_KV, F_GATE, F_Q, F_GATE_T, F_KVS, F_QMEM, F_PLAIN = 0, 2, 4, 10, 11, 12, 14, 15, (17, 20), 18
F_MERGE = [21, 24, 29, 32] + list(range(34, 42))
F_CMP, F_HID, F_ROT, F_KCVC, F_FILLS = (22, 27), (26, 31), (23, 25, 28, 30), 33, 42
assert F1_FILLS % 3 == 0 and F_FILLS % 3 == 0
S1_GATE, S1_SMALL = 0, 8
S1_HEADS = {"q": 4, "k": 5, "mem_k": 6, "mem_q": 7}
S_GATE, S_GATE_T, S_PLAIN, S_ROT, S_HID, S_KCVC, S_SMALL = 0, 1, 2, (4, 5, 7, 8), (6, 9), 10, 11
STEP_WORK = {0: (("cmp", 0),),
             1: (("rot", 0), ("merge", 1), ("rot", 1), ("hid", 0)),
             2: (("cmp", 1), ("rot", 2), ("merge", 2), ("rot", 3)),
             3: (("hid", 1), ("merge", 3)),
             4: (("kcvc", 0),)}
HEADS = {"q": 0, "k": 1, "mem_q": 2, "mem_k": 3}
FIRST_NSA = 4
CONV_STEP = 6
CONV_FREE = 8


def merge_part(n):
    h, b = divmod(n - FIRST_NSA, 3)
    cuts = (0, 6, 11, 2 * KD)
    return (4 + h, cuts[b], cuts[b + 1]) if n >= FIRST_NSA else None


BRANCHES = (0, 2, 1)

B1P, LP = {}, {}


def columns(table, widths):
    at = 0
    for name, width in widths:
        table[name] = (at, width)
        at += width
    return at


B1P_N = columns(B1P, [("a_w", 512), ("x_w", 512), ("conv_w", 16), ("conv_b", 4), ("a_b", 4), ("x_b", 4),
                      ("lam", 4), ("g_mem", 8), ("g_heads", 4)])
LP_N = columns(LP, [("gate_w", KD * GATES), ("k_w2", 256), ("v_w2", 128), ("k_b1", 2), ("v_b1", 2),
                    ("pos_k", 16), ("pos_v", 16), ("conv_w", 12), ("g_mem", 8)])
CONST = {}
CONST_N = columns(CONST, [("ident", P), ("causal", 384), ("zero", 1), ("cmp_mask", TT * 16),
                          ("cmp_valid", TT), ("inv_freq", ROT)])
ALIBI_N = 4 * 384


class Section:

    def __init__(self, layer=None):
        self.layer = layer

    def at(self, first, per_layer, k):
        return k if self.layer is None else self.layer * per_layer + (first + k)

    def unit(self, n):
        return self.at(B1_UNITS, L_UNITS, n)

    def landed(self, n):
        return self.at(16 * B1_UNITS // RING, 16 * L_UNITS // RING, 16 * (n // RING + 1))

    def small(self, f):
        return self.at(S1_SMALL, S_SMALL, f)

    def fill(self, f):
        return self.at(F1_FILLS, F_FILLS, f)


def wait(eng, sem, value):
    if not isinstance(value, int) or value > 0:
        eng.wait_ge(sem, value)


class Steps:

    def __init__(self, eng, sem, first, per_layer):
        self.eng, self.sem, self.totals = eng, sem, (first, per_layer)

    def enter(self, sec):
        self.sec, self.n = sec, 0

    def mark(self, ins):
        ins.then_inc(self.sem, 1)
        self.n += 1
        return self.sec.at(*self.totals, self.n)

    def after(self, value):
        self.eng.wait_ge(self.sem, value)

    def link(self, ins):
        self.after(self.mark(ins))

    def leave(self):
        want = self.totals[0 if self.sec.layer is None else 1]
        assert self.n == want, (self.n, self.totals)


class Job:

    def __init__(self, q, k, v, bias, scale, keys, causal, m, row, tile, first, last, factor=None):
        self.q, self.k, self.v, self.bias, self.scale = q, k, v, bias, scale
        self.keys, self.causal, self.m, self.row = keys, causal, m, row
        self.tile, self.first, self.last, self.factor = tile, first, last, factor
        self.key_tiles = -(-keys // P)
        self.tile_done = last and (m == P or row > 0)

    def width(self, i):
        return min(self.keys, P * (i + 1)) if self.causal else self.keys

    def rows(self, kt):
        return min(P, self.keys - P * kt)

    def span(self, kt):
        return P * kt if self.causal else 0

    def blocks(self):
        return [(kt, i, T * kt + P * i - self.span(kt))
                for kt in range(self.key_tiles) for i in range(TT) if P * i >= self.span(kt)]

    def pt_width(self):
        return T * self.key_tiles - sum(self.span(kt) for kt in range(self.key_tiles))


def build(nc, stream, b1_params, l_params, pre_in, post_in, x_in, mem1_in, mem2_in, pos_in, const_in, alibi_in, out):
    with ExitStack() as ctx:
        plan = {"at": -(-nc.sbuf_base // 64) * 64}

        def room(size):
            start = plan["at"]
            plan["at"] += -(-size // 32) * 32
            assert plan["at"] <= nc.sbuf_usable_end, plan["at"]
            return start

        def place(name, shape, start, dtype=F32):
            return nc.alloc_sbuf_tensor_at(name, shape, dtype, offset=start).ap()

        def new(name, shape, dtype=F32):
            return place(name, shape, room(4 * int(np.prod(shape[1:]))), dtype)

        raw = new("raw", [P, RING, UNIT])
        hi = new("hi", [P, RING, UNIT], F32R)
        lo = new("lo", [P, RING, UNIT], F32R)
        x = new("x", [P, TT, D])
        r_scaled = room(8192)
        xs = place("xs", [P, TT, D], r_scaled)
        heads1 = place("heads1", [P, TT, 16, HD], r_scaled)
        rot = place("rot", [P, TT, 16, HD], r_scaled)
        xT_hi = new("xT_hi", [P, KD, T], F32R)
        xT_lo = new("xT_lo", [P, KD, T], F32R)
        params = new("params", [P, max(B1P_N, LP_N)])
        pre = new("pre", [P, D])
        post = new("post", [P, D])
        r_memk = room(4096)
        memkT = place("memkT", [P, 4, T], r_memk)
        lru_y = place("lru_y", [P, LRU_TILES, T], r_memk)
        memv = new("memv", [P, TT, 512])
        r_big = room(24576)
        mem_in = place("mem_in", [P, TT, D], r_big)
        memT_hi = place("memT_hi", [P, KD, T], r_big + 8192, F32R)
        memT_lo = place("memT_lo", [P, KD, T], r_big + 16384, F32R)
        lru_in = place("lru_in", [P, LRU_TILES, T + CONV_W - 1], r_big)
        lru_xb = place("lru_xb", [P, LRU_TILES, T], r_big + 4160)
        lru_r = place("lru_r", [P, LRU_TILES, T], r_big + 4160 + 4096)
        lru_i = place("lru_i", [P, LRU_TILES, T], r_big + 4160 + 2 * 4096)
        lru_m = place("lru_m", [P, LRU_TILES, T], r_big)
        lru_a = place("lru_a", [P, LRU_TILES, T], r_big + 4160 + 3 * 4096)
        conv_in = place("conv_in", [P, 3 * 4 * T], r_big)
        conv_v = place("conv_v", [P, 4, T + CONV2_W - 1], r_big + 12288)
        conv_y = place("conv_y", [P, 4, T], r_big + 12288 + 4160)
        merge = place("merge", [P, 3 * KD * T], r_big)
        merged_hi = place("merged_hi", [P, KD, T], r_big, F32R)
        merged_lo = place("merged_lo", [P, KD, T], r_big + 8192, F32R)
        r_mix = room(24576)
        mix_hi = place("mix_hi", [P, KD, T], r_mix, F32R)
        mix_lo = place("mix_lo", [P, KD, T], r_mix + 8192, F32R)
        alibi = place("alibi", [P, 4, 384], r_mix + 16384)
        br_hi = [place(f"br_hi{b}", [P, 4, T], r_mix + 8192 * (2 - b), F32R) for b in range(3)]
        br_lo = [place(f"br_lo{b}", [P, 4, T], r_mix + 8192 * (2 - b) + 4096, F32R) for b in range(3)]
        cmp_src = [place(f"cmp_src{c}", [P, GROUPS, T], r_mix + 8192 + 2048 * c) for c in range(2)]
        n_cmp = CMP_PAIRS * GROUPS * N_CMP * 4
        cmp_x = [place(f"cmp_x{c}", [P, CMP_PAIRS, GROUPS, N_CMP], r_mix + 12288 + 3 * n_cmp * c)
                 for c in range(2)]
        cmp_hi = [place(f"cmp_hi{c}", [P, CMP_PAIRS, GROUPS * N_CMP], r_mix + 12288 + 3 * n_cmp * c + n_cmp,
                        F32R) for c in range(2)]
        cmp_lo = [place(f"cmp_lo{c}", [P, CMP_PAIRS, GROUPS * N_CMP],
                        r_mix + 12288 + 3 * n_cmp * c + 2 * n_cmp, F32R) for c in range(2)]
        r_qT = room(4096)
        qT = place("qT", [P, 4, T], r_qT)
        lru_g = place("lru_g", [P, LRU_TILES, T], r_qT)
        hT_hi = place("hT_hi", [P, 2, T], r_qT, F32R)
        hT_lo = place("hT_lo", [P, 2, T], r_qT + 2048, F32R)
        r_headT = room(8192)
        headT = place("headT", [P, 8, T], r_headT)
        squared = [place(f"squared{i}", [P, D], at) for i, at in enumerate((r_headT + 4096, r_qT))]
        diag = place("diag", [P, TT, P], r_headT)
        merged = place("merged", [P, KD, T], r_headT)
        qmemT = new("qmemT", [P, 4, T])
        v_sb = new("v_sb", [P, TT, 2, P])
        r_prob = room(4096)
        prob = place("prob", [P, 2, TT, T], r_prob)
        silu_a = place("silu_a", [P, 2 * T], r_prob)
        h_sb = place("h_sb", [P, 2 * T], r_prob + 2048)
        rope_t = place("rope_t", [P, 4, TT, 16, ROT], r_prob)
        br_t = place("br_t", [P, 2, 512], r_prob)
        r_pT = room(4096)
        squares = place("squares", [P, TT, 16, HD], r_prob)
        probT = place("probT", [P, 2, 512], r_pT)
        q_sb = place("q_sb", [P, TT, 512], r_pT)
        hT_last = [place(f"hT_last_{part}", [P, 2, T], r_pT + 2048 * n, F32R) for n, part in enumerate(("hi", "lo"))]
        const = new("const", [P, CONST_N])
        gw_hi = place("gw_hi", [P, KD, GATES], r_pT, F32R)
        gw_lo = place("gw_lo", [P, KD, GATES], r_pT + 4 * KD * GATES, F32R)
        cmp_rows_at = plan["at"]
        cmp_rows = [new(f"cmp_rows{c}", [GROUPS * N_CMP, CMP_HIDDEN]) for c in range(2)]
        gate_rows = place("gate_rows", [GATES, T], cmp_rows_at)
        hid = [new(f"hid{c}", [P, 2, GROUPS * N_CMP]) for c in range(2)]
        kcT = new("kcT", [P, GROUPS * N_CMP])
        vc = new("vc", [P, GROUPS, HD])
        gates = new("gates", [P, TT, GATES])
        pos_i = new("pos_i", [P, TT], I32)
        angle = new("angle", [P, 6, TT * ROT])
        trig = new("trig", [P, 2, TT, ROT])
        sums = new("sums", [P, 32])
        var = new("var", [P, 32])
        rstd = new("rstd", [P, 32])
        ysums = new("ysums", [P, 2 * TT])
        neg_half = new("neg_half", [P, 32])
        minus_one = new("minus_one", [P, LRU_TILES])
        soft = new("soft", [P, 2, 3, TT])
        lam_t = new("lam_t", [P, 7, LRU_TILES])

        def cst(name):
            at, n = CONST[name]
            return const[:, at:at + n]

        def b1p(name):
            at, n = B1P[name]
            return params[:, at:at + n]

        def lp(name):
            at, n = LP[name]
            return params[:, at:at + n]

        ident = cst("ident")
        causal = cst("causal")
        cmp_mask = cst("cmp_mask").rearrange("p (i n) -> p i n", i=TT)

        def psum(name):
            return ctx.enter_context(nc.psum_tensor(name, [P, 4, 512], F32))

        acc = psum("acc")
        work = psum("work")

        def sem(name):
            return ctx.enter_context(nc.semaphore(name))

        landed = [sem(f"landed{s}") for s in range(RING)]
        hi_ready, lo_ready, unit_used = sem("hi_ready"), sem("lo_ready"), sem("unit_used")
        ident_loaded, x_loaded, mem_loaded = sem("ident_loaded"), [sem(f"x_loaded{i}") for i in range(TT)], sem("mem_loaded")
        tables_loaded, half_set = sem("tables_loaded"), sem("half_set")
        sq_ready, pow_asked, pow_ready = sem("sq_ready"), sem("pow_asked"), sem("pow_ready")
        xs_ready, xT_ready = sem("xs_ready"), sem("xT_ready")
        xhi_ready, xlo_ready = sem("xhi_ready"), sem("xlo_ready")
        pre_loaded, post_loaded = sem("pre_loaded"), sem("post_loaded")
        silu_ready, h_ready = sem("silu_ready"), sem("h_ready")
        hThi_ready, hTlo_ready = sem("hThi_ready"), sem("hTlo_ready")
        sum0_ready, sum1_ready = sem("sum0_ready"), sem("sum1_ready")
        ysq_ready, x_ready = sem("ysq_ready"), sem("x_ready")
        small_ready, evac_done = sem("small_ready"), sem("evac_done")
        qk_ready, scored, exp_ready, p_ready = sem("qk_ready"), sem("scored"), sem("exp_ready"), sem("p_ready")
        pT_ready, pT_copied = sem("pT_ready"), sem("pT_copied")
        tile_ready, tile_hi, tile_lo = sem("tile_ready"), sem("tile_hi"), sem("tile_lo")
        trig_asked, trig_ready = sem("trig_asked"), sem("trig_ready")
        dve_step, pool_step = sem("dve_step"), sem("pool_step")
        heads_ready, lam_asked, lam_exp, lam_ready = (sem("heads_ready"), sem("lam_asked"), sem("lam_exp"),
                                                      sem("lam_ready"))
        xb_ready, lru_a_ready, m2_ready, mult_ready, lruy_ready, lruhi_ready = (
            sem("xb_ready"), sem("lru_a_ready"), sem("m2_ready"), sem("mult_ready"), sem("lruy_ready"),
            sem("lruhi_ready"))
        lrulo_ready, gelu_ready = sem("lrulo_ready"), sem("gelu_ready")
        gwhi_ready, gwlo_ready = sem("gwhi_ready"), sem("gwlo_ready")
        hi_piece = sem("hi_piece")
        conv_ready, convhi_ready, convlo_ready = sem("conv_ready"), sem("convhi_ready"), sem("convlo_ready")
        rot_ready, cmpx_ready, cmphi_ready, cmplo_ready = (sem("rot_ready"), sem("cmpx_ready"),
                                                           sem("cmphi_ready"), sem("cmplo_ready"))
        br_half, gate_ready = sem("br_half"), sem("gate_ready")
        br_read, merged_ready = sem("br_read"), sem("merged_ready")
        mhi_ready, mlo_ready = sem("mhi_ready"), sem("mlo_ready")
        stored = sem("stored")

        block = ctx.enter_context(nc.Block())

        POWS = (10, 13)
        JOBS = (8, 28)
        TILES = (4, 8)
        PIECES = (6, 2 * NSA_HEADS)

        def jobs_of(sec):
            if sec.layer is None:
                def head(kind, h):
                    return headT[HD * (h % 2):HD * (h % 2) + HD, 2 * kind + h // 2, :]

                made = []
                for h in range(4):
                    made.append(Job(
                        q=lambda i, h=h: head(0, h)[:, P * i:P * i + P], k=lambda n, h=h: head(1, h)[:, 0:n],
                        v=lambda kt, h=h: v_sb[:, kt, h // 2, HD * (h % 2):HD * (h % 2) + HD],
                        bias=lambda i, n, h=h: alibi[:, h, P * i:P * i + n], scale=HD ** -0.5, keys=T,
                        causal=True, m=HD, row=HD * (h % 2), tile=h // 2, first=True, last=True))
                for h in range(4):
                    made.append(Job(
                        q=lambda i, h=h: head(2, h)[:, P * i:P * i + P], k=lambda n, h=h: head(3, h)[:, 0:n],
                        v=lambda kt, h=h: memv[:, kt, T + HD * h:T + HD * h + HD],
                        bias=lambda i, n: cst("zero").to_broadcast([P, n]), scale=HD ** -0.5, keys=T,
                        causal=False, m=HD, row=HD * (h % 2), tile=2 + h // 2, first=True, last=True))
                return made
            made = []
            for h in range(4):
                made.append(Job(
                    q=lambda i, h=h: qmemT[:, h, P * i:P * i + P], k=lambda n, h=h: memkT[:, h, 0:n],
                    v=lambda kt, h=h: memv[:, kt, MEM_HD * h:MEM_HD * h + MEM_HD],
                    bias=lambda i, n: cst("zero").to_broadcast([P, n]), scale=MEM_HD ** -0.5, keys=T, causal=False,
                    m=MEM_HD, row=0, tile=h, first=True, last=True))
            for h in range(NSA_HEADS):
                g, pair, row = h // (NSA_HEADS // GROUPS), h // 2, HD * (h % 2)
                rows = slice(row, row + HD)
                common = dict(scale=HD ** -0.5, m=HD, row=row, tile=4 + pair)
                for s in range(2):
                    made.append(Job(
                        q=lambda i, rows=rows, pair=pair: headT[rows, pair, P * i:P * i + P],
                        k=lambda n, rows=rows, g=g, s=s: headT[rows, 4 + 2 * s + g, 0:n],
                        v=lambda kt, g=g, s=s: v_sb[:, kt, s, HD * g:HD * g + HD],
                        bias=lambda i, n: causal[:, P * i:P * i + n], keys=T, causal=True,
                        first=s == 0, last=False,
                        factor=lambda i, h=h, s=s: gates[:, i, 3 * h + 1 + s:3 * h + 2 + s], **common))
                made.append(Job(
                    q=lambda i, rows=rows, pair=pair: qT[rows, pair, P * i:P * i + P],
                    k=lambda n, rows=rows, g=g: kcT[rows, N_CMP * g:N_CMP * g + n],
                    v=lambda kt, g=g: vc[0:N_CMP, g, :], bias=lambda i, n: cmp_mask[:, i, 0:n], keys=N_CMP,
                    causal=False, first=False, last=True,
                    factor=lambda i, h=h: gates[:, i, 3 * h:3 * h + 1], **common))
            return made

        def tile_bank(t):
            return (acc, work)[t % 2][:, 3, 0:T]

        def tile_dst(sec, t):
            if sec.layer is None:
                return mix_hi[:, 4 + t, :], mix_lo[:, 4 + t, :]
            b = 2 if t < 4 else 1
            return br_hi[b][:, t % 4, :], br_lo[b][:, t % 4, :]

        def head_sums(tile, first, n):
            return tile.rearrange("p (i h) -> p i h", i=TT)[:, :, first:first + n]

        def sums_ready(eng, sec, r, n, i, c):
            if i == 0:
                eng.wait_ge(sum0_ready, sec.at(3, 3, r + 1))
            elif c == 1:
                eng.wait_ge(unit_used, sec.unit(n + 1))
            elif r == 1:
                eng.wait_ge(unit_used, sec.unit(n))
            else:
                eng.wait_ge(sum1_ready, sec.at(2, 2, r // 2 + 1))

        def cols(c):
            return slice(512 * c, 512 * c + 512)

        def x_norm_at(k):
            return {0: 0, 2: 4, 3: 6}[k]

        def rows_bank(i, b):
            return acc[:, 2 * i + b, :].rearrange("p (k t) -> p k t", k=4)

        def rows_operand(part, i, b):
            return part[:, 4 * b:4 * b + 4, P * i:P * i + P]

        def br_bank(w, k):
            if (w, k) == (1, 1):
                return acc[:, 0, :]
            return work[:, 2 * (w % 2) + k, :]

        @block.sync
        def _(sp):
            def load(sec, n, at, trip=0, static=False):
                wait(sp, lo_ready, sec.unit(n - RING + 1) + trip * RING)
                sp.dma_start(raw[:, n % RING, :], stream[at]).then_inc(landed[n % RING], 16)

            sec = Section()
            for i in range(TT):
                sp.dma_start(x[:, i, :], x_in[P * i:P * i + P, :]).then_inc(x_loaded[i], 16)
            load(sec, 1, 0)
            sp.dma_start(params[:, 0:B1P_N], b1_params).then_inc(landed[0], 16)
            load(sec, 2, 1)
            with sp.Fori(1, B1_UNITS // RING) as turn:
                for s in range(RING):
                    load(sec, s, turn * RING + (s - 1), turn)
            with sp.Fori(0, LAYERS) as layer:
                sec = Section(layer)
                first = layer * (L_UNITS - L_FFN1) + (B1_UNITS - 1 - L_FFN1)
                sp.wait_ge(lo_ready, sec.unit(L_PARAM - RING + 1))
                sp.dma_start(params[:, 0:LP_N], l_params[bass.ds(layer, 1)].rearrange("l p n -> p (l n)")).then_inc(landed[L_PARAM], 16)
                sp.wait_ge(lo_ready, sec.unit(L_GAIN - RING + 1))
                sp.dma_start(pre, pre_in[bass.ds(layer * 3 + 3, 1)].to_broadcast([P, D])).then_inc(landed[L_GAIN], 16)
                load(sec, L_FFN1, first + L_FFN1)
                with sp.Fori(1, L_UNITS // RING) as turn:
                    for s in range(RING):
                        load(sec, s, first + turn * RING + s, turn)
            for i in range(TT):
                for c in range(2):
                    sp.wait_ge(x_ready, 12 * (1 + LAYERS) - 3 + 2 * i + c)
                    sp.dma_start(out[P * i:P * i + P, cols(c)], x[:, i, cols(c)]).then_inc(stored, 16)
            sp.wait_ge(stored, 64)

        @block.gpsimd
        def _(pool):
            nc.gpsimd.memset(neg_half, -0.5).then_inc(half_set, 1)
            nc.gpsimd.memset(minus_one, -1.0).then_inc(half_set, 1)
            pool.wait_ge(half_set, 2)

            def root(sec, k, place):
                pool.wait_ge(pow_asked, sec.at(*POWS, k + 1))
                nc.gpsimd.tensor_tensor(place(rstd), place(var), place(neg_half), ALU.pow).then_inc(pow_ready, 1)

            def columns(c, n=1):
                return lambda tile: tile[:, c:c + n]

            def head_columns(first, n):
                return lambda tile: head_sums(tile, first, n)

            step = Steps(pool, pool_step, POOL_STEPS, 0)
            sec = Section()
            step.enter(sec)
            x_norm, post_norm, mem_norm = [columns(0), columns(1)], [columns(2), columns(3)], [columns(4, TT)]
            for k in range(2):
                root(sec, k, x_norm[k])
            root(sec, 2, mem_norm[0])
            for k in range(2):
                root(sec, 3 + k, x_norm[k])
            pool.wait_ge(lam_exp, 1)
            step.link(nc.gpsimd.tensor_scalar(lam_t[:, 3, :], lam_t[:, 1, :], 2.0, None, ALU.add))
            step.link(nc.gpsimd.tensor_tensor(lam_t[:, 3, :], lam_t[:, 3, :], minus_one, ALU.pow))
            step.link(nc.gpsimd.tensor_tensor(lam_t[:, 3, :], lam_t[:, 1, :], lam_t[:, 3, :], ALU.mult))
            step.link(nc.gpsimd.tensor_tensor(lam_t[:, 4, :], lam_t[:, 3, :], lam_t[:, 3, :], ALU.mult))
            step.link(nc.gpsimd.tensor_scalar(lam_t[:, 5, :], lam_t[:, 4, :], 1.0 / 17, None, ALU.mult))
            for odd in (15, 13, 11, 9, 7, 5, 3):
                step.link(nc.gpsimd.tensor_scalar(lam_t[:, 5, :], lam_t[:, 5, :], 1.0 / odd, None, ALU.add))
                step.link(nc.gpsimd.tensor_tensor(lam_t[:, 5, :], lam_t[:, 5, :], lam_t[:, 4, :], ALU.mult))
            step.link(nc.gpsimd.tensor_scalar(lam_t[:, 5, :], lam_t[:, 5, :], 1.0, 2.0, ALU.add, ALU.mult))
            step.link(nc.gpsimd.tensor_tensor(lam_t[:, 5, :], lam_t[:, 5, :], lam_t[:, 3, :], ALU.mult))
            step.link(nc.gpsimd.tensor_tensor(lam_t[:, 2, :], lam_t[:, 5, :], lam_t[:, 2, :], ALU.add))
            step.link(nc.gpsimd.tensor_scalar(lam_t[:, 5, :], lam_t[:, 2, :], -LRU_C, None, ALU.mult))
            nc.gpsimd.tensor_scalar(lam_t[:, 6, :], lam_t[:, 2, :], LRU_C, None, ALU.mult).then_inc(lam_ready, 1)
            step.leave()
            for k, place in enumerate((head_columns(12, 4), head_columns(0, 8), head_columns(8, 4))):
                root(sec, 5 + k, place)
            for k in range(2):
                root(sec, 8 + k, x_norm[k])
            with pool.Fori(0, LAYERS) as layer:
                for k, place in enumerate(x_norm + mem_norm + 2 * [post_norm[0], x_norm[0], post_norm[1], x_norm[1]] + post_norm):
                    root(Section(layer), k, place)

        @block.scalar
        def _(act):
            def split_high(sec, n, trip=0):
                s = n % RING
                wait(act, unit_used, sec.unit(n - RING + 1) + trip * RING)
                act.wait_ge(landed[s], sec.landed(n) + trip * 16)
                nc.scalar.activation(hi[:, s, :], raw[:, s, :], ACT.Copy).then_inc(hi_ready, 1)

            def high_piece(sec, n, begin, end):
                s = n % RING
                if begin == 0:
                    act.wait_ge(unit_used, sec.unit(n - RING + 1))
                    act.wait_ge(landed[s], sec.landed(n))
                nc.scalar.activation(hi[:, s, begin:end], raw[:, s, begin:end], ACT.Copy).then_inc(hi_ready if end == UNIT else hi_piece, 1)

            def load_pre(sec, r):
                row = r if sec.layer is None else sec.layer * 3 + (3 + r)
                act.dma_start(pre, pre_in[bass.ds(row, 1)].to_broadcast([P, D])).then_inc(pre_loaded, 16)

            def load_post(sec, r):
                act.dma_start(post, post_in[bass.ds(sec.layer * 3 + r, 1)].to_broadcast([P, D])).then_inc(post_loaded, 16)

            def x_half_squares(i, c):
                nc.scalar.activation(squared[i][:, cols(c)], x[:, i, cols(c)], ACT.Square,
                                     accum_out=sums[:, 2 * i + c:2 * i + c + 1]).then_inc(sq_ready, 1)

            def x_squares(sec, r, i):
                for c in range(2):
                    act.wait_ge(x_ready, sec.at(12, 12, 4 * r + 2 * i + c + 1))
                    x_half_squares(i, c)

            def x_high(sec, k):
                for i in range(TT):
                    for b in range(2):
                        act.wait_ge(xT_ready, sec.at(16, 16, 4 * k + 2 * i + b + 1))
                        nc.scalar.activation(rows_operand(xT_hi, i, b), rows_bank(i, b), ACT.Copy).then_inc(xhi_ready, 1)

            def mem_high(sec, r, gain):
                act.wait_ge(xT_ready, sec.at(16, 16, 4 + r + 1))
                for c in range(2):
                    kt = 2 * r + c
                    ins = nc.scalar.activation(memT_hi[:, kt, :], work[:, 2 + r % 2, T * c:T * c + T], ACT.Copy,
                                               scale=gain[:, kt:kt + 1])
                ins.then_inc(xhi_ready, 1)

            def ffn(sec, u0, k, begin=None, mem_gain=None, more=True):
                c0 = sec.at(2 * CHUNKS, 2 * CHUNKS, k * CHUNKS)

                def silu(j, n, trip=0):
                    act.wait_ge(unit_used, sec.unit(n + 1) + trip * RING)
                    wait(act, h_ready, c0 + j)
                    nc.scalar.activation(silu_a, work[:, 0, :], ACT.Silu).then_inc(silu_ready, 1)

                def high_h(j, n, trip=0):
                    act.wait_ge(h_ready, c0 + j + 1)
                    if n is not None:
                        act.wait_ge(unit_used, sec.unit(n + 1) + trip * RING)
                    nc.scalar.activation(hT_hi.rearrange("p f t -> p (f t)"), h_sb, ACT.Copy).then_inc(hThi_ready, 1)

                split_high(sec, u0 + 2)
                silu(0, u0)
                split_high(sec, u0 + 3)
                high_h(0, None)
                split_high(sec, u0 + 4)
                if begin:
                    begin()
                with act.Fori(1, CHUNKS - 1) as j:
                    silu(j, u0 - 1, j)
                    split_high(sec, u0 + 2, j)
                    split_high(sec, u0 + 3, j)
                    high_h(j, u0 + 1, j)
                    split_high(sec, u0 + 4, j)
                last = CHUNKS - 1
                silu(last, u0 - 1 + 3 * last)
                split_high(sec, u0 + 2 + 3 * last)
                if mem_gain is not None:
                    mem_high(sec, 0, mem_gain)
                    mem_high(sec, 1, mem_gain)
                act.wait_ge(h_ready, c0 + last + 1)
                nc.scalar.activation(hT_last[0].rearrange("p f t -> p (f t)"), h_sb, ACT.Copy).then_inc(hThi_ready, 1)
                if more:
                    split_high(sec, u0 + FFN_UNITS)
                if mem_gain is not None:
                    mem_high(sec, 2, mem_gain)
                    mem_high(sec, 3, mem_gain)
                if more:
                    split_high(sec, u0 + FFN_UNITS + 1)

            def post_sums(sec, r, n, i):
                for c in range(2):
                    sums_ready(act, sec, r, n, i, c)
                    nc.scalar.activation(xs[:, i, cols(c)], acc[:, 2 * i + c, :], ACT.Square,
                                         accum_out=ysums[:, 2 * i + c:2 * i + c + 1]).then_inc(ysq_ready, 1)

            def by_unit(sec, f, n, trip=0):
                act.wait_ge(unit_used, sec.unit(n + 1) + trip * RING)
                return work[:, f % 3, :]

            def by_small(sec, f, k):
                act.wait_ge(small_ready, sec.small(k + 1))
                return work[:, f % 3, :]

            def copy_out(bank, dst, func=ACT.Copy):
                nc.scalar.activation(dst, bank, func).then_inc(evac_done, 1)

            def pair(tile, w):
                return tile[:, 2 * w:2 * w + 2, :].rearrange("p c t -> p (c t)")

            def exps(sec, n, job):
                for i in range(TT):
                    act.wait_ge(scored, sec.at(2 * JOBS[0], 2 * JOBS[1], 2 * n + i + 1))
                    p = prob[:, n % 2, i, 0:job.width(i)]
                    nc.scalar.activation(p, p, ACT.Exp, bias=soft[:, n % 2, 0, i:i + 1], scale=-1.0,
                                         accum_out=soft[:, n % 2, 1, i:i + 1]).then_inc(exp_ready, 1)

            def copy_pT(sec, n, job):
                act.wait_ge(pT_ready, sec.at(*JOBS, n + 1))
                r, w = job.rows(0), job.pt_width()
                nc.scalar.activation(probT[0:r, n % 2, 0:w], acc[0:r, 2, 0:w], ACT.Copy).then_inc(pT_copied, 1)

            def high_tile(sec, job):
                if job.tile_done:
                    act.wait_ge(tile_ready, sec.at(*TILES, job.tile + 1))
                    nc.scalar.activation(tile_dst(sec, job.tile)[0], tile_bank(job.tile), ACT.Copy).then_inc(tile_hi, 1)

            sec = Section()
            act.dma_start(ident, const_in[:, 0:P]).then_inc(ident_loaded, 16)
            load_pre(sec, 0)
            act.dma_start(const[:, P:CONST_N], const_in[:, P:CONST_N]).then_inc(tables_loaded, 16)
            act.dma_start(pos_i, pos_in).then_inc(tables_loaded, 16)
            act.dma_start(alibi.rearrange("p h n -> p (h n)"), alibi_in).then_inc(tables_loaded, 16)
            act.dma_start(mem_in, mem1_in.rearrange("(i p) d -> p i d", p=P)).then_inc(mem_loaded, 16)
            act.sem_inc(hi_ready, 1)
            act.wait_ge(half_set, 2)
            nc.scalar.activation(trig[:, 0, 0, :], neg_half[:, 0:ROT], ACT.Square)
            for i in range(TT):
                act.wait_ge(x_loaded[i], 16)
                for c in range(2):
                    x_half_squares(i, c)
            split_high(sec, B1_FFN1)
            x_high(sec, 0)
            split_high(sec, B1_FFN1 + 1)
            load_pre(sec, 1)

            def mem_squares(sec):
                act.wait_ge(mem_loaded, sec.at(16, 16, 16))
                for i in range(TT):
                    nc.scalar.activation(xs[:, i, :], mem_in[:, i, :], ACT.Square, accum_out=sums[:, i:i + 1]).then_inc(sq_ready, 1)

            ffn(sec, B1_FFN1, 0, lambda: mem_squares(sec), b1p("g_mem"))
            for i in range(TT):
                x_squares(sec, 0, i)
            split_high(sec, B1_MEM + 2)
            split_high(sec, B1_MEM + 3)
            x_high(sec, 2)
            load_pre(sec, 2)
            split_high(sec, B1_LRU_X + 2)
            for i in range(TT):
                copy_out(by_unit(sec, F1_MEM + i, B1_MEM + 1), memv[:, i, :])
            act.wait_ge(lam_asked, 2)
            nc.scalar.activation(lam_t[:, 1, :], lam_t[:, 0, :], ACT.Exp).then_inc(lam_exp, 1)
            for w in range(2):
                bank = by_unit(sec, F1_LRU_X + w, B1_LRU_X + w)
                nc.scalar.activation(lru_in[:, 2 * w:2 * w + 2, CONV_W - 1:], bank.rearrange("p (c t) -> p c t", c=2),
                                     ACT.Copy).then_inc(evac_done, 1)
                split_high(sec, B1_LRU_X + w + 3)
            split_high(sec, B1_QK + 3)
            for i in range(TT):
                copy_out(by_unit(sec, F1_QK + i, B1_QK + 1), heads1[:, i, 0:8, :].rearrange("p h d -> p (h d)"))
            split_high(sec, B1_VC + 2)
            split_high(sec, B1_VC + 3)
            for i in range(TT):
                bank = by_unit(sec, F1_VC + i, B1_VC + 1)
                nc.scalar.activation(v_sb[:, i, :, :].rearrange("p s n -> p (s n)"), bank[:, 0:T], ACT.Copy)
                nc.scalar.activation(heads1[:, i, 8:12, :].rearrange("p h d -> p (h d)"), bank[:, T:2 * T],
                                     ACT.Copy).then_inc(evac_done, 1)
            for w in range(4):
                bank = by_small(sec, F1_GATE + w, S1_GATE + w)
                dst, bias = (lru_r, b1p("a_b")) if w < 2 else (lru_i, b1p("x_b"))
                for c in range(2):
                    ct = 2 * (w % 2) + c
                    ins = nc.scalar.activation(dst[:, ct, :], bank[:, T * c:T * c + T], ACT.Sigmoid, bias=bias[:, ct:ct + 1])
                ins.then_inc(evac_done, 1)

            def head_out(name):
                kind = HEADS[name]
                nc.scalar.activation(pair(headT, kind), by_small(sec, F1_HEADS[name], S1_HEADS[name]), ACT.Copy,
                                     scale=b1p("g_heads")[:, kind:kind + 1]).then_inc(evac_done, 1)

            for name in ("q", "k", "mem_k"):
                head_out(name)
            act.wait_ge(lam_ready, 1)
            act.wait_ge(evac_done, F1_GATE + 2)
            jobs = jobs_of(sec)
            exps(sec, 0, jobs[0])
            for n, job in enumerate(jobs):
                if n + 1 < len(jobs):
                    exps(sec, n + 1, jobs[n + 1])
                if n == 0:
                    head_out("mem_q")
                if n < LRU_TILES:
                    nc.scalar.activation(lru_a[:, n, :], lru_r[:, n, :], ACT.Exp, scale=lam_t[:, 5, n:n + 1])
                    nc.scalar.activation(lru_m[:, n, :], lru_r[:, n, :], ACT.Tanh, scale=lam_t[:, 6, n:n + 1]).then_inc(lru_a_ready, 1)
                g, q = divmod(n, 4)
                if q == 3:
                    copy_out(by_unit(sec, F1_LRU_G[g], B1_LRU_G + g), pair(lru_g, g))
                copy_pT(sec, n, job)
                high_piece(sec, B1_OUT + g, UNIT // 4 * q, UNIT // 4 * (q + 1))
                if n:
                    high_tile(sec, jobs[n - 1])
            high_tile(sec, jobs[-1])
            split_high(sec, B1_OUT + 2)
            act.wait_ge(m2_ready, 1)
            nc.scalar.activation(lru_r, lru_m, ACT.Sqrt).then_inc(mult_ready, 1)
            act.wait_ge(evac_done, F1_FILLS)
            nc.scalar.activation(lru_g, lru_g, ACT.Gelu_apprx_tanh).then_inc(gelu_ready, 1)
            split_high(sec, B1_OUT + 3)
            act.wait_ge(lruy_ready, 1)
            nc.scalar.activation(mix_hi[:, 0:LRU_TILES, :], lru_y, ACT.Copy).then_inc(lruhi_ready, 1)
            split_high(sec, B1_OUT + 4)
            for i in range(TT):
                x_squares(sec, 1, i)
            x_high(sec, 3)
            split_high(sec, B1_FFN2 + 1)

            def angles():
                act.wait_ge(trig_asked, 1)
                nc.scalar.activation(trig.rearrange("p c i r -> p (c i r)"), angle[:, 4:6, :].rearrange("p c n -> p (c n)"),
                                     ACT.Sin).then_inc(trig_ready, 1)

            ffn(sec, B1_FFN2, 1, angles, more=False)

            with act.Fori(0, LAYERS) as layer:
                sec = Section(layer)
                act.dma_start(mem_in, mem2_in.rearrange("(i p) d -> p i d", p=P)).then_inc(mem_loaded, 16)
                act.wait_ge(hi_ready, sec.unit(0))
                act.sem_inc(hi_ready, L_FFN1)
                for i in range(TT):
                    x_squares(sec, -1, i)
                split_high(sec, L_FFN1)
                x_high(sec, 0)
                split_high(sec, L_FFN1 + 1)
                load_post(sec, 0)
                load_pre(sec, 1)
                ffn(sec, L_FFN1, 0, lambda: mem_squares(sec), lp("g_mem"))
                for i in range(TT):
                    post_sums(sec, 0, L_MEM - 1, i)
                    x_squares(sec, 0, i)
                split_high(sec, L_MEM + 2)
                load_post(sec, 1)
                split_high(sec, L_MEM + 3)
                copy_out(by_unit(sec, F_MEMK, L_MEM), pair(memkT, 0))
                nc.scalar.activation(gw_hi.rearrange("p k n -> p (k n)"), lp("gate_w"), ACT.Copy).then_inc(gwhi_ready, 1)
                split_high(sec, L_MEM + 4)
                copy_out(by_unit(sec, F_MEMK + 1, L_MEM + 1), pair(memkT, 1))
                x_high(sec, 2)
                load_pre(sec, 2)
                split_high(sec, L_MEM + 5)
                for i in range(TT):
                    copy_out(by_unit(sec, F_MEMV + i, L_MEM + 3), memv[:, i, :])
                with act.Fori(0, 2) as trip:
                    for w in range(3):
                        split_high(sec, L_CONV + w + 2, trip)
                        copy_out(by_unit(sec, F_CONV + w, L_CONV + w, trip), conv_in[:, bass.ds(trip * 1536 + 512 * w, 512)])
                split_high(sec, L_KV + 2)
                bank = by_unit(sec, F_KV, L_KV)
                for c in range(2):
                    for g in range(GROUPS):
                        part = bank[HD * g:HD * g + HD, T * c:T * c + T]
                        nc.scalar.activation(cmp_src[c][0:HD, g, :], part, ACT.Copy)
                        ins = nc.scalar.activation(cmp_src[c][HD:P, g, 0:T - 1], part[:, 1:T], ACT.Copy)
                ins.then_inc(evac_done, 1)
                copy_out(by_small(sec, F_GATE, S_GATE)[0:GATES, 0:T], gate_rows)
                split_high(sec, L_Q + 2)
                split_high(sec, L_Q + 3)
                for i in range(TT):
                    copy_out(by_unit(sec, F_Q + i, L_Q + 1), q_sb[:, i, :])
                bank = by_small(sec, F_GATE_T, S_GATE_T)
                nc.scalar.activation(gates.rearrange("p i n -> p (i n)"), bank[:, 0:TT * GATES], ACT.Sigmoid).then_inc(evac_done, 1)
                split_high(sec, L_KVS + 2)
                act.wait_ge(evac_done, sec.fill(F_Q + TT))
                for i in range(TT):
                    nc.scalar.activation(rot[:, i, 0:8, :].rearrange("p h d -> p (h d)"), q_sb[:, i, :], ACT.Copy)
                split_high(sec, L_KVS + 3)
                for i in range(TT):
                    bank = by_unit(sec, F_KVS + i, L_KVS + 1).rearrange("p (s kv g d) -> p s kv g d", s=2, kv=2, g=GROUPS)
                    dst = rot[:, i, 8:16, :].rearrange("p (s g u) d -> p s g u d", s=2, g=GROUPS)
                    for u in range(2):
                        nc.scalar.activation(dst[:, :, :, u, :], bank[:, :, 0, :, :], ACT.Copy)
                    nc.scalar.activation(v_sb[:, i, :, :].rearrange("p s (g d) -> p s g d", g=GROUPS),
                                         bank[:, :, 1, :, :], ACT.Copy).then_inc(evac_done, 1)
                act.wait_ge(cmpx_ready, layer * 2 + 2)
                for c in range(2):
                    nc.scalar.activation(cmp_hi[c], cmp_x[c].rearrange("p m g n -> p m (g n)"), ACT.Copy).then_inc(cmphi_ready, 1)
                for w in range(2):
                    split_high(sec, L_QMEM + w + 2)
                    copy_out(by_unit(sec, F_QMEM[w], L_QMEM + w), pair(qmemT, w))
                    if w == 0:
                        for t in range(2):
                            copy_out(by_small(sec, F_PLAIN + t, S_PLAIN + t), pair(qT, t))
                act.wait_ge(conv_ready, layer + 1)

                def merge_out(w):
                    copy_out(by_unit(sec, F_MERGE[w], L_MERGE[w]), merge[:, 512 * w:512 * w + 512])

                def step_work(kind, k):
                    if kind == "merge":
                        split_high(sec, L_MERGE[k] + 2)
                        merge_out(k)
                    elif kind == "cmp":
                        for half in range(k, 2):
                            split_high(sec, L_CMP[k] + half + 2)
                        copy_out(by_unit(sec, F_CMP[k], L_CMP[k] + 1)[0:GROUPS * N_CMP, 0:CMP_HIDDEN], cmp_rows[k])
                    elif kind == "hid":
                        bank = by_small(sec, F_HID[k], S_HID[k])
                        for t in range(2):
                            ins = nc.scalar.activation(hid[k][:, t, :], bank[:, GROUPS * N_CMP * t:GROUPS * N_CMP * (t + 1)],
                                                       ACT.Gelu_apprx_tanh, bias=lp(("k_b1", "v_b1")[k])[:, t:t + 1])
                        ins.then_inc(evac_done, 1)
                    elif kind == "rot":
                        copy_out(by_small(sec, F_ROT[k], S_ROT[k]), pair(headT, k))
                    else:
                        bank = by_small(sec, F_KCVC, S_KCVC)
                        nc.scalar.activation(kcT, bank[:, 0:GROUPS * N_CMP], ACT.Copy)
                        copy_out(bank[0:N_CMP, T:T + GROUPS * HD], vc[0:N_CMP, :, :].rearrange("p g d -> p (g d)"))

                def sigmoid(b):
                    g = merge[:, KD * T * b:KD * T * (b + 1)]
                    nc.scalar.activation(g, g, ACT.Sigmoid).then_inc(gate_ready, 1)

                jobs = jobs_of(sec)
                step_work("merge", 0)
                exps(sec, 0, jobs[0])
                for n, job in enumerate(jobs):
                    if n + 1 < len(jobs):
                        exps(sec, n + 1, jobs[n + 1])
                    for kind, k in STEP_WORK.get(n, ()):
                        step_work(kind, k)
                    if merge_part(n):
                        w, begin, end = merge_part(n)
                        if end == 2 * KD:
                            if w == CONV_FREE:
                                act.wait_ge(convlo_ready, layer + 1)
                            merge_out(w)
                    if n == CONV_STEP:
                        nc.scalar.activation(br_hi[0], conv_y, ACT.Copy).then_inc(convhi_ready, 1)
                    copy_pT(sec, n, job)
                    if merge_part(n):
                        w, begin, end = merge_part(n)
                        high_piece(sec, L_MERGE[w] + 2, P * begin, P * end)
                    if n:
                        high_tile(sec, jobs[n - 1])
                    if n == 1:
                        split_high(sec, L_CMP[1] + 2)
                act.wait_ge(evac_done, sec.fill(F_FILLS))
                sigmoid(BRANCHES[0])
                split_high(sec, L_BR + 2)
                high_tile(sec, jobs[-1])
                split_high(sec, L_BR + 3)
                sigmoid(BRANCHES[1])
                split_high(sec, L_BR + 4)
                sigmoid(BRANCHES[2])
                for w in range(3, 6):
                    split_high(sec, L_BR + w + 2)
                for c in range(4):
                    act.wait_ge(merged_ready, layer * 4 + c + 1)
                    nc.scalar.activation(pair(merged_hi, c), pair(merged, c), ACT.Copy).then_inc(mhi_ready, 1)
                for w in range(3):
                    split_high(sec, L_OUT + w + 2)
                for i in range(TT):
                    post_sums(sec, 1, L_FFN2 - 1, i)
                    x_squares(sec, 1, i)
                load_post(sec, 2)
                x_high(sec, 3)
                split_high(sec, L_FFN2 + 1)
                ffn(sec, L_FFN2, 1, more=False)
                for i in range(TT):
                    post_sums(sec, 2, L_UNITS - 1, i)

        @block.vector
        def _(dve):
            step = Steps(dve, dve_step, DVE_STEPS[0], DVE_STEPS[1])

            def split_low(sec, n, trip=0):
                s = n % RING
                dve.wait_ge(hi_ready, sec.unit(n + 1) + trip * RING)
                nc.vector.tensor_tensor(lo[:, s, :], raw[:, s, :], hi[:, s, :].bitcast(F32), ALU.subtract).then_inc(lo_ready, 1)

            def low_piece(sec, n, begin, end, count):
                s = n % RING
                if end == UNIT:
                    dve.wait_ge(hi_ready, sec.unit(n + 1))
                else:
                    dve.wait_ge(hi_piece, sec.at(*PIECES, count))
                ins = nc.vector.tensor_tensor(lo[:, s, begin:end], raw[:, s, begin:end], hi[:, s, begin:end].bitcast(F32), ALU.subtract)
                if end == UNIT:
                    ins.then_inc(lo_ready, 1)

            def ask_root(c, parts):
                nc.vector.tensor_scalar(var[:, c:c + 1], parts[:, 0:1], parts[:, 1:2], D * EPS, ALU.add, ALU.add).then_inc(pow_asked, 1)

            def root_ready(sec, p):
                dve.wait_ge(pow_ready, sec.at(*POWS, p + 1))

            def x_scaled(sec, k, p, i):
                if sec.layer is None and k == 0:
                    dve.wait_ge(x_loaded[i], 16)
                else:
                    dve.wait_ge(x_ready, sec.at(12, 12, 4 * {0: -1, 2: 0, 3: 1}[k] + 2 * i + 2))
                if i == 0:
                    if sec.layer is None:
                        dve.wait_ge(pre_loaded, 16 * max(k, 1))
                    elif k > 0:
                        dve.wait_ge(pre_loaded, sec.at(48, 32, 16 * (k - 1)))
                nc.vector.tensor_tensor(xs[:, i, cols(0)], x[:, i, cols(0)], pre[:, cols(0)], ALU.mult)
                dve.wait_ge(sq_ready, sec.at(14, 14, {0: 0, 2: 6, 3: 10}[k] + 2 * i + 2))
                ask_root(i, sums[:, 2 * i:2 * i + 2])
                nc.vector.tensor_tensor(xs[:, i, cols(1)], x[:, i, cols(1)], pre[:, cols(1)], ALU.mult)
                root_ready(sec, p)
                nc.vector.tensor_scalar(diag[:, i, :], ident, rstd[:, i:i + 1], ROOT_D, ALU.mult, ALU.mult).then_inc(xs_ready, 1)

            def x_low(sec, k):
                for i in range(TT):
                    for b in range(2):
                        dve.wait_ge(xhi_ready, sec.at(16, 16, 4 * k + 2 * i + b + 1))
                        nc.vector.tensor_tensor(rows_operand(xT_lo, i, b), rows_bank(i, b), rows_operand(xT_hi, i, b).bitcast(F32),
                                                ALU.subtract).then_inc(xlo_ready, 1)

            def mem_scaled(sec, p):
                dve.wait_ge(sq_ready, sec.at(14, 14, 6))
                nc.vector.tensor_scalar(var[:, 4:4 + TT], sums[:, 0:TT], D * EPS, None, ALU.add).then_inc(pow_asked, 1)
                root_ready(sec, p)
                for i in range(TT):
                    nc.vector.tensor_scalar(xs[:, i, :], mem_in[:, i, :], rstd[:, 4 + i:5 + i], ROOT_D, ALU.mult,
                                            ALU.mult).then_inc(xs_ready, 1)

            def mem_low(sec, r, gain):
                dve.wait_ge(xhi_ready, sec.at(16, 16, 4 + r + 1))
                for c in range(2):
                    kt = 2 * r + c
                    ins = nc.vector.scalar_tensor_tensor(memT_lo[:, kt, :], work[:, 2 + r % 2, T * c:T * c + T], gain[:, kt:kt + 1],
                                                         memT_hi[:, kt, :].bitcast(F32), ALU.mult, ALU.subtract)
                ins.then_inc(xlo_ready, 1)

            def ffn(sec, u0, k, begin=None, mem_gain=None, more=True):
                c0 = sec.at(2 * CHUNKS, 2 * CHUNKS, k * CHUNKS)

                def gated(j, n, trip=0):
                    dve.wait_ge(silu_ready, c0 + j + 1)
                    dve.wait_ge(unit_used, sec.unit(n + 1) + trip * RING)
                    wait(dve, hTlo_ready, c0 + j)
                    nc.vector.tensor_tensor(h_sb, silu_a, work[:, 1, :], ALU.mult).then_inc(h_ready, 1)

                def low_h(j, high, low):
                    dve.wait_ge(hThi_ready, c0 + j + 1)
                    nc.vector.tensor_tensor(low.rearrange("p f t -> p (f t)"), h_sb,
                                            high.rearrange("p f t -> p (f t)").bitcast(F32), ALU.subtract).then_inc(hTlo_ready, 1)

                split_low(sec, u0 + 2)
                split_low(sec, u0 + 3)
                gated(0, u0 + 1)
                low_h(0, hT_hi, hT_lo)
                split_low(sec, u0 + 4)
                if begin:
                    begin()
                with dve.Fori(1, CHUNKS - 1) as j:
                    split_low(sec, u0 + 2, j)
                    gated(j, u0, j)
                    split_low(sec, u0 + 3, j)
                    low_h(j, hT_hi, hT_lo)
                    split_low(sec, u0 + 4, j)
                last = CHUNKS - 1
                split_low(sec, u0 + 2 + 3 * last)
                gated(last, u0 + 3 * last)
                if mem_gain is not None:
                    mem_low(sec, 0, mem_gain)
                    mem_low(sec, 1, mem_gain)
                low_h(last, *hT_last)
                if more:
                    split_low(sec, u0 + FFN_UNITS)
                if mem_gain is not None:
                    mem_low(sec, 2, mem_gain)
                    mem_low(sec, 3, mem_gain)
                if more:
                    split_low(sec, u0 + FFN_UNITS + 1)

            def residual(sec, r, n, i, scale):
                for c in range(2):
                    sums_ready(dve, sec, r, n, i, c)
                    nc.vector.scalar_tensor_tensor(x[:, i, cols(c)], acc[:, 2 * i + c, :], scale, x[:, i, cols(c)], ALU.mult,
                                                   ALU.add).then_inc(x_ready, 1)

            def post_residual(sec, r, p, scale, i):
                scaled = []
                for c in range(2):
                    dve.wait_ge(ysq_ready, sec.at(0, 12, 4 * r + 2 * i + c + 1))
                    if c == 1:
                        ask_root(2 + i, ysums[:, 2 * i:2 * i + 2])
                    elif i == 0:
                        dve.wait_ge(post_loaded, sec.at(0, 48, 16 * (r + 1)))
                    scaled.append(step.mark(nc.vector.scalar_tensor_tensor(xs[:, i, cols(c)], acc[:, 2 * i + c, :], scale * ROOT_D,
                                                                           post[:, cols(c)], ALU.mult, ALU.mult)))
                root_ready(sec, p)
                for c in range(2):
                    step.after(scaled[c])
                    nc.vector.scalar_tensor_tensor(x[:, i, cols(c)], xs[:, i, cols(c)], rstd[:, 2 + i:3 + i], x[:, i, cols(c)],
                                                   ALU.mult, ALU.add).then_inc(x_ready, 1)

            def score(sec, n, job):
                dve.wait_ge(qk_ready, sec.at(*JOBS, n + 1))
                nc.vector.memset(soft[:, n % 2, 2, :], 0.0)
                for i in range(TT):
                    w = job.width(i)
                    nc.vector.tensor_tensor_reduce(
                        out=prob[:, n % 2, i, 0:w], in0=acc[:, n % 2, T * i:T * i + w], in1=job.bias(i, w),
                        scale=-job.scale, scalar=BIG, op0=ALU.add, op1=ALU.min,
                        accum_out=soft[:, n % 2, 0, i:i + 1]).then_inc(scored, 1)

            def normalise(sec, n, job):
                dve.wait_ge(exp_ready, sec.at(2 * JOBS[0], 2 * JOBS[1], 2 * n + 2))
                step.link(nc.vector.reciprocal(soft[:, n % 2, 2, :], soft[:, n % 2, 1, :]))
                for i in range(TT):
                    p = prob[:, n % 2, i, 0:job.width(i)]
                    if job.factor is None:
                        ins = nc.vector.tensor_scalar(p, p, soft[:, n % 2, 2, i:i + 1], None, ALU.mult)
                    else:
                        ins = nc.vector.tensor_scalar(p, p, soft[:, n % 2, 2, i:i + 1], job.factor(i), ALU.mult, ALU.mult)
                    ins.then_inc(p_ready, 1)

            def low_tile(sec, job):
                if job.tile_done:
                    dve.wait_ge(tile_hi, sec.at(*TILES, job.tile + 1))
                    high, low = tile_dst(sec, job.tile)
                    nc.vector.tensor_tensor(low, tile_bank(job.tile), high.bitcast(F32), ALU.subtract).then_inc(tile_lo, 1)

            sec = Section()
            step.enter(sec)
            dve.sem_inc(lo_ready, 1)
            dve.wait_ge(ident_loaded, 16)
            for i in range(TT):
                x_scaled(sec, 0, i, i)
            x_low(sec, 0)
            split_low(sec, B1_FFN1)
            split_low(sec, B1_FFN1 + 1)

            def begin():
                mem_scaled(sec, 2)
                lam = b1p("lam")
                step.link(nc.vector.tensor_scalar(lam_t[:, 6, :], lam, -1.0, None, ALU.mult))
                nc.vector.tensor_scalar(lam_t[:, 2, :], lam, -1.0, 0.0, ALU.mult, ALU.max).then_inc(lam_asked, 1)
                nc.vector.tensor_tensor(lam_t[:, 0, :], lam, lam_t[:, 6, :], ALU.min).then_inc(lam_asked, 1)

            ffn(sec, B1_FFN1, 0, begin, b1p("g_mem"))
            for i in range(TT):
                residual(sec, 0, B1_MEM - 1, i, 0.5)
                x_scaled(sec, 2, 3 + i, i)
            split_low(sec, B1_MEM + 2)
            split_low(sec, B1_MEM + 3)
            x_low(sec, 2)
            split_low(sec, B1_LRU_X + 2)
            pads = step.mark(nc.vector.memset(lru_in[:, :, 0:CONV_W - 1], 0.0))

            def head_roots(first, n):
                for i in range(TT):
                    part, square = heads1[:, i, first:first + n, :], squares[:, i, first:first + n, :]
                    ins = nc.vector.tensor_tensor(square, part, part, ALU.mult)
                step.link(ins)
                for i in range(TT):
                    ins = nc.vector.reduce_sum(sums[:, 16 * i + first:16 * i + first + n], squares[:, i, first:first + n, :], axis=AX_X)
                step.link(ins)
                nc.vector.tensor_scalar(head_sums(var, first, n), head_sums(sums, first, n), 1.0 / HD, EPS, ALU.mult,
                                        ALU.add).then_inc(pow_asked, 1)

            def head_scaled(p, first, n):
                root_ready(sec, p)
                for i in range(TT):
                    part = heads1[:, i, first:first + n, :]
                    ins = nc.vector.tensor_tensor(part, part, rstd[:, 16 * i + first:16 * i + first + n].unsqueeze(2).to_broadcast([P, n, HD]),
                                                  ALU.mult)
                ins.then_inc(heads_ready, 1)

            conv_w = b1p("conv_w").rearrange("p (c w) -> p c w", c=LRU_TILES)
            for half in range(2):
                split_low(sec, B1_LRU_X + half + 3)
                dve.wait_ge(evac_done, F1_LRU_X + half + 1)
                step.after(pads)
                for tap in range(CONV_W):
                    for c in (2 * half, 2 * half + 1):
                        shifted = lru_in[:, c, tap:tap + T]
                        if tap == 0:
                            m = step.mark(nc.vector.tensor_scalar(lru_xb[:, c, :], shifted, conv_w[:, c, 0:1],
                                                                  b1p("conv_b")[:, c:c + 1], ALU.mult, ALU.add))
                            continue
                        step.after(m - 1 + c % 2 if tap == 1 or c % 2 == 0 else m)
                        ins = nc.vector.scalar_tensor_tensor(lru_xb[:, c, :], shifted, conv_w[:, c, tap:tap + 1],
                                                             lru_xb[:, c, :], ALU.mult, ALU.add)
                        if tap < CONV_W - 1:
                            m = step.mark(ins)
                        elif c % 2:
                            ins.then_inc(xb_ready, 1)
            split_low(sec, B1_QK + 3)
            for i in range(TT):
                ins = nc.vector.tensor_copy(heads1[:, i, 12:16, :].rearrange("p h d -> p (h d)"), memv[:, i, 0:T])
            step.link(ins)
            head_roots(12, 4)
            dve.wait_ge(evac_done, F1_QK + 2)
            head_roots(0, 8)
            split_low(sec, B1_VC + 2)
            head_scaled(5, 12, 4)
            head_scaled(6, 0, 8)
            split_low(sec, B1_VC + 3)
            dve.wait_ge(evac_done, F1_VC + 2)
            head_roots(8, 4)
            head_scaled(7, 8, 4)

            def out_low(n):
                u, q = divmod(n, 4)
                low_piece(sec, B1_OUT + u, UNIT // 4 * q, UNIT // 4 * (q + 1), 3 * u + q + 1)

            jobs = jobs_of(sec)
            dve.wait_ge(tables_loaded, 48)
            score(sec, 0, jobs[0])
            normalise(sec, 0, jobs[0])
            for n, job in enumerate(jobs):
                if n + 1 < len(jobs):
                    score(sec, n + 1, jobs[n + 1])
                    normalise(sec, n + 1, jobs[n + 1])
                if 1 <= n <= LRU_TILES:
                    c = n - 1
                    if c == 0:
                        dve.wait_ge(evac_done, F1_GATE + 4)
                    xi = step.mark(nc.vector.tensor_tensor(lru_xb[:, c, :], lru_xb[:, c, :], lru_i[:, c, :], ALU.mult))
                    dve.wait_ge(lru_a_ready, c + 1)
                    step.link(nc.vector.tensor_tensor(lru_y[:, c, :], lru_a[:, c, :], lru_a[:, c, :], ALU.mult))
                    ins = nc.vector.scalar_tensor_tensor(lru_m[:, c, :], lru_y[:, c, :], 1.0, lru_m[:, c, :], ALU.add, ALU.mult)
                    if c == LRU_TILES - 1:
                        ins.then_inc(m2_ready, 1)
                if n:
                    out_low(n - 1)
                    low_tile(sec, jobs[n - 1])
            out_low(len(jobs) - 1)
            low_tile(sec, jobs[-1])
            split_low(sec, B1_OUT + 2)
            dve.wait_ge(mult_ready, 1)
            step.link(nc.vector.memset(lru_r[:, :, 0:1], 1.0))
            step.after(xi)
            step.link(nc.vector.tensor_tensor(lru_xb, lru_xb, lru_r, ALU.mult))
            for c in range(LRU_TILES):
                ins = nc.vector.tensor_tensor_scan(lru_m[:, c, :], lru_a[:, c, :], lru_xb[:, c, :], 0.0, ALU.mult, ALU.add)
            step.link(ins)
            dve.wait_ge(gelu_ready, 1)
            nc.vector.tensor_tensor(lru_y, lru_m, lru_g, ALU.mult).then_inc(lruy_ready, 1)
            split_low(sec, B1_OUT + 3)
            dve.wait_ge(lruhi_ready, 1)
            nc.vector.tensor_tensor(mix_lo[:, 0:LRU_TILES, :], lru_y, mix_hi[:, 0:LRU_TILES, :].bitcast(F32),
                                    ALU.subtract).then_inc(lrulo_ready, 1)
            split_low(sec, B1_OUT + 4)
            for i in range(TT):
                residual(sec, 1, B1_FFN2 - 1, i, 1.0)
                x_scaled(sec, 3, 8 + i, i)
            x_low(sec, 3)
            split_low(sec, B1_FFN2 + 1)

            def angles():
                dve.wait_ge(tables_loaded, 48)
                step.link(nc.vector.tensor_copy(angle[:, 0, 0:TT], pos_i))
                for i in range(TT):
                    ins = nc.vector.tensor_scalar(angle[:, 1, ROT * i:ROT * i + ROT], cst("inv_freq"), angle[:, 0, i:i + 1],
                                                  None, ALU.mult)
                step.link(ins)
                step.link(nc.vector.tensor_scalar(angle[:, 2, :], angle[:, 1, :], 1.0 / TURN, ROUND, ALU.mult, ALU.add))
                step.link(nc.vector.tensor_scalar(angle[:, 2, :], angle[:, 2, :], -ROUND, None, ALU.add))
                for part in TURN_PARTS:
                    step.link(nc.vector.scalar_tensor_tensor(angle[:, 1, :], angle[:, 2, :], -part, angle[:, 1, :], ALU.mult, ALU.add))
                step.link(nc.vector.tensor_scalar(angle[:, 5, :], angle[:, 1, :], PI, -PI, ALU.min, ALU.max))
                step.link(nc.vector.tensor_scalar(angle[:, 3, :], angle[:, 5, :], -1.0, None, ALU.mult))
                step.link(nc.vector.tensor_tensor(angle[:, 3, :], angle[:, 3, :], angle[:, 5, :], ALU.max))
                nc.vector.tensor_scalar(angle[:, 4, :], angle[:, 3, :], -1.0, PI / 2, ALU.mult, ALU.add).then_inc(trig_asked, 1)

            ffn(sec, B1_FFN2, 1, angles, more=False)
            for i in range(TT):
                residual(sec, 2, B1_UNITS - 1, i, 0.5)
            step.leave()

            with dve.Fori(0, LAYERS) as layer:
                sec = Section(layer)
                step.enter(sec)
                dve.wait_ge(landed[L_PARAM], sec.landed(L_PARAM))
                dve.wait_ge(landed[L_GAIN], sec.landed(L_GAIN))
                dve.wait_ge(lo_ready, sec.unit(0))
                dve.sem_inc(lo_ready, L_FFN1)
                for i in range(TT):
                    x_scaled(sec, 0, i, i)
                x_low(sec, 0)
                split_low(sec, L_FFN1)
                split_low(sec, L_FFN1 + 1)
                ffn(sec, L_FFN1, 0, lambda: mem_scaled(sec, 2), lp("g_mem"))
                for i in range(TT):
                    post_residual(sec, 0, 3 + 2 * i, 0.5, i)
                    x_scaled(sec, 2, 4 + 2 * i, i)
                split_low(sec, L_MEM + 2)
                split_low(sec, L_MEM + 3)
                dve.wait_ge(gwhi_ready, layer + 1)
                nc.vector.tensor_tensor(gw_lo.rearrange("p k n -> p (k n)"), lp("gate_w"),
                                        gw_hi.rearrange("p k n -> p (k n)").bitcast(F32), ALU.subtract).then_inc(gwlo_ready, 1)
                split_low(sec, L_MEM + 4)
                x_low(sec, 2)
                split_low(sec, L_MEM + 5)
                with dve.Fori(0, 2) as trip:
                    for w in range(3):
                        split_low(sec, L_CONV + w + 2, trip)
                split_low(sec, L_KV + 2)
                convolved = conv_in.rearrange("p (k c t) -> p k c t", k=3, c=4)
                conv_w = lp("conv_w").rearrange("p (c w) -> p c w", c=4)

                def conv_tile(c):
                    for tap in range(CONV2_W):
                        shifted = conv_v[:, c, tap:tap + T]
                        if tap == 0:
                            step.link(nc.vector.tensor_scalar(conv_y[:, c, :], shifted, conv_w[:, c, 0:1], None, ALU.mult))
                        else:
                            step.link(nc.vector.scalar_tensor_tensor(conv_y[:, c, :], shifted, conv_w[:, c, tap:tap + 1],
                                                                     conv_y[:, c, :], ALU.mult, ALU.add))
                    return nc.vector.tensor_tensor(conv_y[:, c, :], conv_y[:, c, :], convolved[:, 1, c, :], ALU.mult)

                dve.wait_ge(evac_done, sec.fill(F_KV))
                step.link(nc.vector.memset(conv_v[:, :, 0:CONV2_W - 1], 0.0))
                step.link(nc.vector.tensor_tensor(conv_v[:, :, CONV2_W - 1:], convolved[:, 2, :, :], convolved[:, 0, :, :], ALU.mult))
                split_low(sec, L_Q + 2)
                conv_tile(0)
                split_low(sec, L_Q + 3)
                conv_tile(1)
                for c, name in enumerate(("pos_k", "pos_v")):
                    for g in range(GROUPS):
                        base = cmp_src[c][:, g, :]
                        windows = bass.AP(base.tensor, base.offset, [base.ap[0], [2, CMP_PAIRS], [CMP_STRIDE, N_CMP]])
                        ins = nc.vector.tensor_tensor(cmp_x[c][:, :, g, :], windows,
                                                      lp(name).unsqueeze(2).to_broadcast([P, CMP_PAIRS, N_CMP]), ALU.add)
                    ins.then_inc(cmpx_ready, 1)
                split_low(sec, L_KVS + 2)
                conv_tile(2)
                split_low(sec, L_KVS + 3)
                conv_tile(3).then_inc(conv_ready, 1)
                dve.wait_ge(evac_done, sec.fill(F_GATE_T + 1))
                for i in range(TT):
                    g0 = gates[:, i, :].rearrange("p (h b) -> p h b", b=3)[:, :, 0]
                    ins = nc.vector.tensor_scalar(g0, g0, cst("cmp_valid")[:, i:i + 1], None, ALU.mult)
                step.link(ins)
                for c in range(2):
                    dve.wait_ge(cmphi_ready, layer * 2 + c + 1)
                    nc.vector.tensor_tensor(cmp_lo[c], cmp_x[c].rearrange("p m g n -> p m (g n)"), cmp_hi[c].bitcast(F32),
                                            ALU.subtract).then_inc(cmplo_ready, 1)
                split_low(sec, L_QMEM + 2)
                t1, t2 = rot[:, :, :, 0:ROT], rot[:, :, :, ROT:2 * ROT]
                cosines, sines = (trig[:, c, :, :].unsqueeze(2).to_broadcast([P, TT, 16, ROT]) for c in range(2))
                for n, (a, b) in enumerate(((t1, cosines), (t2, sines), (t2, cosines), (t1, sines))):
                    for i in range(TT):
                        ins = nc.vector.tensor_tensor(rope_t[:, n, i], a[:, i], b[:, i], ALU.mult)
                step.link(ins)
                nc.vector.tensor_tensor(t1, rope_t[:, 0], rope_t[:, 1], ALU.subtract)
                nc.vector.tensor_tensor(t2, rope_t[:, 2], rope_t[:, 3], ALU.add).then_inc(rot_ready, 1)
                dve.wait_ge(rot_ready, layer + 1)
                split_low(sec, L_QMEM + 3)

                def step_work(kind, k):
                    if kind == "merge":
                        split_low(sec, L_MERGE[k] + 2)
                    elif kind == "cmp":
                        for half in range(2):
                            split_low(sec, L_CMP[k] + half + 2)

                def merge_low(n):
                    w, begin, end = merge_part(n)
                    h, b = divmod(n - FIRST_NSA, 3)
                    low_piece(sec, L_MERGE[w] + 2, P * begin, P * end, 2 * h + b + 1)

                jobs = jobs_of(sec)
                step_work("merge", 0)
                score(sec, 0, jobs[0])
                normalise(sec, 0, jobs[0])
                for n, job in enumerate(jobs):
                    if n + 1 < len(jobs):
                        score(sec, n + 1, jobs[n + 1])
                    for kind, k in STEP_WORK.get(n, ()):
                        step_work(kind, k)
                    if merge_part(n - 1):
                        merge_low(n - 1)
                    if n == CONV_STEP + 1:
                        dve.wait_ge(convhi_ready, layer + 1)
                        nc.vector.tensor_tensor(br_lo[0], conv_y, br_hi[0].bitcast(F32), ALU.subtract).then_inc(convlo_ready, 1)
                    if n + 1 < len(jobs):
                        normalise(sec, n + 1, jobs[n + 1])
                    if n:
                        low_tile(sec, jobs[n - 1])
                merge_low(len(jobs) - 1)
                partial = []
                gate = merge.rearrange("p (b c t) -> p b c t", b=3, c=KD)

                def merged_low(c):
                    dve.wait_ge(mhi_ready, layer * 4 + c + 1)
                    c2 = slice(2 * c, 2 * c + 2)
                    nc.vector.tensor_tensor(merged_lo[:, c2, :], merged[:, c2, :], merged_hi[:, c2, :].bitcast(F32),
                                            ALU.subtract).then_inc(mlo_ready, 1)

                for w in range(6):
                    split_low(sec, L_BR + w + 2)
                    b, half = w // 2, w % 2
                    if w == 1:
                        low_tile(sec, jobs[-1])
                    if w == 5:
                        merged_low(0)
                        merged_low(1)
                    dve.wait_ge(gate_ready, layer * 3 + b + 1)
                    for k in range(2):
                        if k == 0:
                            dve.wait_ge(br_half, layer * 6 + w + 1)
                        else:
                            dve.wait_ge(unit_used, sec.unit(L_BR + w + 1))
                        c = slice(4 * half + 2 * k, 4 * half + 2 * k + 2)
                        bank = br_bank(w, k).rearrange("p (c t) -> p c t", c=2)
                        g = gate[:, BRANCHES[b], c, :]
                        if b == 0:
                            nc.vector.tensor_tensor(merged[:, c, :], bank, g, ALU.mult).then_inc(br_read, 1)
                            continue
                        t = br_t[:, k, :].rearrange("p (c t) -> p c t", c=2)
                        nc.vector.tensor_tensor(t, bank, g, ALU.mult).then_inc(br_read, 1)
                        dve.wait_ge(br_read, layer * 12 + (2 * w + k + 1))
                        if b == 2:
                            step.after(partial[2 * half + k])
                        ins = nc.vector.tensor_tensor(merged[:, c, :], merged[:, c, :], t, ALU.add)
                        if b == 1:
                            partial.append(step.mark(ins))
                        else:
                            ins.then_inc(merged_ready, 1)
                merged_low(2)
                merged_low(3)
                for w in range(3):
                    split_low(sec, L_OUT + w + 2)
                for i in range(TT):
                    post_residual(sec, 1, 7 + 2 * i, 1.0, i)
                    x_scaled(sec, 3, 8 + 2 * i, i)
                x_low(sec, 3)
                split_low(sec, L_FFN2 + 1)
                ffn(sec, L_FFN2, 1, more=False)
                for i in range(TT):
                    post_residual(sec, 2, 11 + i, 0.5, i)
                step.leave()

        @block.tensor
        def _(pe):
            def product(dst, a_hi, a_lo, b_hi, b_lo, start, stop):
                nc.tensor.matmul(dst, a_hi, b_hi, start=start, stop=False)
                nc.tensor.matmul(dst, a_hi, b_lo, start=False, stop=False)
                return nc.tensor.matmul(dst, a_lo, b_hi, start=False, stop=stop)

            def parts_ready(sec, n, trip=0):
                pe.wait_ge(lo_ready, sec.unit(n + 1) + trip * RING)

            def rows_half(n, half, i, dst, a_hi, a_lo, first=0, ready=None):
                s = n % RING
                for q in range(4):
                    kt = 4 * half + q
                    if ready:
                        ready(kt)
                    last = product(dst, a_hi[:, kt, P * i:P * i + P], a_lo[:, kt, P * i:P * i + P],
                                   hi[:, s, 512 * q:512 * q + 512], lo[:, s, 512 * q:512 * q + 512],
                                   half == first and q == 0, half != first and q == 3)
                return last

            def bank_free(sec, f, trip=0):
                wait(pe, evac_done, sec.fill(f - 2) + trip * 3)

            def rows_unit(sec, n, f, half, a=(xT_hi, xT_lo)):
                parts_ready(sec, n + half)
                for i in range(TT):
                    if half == 0:
                        bank_free(sec, f + i)
                    last = rows_half(n + half, half, i, work[:, (f + i) % 3, :], *a)
                last.then_inc(unit_used, 1)

            def rows(sec, n, f, a=(xT_hi, xT_lo)):
                for half in range(2):
                    rows_unit(sec, n, f, half, a)

            def channel_steps(bank, n, a, begin=0, end=2 * KD):
                s = n % RING
                for at in range(begin, end):
                    c, kt = divmod(at, KD)
                    w = slice(P * at, P * at + P)
                    last = product(bank[:, T * c:T * c + T], hi[:, s, w], lo[:, s, w], a[0][:, kt, :], a[1][:, kt, :],
                                   kt == 0, kt == KD - 1)
                return last

            def first_unit(sec, n, k, bank):
                s = n % RING
                pe.wait_ge(hi_ready, sec.unit(n + 1))
                for turn, (w, a) in enumerate(((hi, xT_hi), (hi, xT_lo), (lo, xT_hi))):
                    if turn == 2:
                        parts_ready(sec, n)
                    for b in range(2):
                        if turn < 2:
                            pe.wait_ge((xhi_ready, xlo_ready)[turn], sec.at(16, 16, 4 * k + 2 + b + 1))
                        for c in range(2):
                            for kt in range(4 * b, 4 * b + 4):
                                at = P * (KD * c + kt)
                                last = nc.tensor.matmul(bank[:, T * c:T * c + T], w[:, s, at:at + P], a[:, kt, :],
                                                        start=(turn, c, kt) == (0, 0, 0), stop=(turn, c, kt) == (2, 1, KD - 1))
                return last

            def channels(sec, n, f, trip=0, a=(xT_hi, xT_lo), begin=0, end=2 * KD):
                if begin == 0:
                    bank_free(sec, f, trip)
                    parts_ready(sec, n, trip)
                last = channel_steps(work[:, f % 3, :], n, a, begin, end)
                if end == 2 * KD:
                    last.then_inc(unit_used, 1)

            def transposes(sec, f, src):
                bank_free(sec, f)
                for c in range(2):
                    for i in range(TT):
                        last = nc.tensor.transpose(work[:, f % 3, T * c + P * i:T * c + P * i + P], src(c, i), ident)
                last.then_inc(small_ready, 1)

            def keep_clock(n):
                for _ in range(n):
                    nc.tensor.matmul(work[:, 3, 0:P], ident, ident, start=True, stop=True)

            def x_transposed(sec, k):
                for i in range(TT):
                    if k != 2:
                        keep_clock(WAITING[sec.layer is None, k][i])
                    pe.wait_ge(xs_ready, sec.at(8, 8, x_norm_at(k) + i + 1))
                    for b in range(2):
                        for q in range(4):
                            last = nc.tensor.matmul(acc[:, 2 * i + b, P * q:P * q + P], xs[:, i, P * (4 * b + q):P * (4 * b + q) + P],
                                                    diag[:, i, :], start=True, stop=True)
                        last.then_inc(xT_ready, 1)

            def mem_transposed(sec, r):
                if r == 0:
                    pe.wait_ge(xs_ready, sec.at(8, 8, 4))
                if r >= 2:
                    pe.wait_ge(xlo_ready, sec.at(16, 16, 4 + r - 1))
                for c in range(2):
                    for i in range(TT):
                        at = T * c + P * i
                        last = nc.tensor.transpose(work[:, 2 + r % 2, at:at + P], xs[:, i, P * (2 * r + c):P * (2 * r + c) + P], ident)
                last.then_inc(xT_ready, 1)

            def operand_ready(sec, k):
                pe.wait_ge(xlo_ready, sec.at(16, 16, 4 * k + 4))

            def ffn(sec, u0, k, before, mem=False):
                c0 = sec.at(2 * CHUNKS, 2 * CHUNKS, k * CHUNKS)
                wait(pe, evac_done, sec.fill(before))

                def chunk_in(n, j, trip, first=False):
                    for part in range(2):
                        if not first:
                            pe.wait_ge((silu_ready, h_ready)[part], c0 + j)
                        if first and part == 0:
                            last = first_unit(sec, n, 3 * k, work[:, 0, :])
                        else:
                            parts_ready(sec, n + part, trip)
                            last = channel_steps(work[:, part, :], n + part, (xT_hi, xT_lo))
                        last.then_inc(unit_used, 1)

                def out_tile(n, i, h, first=False, final=False):
                    s = n % RING
                    for c in range(2):
                        for f in range(2):
                            w = slice(D * f + 512 * c, D * f + 512 * c + 512)
                            last = product(acc[:, 2 * i + c, :], h[0][:, f, P * i:P * i + P], h[1][:, f, P * i:P * i + P],
                                           hi[:, s, w], lo[:, s, w], first and f == 0, final and f == 1)
                        if final and (i, c) == (1, 0):
                            last.then_inc(sum1_ready, 1)
                    return last

                def chunk_out(n, j, trip, first=False):
                    pe.wait_ge(hTlo_ready, c0 + j + 1)
                    parts_ready(sec, n, trip)
                    for i in range(TT):
                        last = out_tile(n, i, (hT_hi, hT_lo), first)
                    last.then_inc(unit_used, 1)

                chunk_in(u0, 0, 0, first=True)
                chunk_in(u0 + 2, 1, 0)
                chunk_out(u0 + 4, 0, 0, first=True)
                with pe.Fori(2, CHUNKS - 1) as j:
                    chunk_in(u0 - 1, j, j)
                    chunk_out(u0 + 1, j - 1, j)
                j = CHUNKS - 1
                chunk_in(u0 + 3 * j - 1, j, 0)
                if mem:
                    mem_transposed(sec, 0)
                    mem_transposed(sec, 1)
                before, last_unit = u0 + 3 * j + 1, u0 + FFN_UNITS - 1
                pe.wait_ge(hTlo_ready, c0 + j)
                parts_ready(sec, before)
                out_tile(before, 0, (hT_hi, hT_lo))
                if mem:
                    mem_transposed(sec, 2)
                    mem_transposed(sec, 3)
                pe.wait_ge(hTlo_ready, c0 + j + 1)
                parts_ready(sec, last_unit)
                out_tile(last_unit, 0, hT_last, final=True).then_inc(sum0_ready, 1)
                out_tile(before, 1, (hT_hi, hT_lo)).then_inc(unit_used, 1)
                out_tile(last_unit, 1, hT_last, final=True).then_inc(unit_used, 1)

            def output(sec, n, a, ready, first=0):
                for c in range(2):
                    parts_ready(sec, n + c)
                    for i in range(TT):
                        last = rows_half(n + c, first, i, acc[:, 2 * i + c, :], *a, first, ready if (c, i) == (0, 0) else None)
                    last.then_inc(unit_used, 1)
                parts_ready(sec, n + 2)
                for i in range(TT):
                    for c in range(2):
                        if i == 0 and c == 1:
                            parts_ready(sec, n + 3)
                        last = rows_half(n + 2 + c, 1 - first, i, acc[:, 2 * i + c, :], *a, first, ready if (c, i) == (0, 0) else None)
                        if (i, c) == (0, 1):
                            last.then_inc(sum0_ready, 1)
                        elif i == 1:
                            last.then_inc(unit_used, 1)

            def scores(sec, n, job):
                if n >= 2:
                    pe.wait_ge(scored, sec.at(2 * JOBS[0], 2 * JOBS[1], 2 * n - 2))
                for i in range(TT):
                    w = job.width(i)
                    last = nc.tensor.matmul(acc[:, n % 2, T * i:T * i + w], job.q(i), job.k(w), start=True, stop=True)
                last.then_inc(qk_ready, 1)

            def turn(sec, n, job):
                pe.wait_ge(p_ready, sec.at(2 * JOBS[0], 2 * JOBS[1], 2 * n + 2))
                if n >= 1:
                    pe.wait_ge(pT_copied, sec.at(*JOBS, n))
                for kt, i, at in job.blocks():
                    r = job.rows(kt)
                    last = nc.tensor.transpose(acc[0:r, 2, at:at + P], prob[:, n % 2, i, P * kt:P * kt + r], ident)
                last.then_inc(pT_ready, 1)

            def values(sec, n, job):
                pe.wait_ge(pT_copied, sec.at(*JOBS, n + 1))
                if job.first and job.tile >= 2:
                    pe.wait_ge(tile_lo, sec.at(*TILES, job.tile - 1))
                at = 0
                for kt in range(job.key_tiles):
                    r, span = job.rows(kt), job.span(kt)
                    y = tile_bank(job.tile)[job.row:job.row + job.m, span:T]
                    last = nc.tensor.matmul(y, job.v(kt), probT[0:r, n % 2, at:at + T - span],
                                            start=job.first and kt == 0, stop=job.last and kt == job.key_tiles - 1)
                    at += T - span
                if job.tile_done:
                    last.then_inc(tile_ready, 1)

            sec = Section()
            pe.sem_inc(unit_used, 1)
            pe.wait_ge(ident_loaded, 16)
            x_transposed(sec, 0)
            ffn(sec, B1_FFN1, 0, 0, mem=True)
            operand_ready(sec, 1)
            rows_unit(sec, B1_MEM, F1_MEM, 0, (memT_hi, memT_lo))
            x_transposed(sec, 2)
            rows_unit(sec, B1_MEM, F1_MEM, 1, (memT_hi, memT_lo))
            operand_ready(sec, 2)
            for w in range(2):
                channels(sec, B1_LRU_X + w, F1_LRU_X + w)
            rows(sec, B1_QK, F1_QK)
            rows(sec, B1_VC, F1_VC)
            pe.wait_ge(xb_ready, 2)
            for w in range(4):
                bank_free(sec, F1_GATE + w)
                for c in range(2):
                    ct = 2 * (w % 2) + c
                    weights = b1p("a_w" if w < 2 else "x_w")[:, P * ct:P * ct + P]
                    last = nc.tensor.matmul(work[:, (F1_GATE + w) % 3, T * c:T * c + T], weights, lru_xb[:, ct, :],
                                            start=True, stop=True)
                last.then_inc(small_ready, 1)

            def head_turn(name):
                kind = HEADS[name]
                transposes(sec, F1_HEADS[name], lambda c, i: heads1[:, i, 4 * kind + 2 * c:4 * kind + 2 * c + 2, :].rearrange("p h d -> p (h d)"))

            pe.wait_ge(heads_ready, 2)
            for name in ("q", "k", "mem_k"):
                head_turn(name)
            jobs = jobs_of(sec)
            pe.wait_ge(evac_done, F1_HEADS["k"] + 1)
            scores(sec, 0, jobs[0])
            for n, job in enumerate(jobs):
                if n + 1 < len(jobs):
                    if n + 1 == 4:
                        pe.wait_ge(evac_done, F1_HEADS["mem_q"] + 1)
                    scores(sec, n + 1, jobs[n + 1])
                if n == 0:
                    pe.wait_ge(heads_ready, 3)
                    head_turn("mem_q")
                g, q = divmod(n, 4)
                channels(sec, B1_LRU_G + g, F1_LRU_G[g], begin=4 * q, end=4 * q + 4)
                turn(sec, n, job)
                if n:
                    values(sec, n - 1, jobs[n - 1])
            values(sec, len(jobs) - 1, jobs[-1])

            def mixed_ready(kt):
                if kt == LRU_TILES:
                    pe.wait_ge(tile_lo, jobs[-1].tile)
                elif kt == KD - 1:
                    pe.wait_ge(tile_lo, jobs[-1].tile + 1)
                elif kt == 0:
                    pe.wait_ge(lrulo_ready, 1)

            output(sec, B1_OUT, (mix_hi, mix_lo), mixed_ready, first=1)
            x_transposed(sec, 3)
            ffn(sec, B1_FFN2, 1, F1_FILLS)

            with pe.Fori(0, LAYERS) as layer:
                sec = Section(layer)
                pe.wait_ge(unit_used, sec.unit(0))
                pe.sem_inc(unit_used, L_FFN1)
                x_transposed(sec, 0)
                ffn(sec, L_FFN1, 0, 0, mem=True)
                operand_ready(sec, 1)
                for w in range(2):
                    channels(sec, L_MEM + w, F_MEMK + w, a=(memT_hi, memT_lo))
                x_transposed(sec, 2)
                rows(sec, L_MEM + 2, F_MEMV, (memT_hi, memT_lo))
                with pe.Fori(0, 2) as trip:
                    operand_ready(sec, 2)
                    for w in range(3):
                        channels(sec, L_CONV + w, F_CONV + w, trip)
                channels(sec, L_KV, F_KV)
                pe.wait_ge(gwlo_ready, layer + 1)
                bank_free(sec, F_GATE)
                for kt in range(KD):
                    last = product(work[0:GATES, F_GATE % 3, 0:T], gw_hi[:, kt, :], gw_lo[:, kt, :], xT_hi[:, kt, :], xT_lo[:, kt, :],
                                   kt == 0, kt == KD - 1)
                last.then_inc(small_ready, 1)
                rows_unit(sec, L_Q, F_Q, 0)
                pe.wait_ge(evac_done, sec.fill(F_GATE + 1))
                assert F_GATE_T % 3 == F_GATE % 3
                rows_unit(sec, L_Q, F_Q, 1)
                for i in range(TT):
                    last = nc.tensor.transpose(work[:, F_GATE_T % 3, GATES * i:GATES * i + GATES], gate_rows[:, P * i:P * i + P],
                                               ident[0:GATES, 0:GATES])
                last.then_inc(small_ready, 1)
                rows(sec, L_KVS, F_KVS)
                channels(sec, L_QMEM, F_QMEM[0])
                for w in range(2):
                    transposes(sec, F_PLAIN + w, lambda c, i: q_sb[:, i, P * (2 * w + c):P * (2 * w + c) + P])
                channels(sec, L_QMEM + 1, F_QMEM[1])

                def compressed(c):
                    pe.wait_ge(cmplo_ready, layer * 2 + c + 1)
                    bank_free(sec, F_CMP[c])
                    bank = work[0:GROUPS * N_CMP, F_CMP[c] % 3, 0:CMP_HIDDEN]
                    for half in range(2):
                        n, pairs = L_CMP[c] + half, CMP_PAIRS // 2
                        parts_ready(sec, n)
                        for q in range(pairs):
                            m, w = pairs * half + q, slice(CMP_HIDDEN * q, CMP_HIDDEN * (q + 1))
                            last = product(bank, cmp_hi[c][:, m, :], cmp_lo[c][:, m, :], hi[:, n % RING, w], lo[:, n % RING, w],
                                           m == 0, m == CMP_PAIRS - 1)
                        last.then_inc(unit_used, 1)

                def hidden(c):
                    n = GROUPS * N_CMP
                    for t in range(2):
                        last = nc.tensor.transpose(work[:, F_HID[c] % 3, n * t:n * t + n], cmp_rows[c][:, P * t:P * t + P], ident[0:n, 0:n])
                    last.then_inc(small_ready, 1)

                def compressed_out():
                    k_w2, v_w2 = (lp(name).rearrange("p (t d) -> p t d", t=2) for name in ("k_w2", "v_w2"))
                    pe.wait_ge(evac_done, sec.fill(F_HID[1] + 1))
                    assert F_HID[1] >= F_KCVC - 3
                    for t in range(2):
                        nc.tensor.matmul(work[:, F_KCVC % 3, 0:GROUPS * N_CMP], k_w2[:, t, :], hid[0][:, t, :],
                                         start=t == 0, stop=t == 1)
                    for g in range(GROUPS):
                        for t in range(2):
                            last = nc.tensor.matmul(work[0:N_CMP, F_KCVC % 3, T + HD * g:T + HD * g + HD],
                                                    hid[1][:, t, N_CMP * g:N_CMP * g + N_CMP], v_w2[:, t, :],
                                                    start=t == 0, stop=t == 1)
                    last.then_inc(small_ready, 1)

                def step_work(kind, k):
                    if kind == "merge":
                        channels(sec, L_MERGE[k], F_MERGE[k])
                    elif kind == "cmp":
                        compressed(k)
                    elif kind == "hid":
                        hidden(k)
                    elif kind == "rot":
                        pe.wait_ge(rot_ready, layer + 1)
                        if k == 1:
                            bank_free(sec, F_HID[0])
                        transposes(sec, F_ROT[k], lambda c, i: rot[:, i, 4 * k + 2 * c:4 * k + 2 * c + 2, :].rearrange("p h d -> p (h d)"))
                    else:
                        compressed_out()

                assert F_HID[0] - 2 > F_CMP[0] and F_ROT[3] + 1 >= F_HID[1] - 2 > F_CMP[1]
                operands = {0: F_QMEM[1] + 1, FIRST_NSA: F_ROT[3] + 1, FIRST_NSA + 2: F_KCVC + 1}
                jobs = jobs_of(sec)
                step_work("merge", 0)
                pe.wait_ge(evac_done, sec.fill(operands[0]))
                scores(sec, 0, jobs[0])
                for n, job in enumerate(jobs):
                    if n + 1 < len(jobs):
                        if n + 1 in operands:
                            pe.wait_ge(evac_done, sec.fill(operands[n + 1]))
                        scores(sec, n + 1, jobs[n + 1])
                    for kind, k in STEP_WORK.get(n, ()):
                        step_work(kind, k)
                    if merge_part(n):
                        w, begin, end = merge_part(n)
                        channels(sec, L_MERGE[w], F_MERGE[w], begin=begin, end=end)
                    turn(sec, n, job)
                    if n:
                        values(sec, n - 1, jobs[n - 1])

                def branch(w):
                    b, n = BRANCHES[w // 2], L_BR + w
                    if w >= 2:
                        pe.wait_ge(br_read, layer * 12 + (2 * w - 2))
                    parts_ready(sec, n)
                    for c in range(4):
                        for kt in range(4):
                            at = slice(P * (4 * c + kt), P * (4 * c + kt) + P)
                            last = product(br_bank(w, c // 2)[:, T * (c % 2):T * (c % 2) + T], hi[:, n % RING, at],
                                           lo[:, n % RING, at], br_hi[b][:, kt, :], br_lo[b][:, kt, :], kt == 0, kt == 3)
                        if c == 1:
                            last.then_inc(br_half, 1)
                    last.then_inc(unit_used, 1)

                pe.wait_ge(convlo_ready, layer + 1)
                pe.wait_ge(evac_done, sec.fill(F_FILLS))
                branch(0)
                values(sec, len(jobs) - 1, jobs[-1])
                branch(1)
                branch(2)
                branch(3)
                pe.wait_ge(tile_lo, sec.at(*TILES, TILES[1]))
                branch(4)
                branch(5)

                def merged_pair(kt):
                    if kt % 2 == 0:
                        pe.wait_ge(mlo_ready, layer * 4 + (kt // 2 + 1))

                output(sec, L_OUT, (merged_hi, merged_lo), merged_pair)
                x_transposed(sec, 3)
                ffn(sec, L_FFN2, 1, F_FILLS)


WAITING = {(True, 0): (16, 0), (True, 3): (2, 3), (False, 0): (14, 0), (False, 3): (0, 10)}

POOL_STEPS = 23
DVE_STEPS = (51, 60)

PI = float(np.float32(np.nextafter(np.float32(np.pi), np.float32(0))))
TURN = float(2 * np.pi)
ROUND = 1.5 * 2.0 ** 23


def turn_parts():
    rest, parts = TURN, []
    for bits in (5, 14, 23):
        part = np.floor(rest * 2.0 ** bits) / 2.0 ** bits
        parts.append(float(part))
        rest -= part
    return parts + [float(np.float32(rest))]


TURN_PARTS = turn_parts()


def rows_units(w):
    t = w.reshape(KD, P, w.shape[1]).transpose(1, 0, 2)
    return [t[:, 0:4].reshape(P, UNIT), t[:, 4:8].reshape(P, UNIT)]


def channel_units(w):
    k, n = w.shape
    t = w.reshape(k // P, P, n // P, P).transpose(1, 2, 0, 3).reshape(P, -1)
    return [t[:, a:a + UNIT] for a in range(0, t.shape[1], UNIT)]


def compression_units(w):
    t = w.reshape(CMP_PAIRS, P, CMP_HIDDEN).transpose(1, 0, 2).reshape(P, -1)
    return [t[:, 0:UNIT], t[:, UNIT:]]


def ffn_units(w_in, w_out):
    into, outof = [], []
    for j in range(CHUNKS):
        a = w_in[:, CHUNK * j:CHUNK * (j + 1)]
        b = w_in[:, D_FF + CHUNK * j:D_FF + CHUNK * (j + 1)]
        into.append(channel_units(a) + channel_units(b))
        outof.append(w_out[CHUNK * j:CHUNK * (j + 1)].reshape(2, P, D).transpose(1, 0, 2).reshape(P, UNIT))
    order = list(into[0])
    for j in range(1, CHUNKS):
        order += [*into[j], outof[j - 1]]
    return order + [outof[-1]]


def output_units(w, first=0):
    a, b = rows_units(w[:, 0:512]), rows_units(w[:, 512:1024])
    return [a[first], b[first], a[1 - first], b[1 - first]]


def by_partition(v):
    return v.reshape(-1, P).T


def pack(table, total, fields):
    packed = np.zeros((P, total), np.float32)
    for name, value in fields.items():
        at, n = table[name]
        packed[:, at:at + n] = value.reshape(P, n)
    return packed


def twice(v):
    return np.concatenate([v, v]).reshape(P, 1)


def block_diagonal(w):
    t = np.zeros((P, LRU_TILES, P), np.float32)
    for n in range(2 * LRU_TILES):
        at = 64 * (n % 2)
        t[at:at + 64, n // 2, at:at + 64] = w[n]
    return t


def constants():
    q = np.arange(P)
    made = np.zeros((P, CONST_N), np.float32)

    def put(name, value):
        at, n = CONST[name]
        made[:, at:at + n] = np.asarray(value, np.float32).reshape(P, n)

    distance = np.concatenate([q[:, None] - np.arange(P)[None], P + q[:, None] - np.arange(T)[None]], axis=1)
    put("ident", np.eye(P))
    put("causal", np.where(distance >= 0, 0.0, NEG))
    token = q[:, None] + P * np.arange(TT)[None]
    ends = np.arange(16) * CMP_STRIDE + CMP_BLOCK - 1
    put("cmp_mask", np.where(ends[None, None] <= token[:, :, None], 0.0, NEG))
    put("cmp_valid", token >= CMP_BLOCK - 1)
    put("inv_freq", np.broadcast_to(np.float32(ROPE_THETA) ** (-np.arange(0, 2 * ROT, 2, dtype=np.float32) / np.float32(2 * ROT)), (P, ROT)))
    slopes = 2.0 ** (-8.0 * np.arange(1, 5) / 4)
    alibi = np.stack([np.where(distance >= 0, -s * HD ** 0.5 * distance, NEG) for s in slopes], axis=1)
    return made, alibi.astype(np.float32).reshape(P, ALIBI_N)


def lay_out(a):
    b1_params = pack(B1P, B1P_N, {
        "a_w": block_diagonal(a["lru_a_w"][0]), "x_w": block_diagonal(a["lru_x_w"][0]),
        "conv_w": a["lru_conv_w"][0].reshape(CONV_W, LRU_TILES, P).transpose(2, 1, 0),
        "conv_b": by_partition(a["lru_conv_b"][0]), "a_b": by_partition(a["lru_a_b"][0]),
        "x_b": by_partition(a["lru_x_b"][0]), "lam": by_partition(a["lru_lambda"][0]),
        "g_mem": by_partition(a["mem_norm"][0]),
        "g_heads": np.concatenate([twice(a[n][0]) for n in ("moba_q_norm", "moba_k_norm", "mem_q_norm", "mem_k_norm")], axis=1)})
    pre, post, l_params = [a["ffn1_norm"][0], a["mix_norm"][0], a["ffn2_norm"][0]], [], []
    s = []
    w = a["w_in"][0]
    s += ffn_units(a["ffn1_w_in"][0], a["ffn1_w_out"][0])
    s += rows_units(a["mem_w_kv"][0])
    s += channel_units(w[:, 0:512])
    s += rows_units(w[:, 1024:1536])
    s += rows_units(w[:, 1536:2048])
    s += channel_units(w[:, 512:1024])
    s += output_units(a["w_out"][0], first=1)
    s += ffn_units(a["ffn2_w_in"][0], a["ffn2_w_out"][0])
    for l in range(LAYERS):
        b = {name[:-2]: a[name][l] for name in a if name.endswith("_2") and name not in ("mem_2", "positions_2")}
        w = b["w_mix_in"]
        k_w2 = b["cmp_k_w2"].reshape(2, P, HD).transpose(1, 0, 2)
        l_params.append(pack(LP, LP_N, {
            "gate_w": w[:, 2816:2840].reshape(KD, P, GATES).transpose(1, 0, 2),
            "k_w2": np.concatenate([k_w2, k_w2], axis=2),
            "v_w2": b["cmp_v_w2"].reshape(2, P, HD).transpose(1, 0, 2),
            "k_b1": by_partition(b["cmp_k_b1"]), "v_b1": by_partition(b["cmp_v_b1"]),
            "pos_k": by_partition(b["cmp_pos_k"].reshape(-1)), "pos_v": by_partition(b["cmp_pos_v"].reshape(-1)),
            "conv_w": b["conv_w"].reshape(CONV2_W, 4, P).transpose(2, 1, 0), "g_mem": by_partition(b["mem_norm"])}))
        pre += [b[f"{n}_norm_pre"] for n in ("ffn1", "mix", "ffn2")]
        post += [b[f"{n}_norm_post"] for n in ("ffn1", "mix", "ffn2")]
        s += ffn_units(b["ffn1_w_in"], b["ffn1_w_out"])
        s += channel_units(b["w_mem_kv"][:, 0:512]) + rows_units(b["w_mem_kv"][:, 512:1024])
        s += channel_units(w[:, 0:1536]) + channel_units(w[:, 2048:2304])
        s += rows_units(w[:, 1536:2048]) + rows_units(w[:, 2304:2816])
        s += channel_units(w[:, 2840:3352])
        m, k, v = channel_units(w[:, 3352:6424]), compression_units(b["cmp_k_w1"]), compression_units(b["cmp_v_w1"])
        s += [m[0], *k, m[1], *v, *m[2:]]
        for name in ("conv", "mem", "nsa"):
            s += channel_units(b[f"w_branch_{name}"])
        s += output_units(b["w_mix_out"])
        s += ffn_units(b["ffn2_w_in"], b["ffn2_w_out"])
    assert len(s) == WEIGHTS
    const, alibi = constants()
    return {"stream": np.stack(s), "b1_params": b1_params, "l_params": np.stack(l_params), "pre": np.stack(pre),
            "post": np.stack(post), "x": a["x"][0], "mem1": a["mem"][0], "mem2": a["mem_2"][0],
            "positions": np.ascontiguousarray(a["positions_2"][0].reshape(TT, P).T), "const": const, "alibi": alibi}


def kernel(**inputs):
    import concourse.bacc as bacc
    from concourse.bass_utils import run_bass_kernel_spmd as run

    arrays = lay_out({name: np.asarray(value) for name, value in inputs.items()})
    nc = bacc.Bacc("TRN2", target_bir_lowering=False, num_devices=1)
    ins = [nc.dram_tensor(name, a.shape, mybir.dt.from_np(a.dtype), kind="ExternalInput").ap() for name, a in arrays.items()]
    out = nc.dram_tensor("out", (T, D), F32, kind="ExternalOutput").ap()
    build(nc, *ins, out)
    result = run(nc, [arrays], core_ids=[0])
    return result.results[0]["out"].reshape(1, T, D)
```
